# Optimizing a Trainium2 kernel written in Bass

```python
import jax, jax.numpy as jnp
from jax import lax
import numpy as np

D_MODEL = 2048
BATCH = 1
SEQ = 256
DEPTH = 1

CONV_CH = 1024
CONV_K = 31
N_HEADS = 8
QK_NOPE = 128
QK_ROPE = 64
V_HEAD = 128
QK_HEAD = QK_NOPE + QK_ROPE
Q_LORA = 768
KV_LORA = 512
ATTN_CH = N_HEADS * V_HEAD
MIX_WIDTH = CONV_CH + ATTN_CH
IN_COLS = 2 * CONV_CH + Q_LORA + KV_LORA + QK_ROPE
ROPE_THETA = 10000.0
Q_BLOCK = 128
D_FF = ((8 * D_MODEL // 3 + 255) // 256) * 256
EPS = 1e-6


def rmsnorm(x, g):
    xf = x.astype(jnp.float32)
    y = xf * lax.rsqrt(jnp.mean(xf * xf, axis=-1, keepdims=True) + EPS)
    return (y * g.astype(jnp.float32)).astype(x.dtype)

def layernorm(x, g, b):
    xf = x.astype(jnp.float32)
    mu = jnp.mean(xf, axis=-1, keepdims=True)
    var = jnp.mean(jnp.square(xf - mu), axis=-1, keepdims=True)
    y = (xf - mu) * lax.rsqrt(var + EPS)
    return (y * g.astype(jnp.float32) + b.astype(jnp.float32)).astype(x.dtype)

def rope_tables(positions, dtype):
    inv_freq = ROPE_THETA ** (-jnp.arange(0, QK_ROPE, 2, dtype=jnp.float32) / QK_ROPE)
    ang = positions.astype(jnp.float32)[..., None] * inv_freq
    return jnp.cos(ang).astype(dtype), jnp.sin(ang).astype(dtype)

def apply_rope(x, cos, sin):
    x1, x2 = jnp.split(x, 2, axis=-1)
    return jnp.concatenate([x1 * cos - x2 * sin, x2 * cos + x1 * sin], axis=-1)

def causal_depthwise_conv(u, w, b):
    y = lax.conv_general_dilated(
        u, w[:, None, :], window_strides=(1,), padding=[(CONV_K - 1, 0)],
        dimension_numbers=("NWC", "WIO", "NWC"), feature_group_count=u.shape[-1])
    return y + b

def causal_attention(q, k, v):
    B, S, H, Dq = q.shape
    nblk = S // Q_BLOCK
    qb = q.reshape(B, nblk, Q_BLOCK, H, Dq).transpose(1, 0, 2, 3, 4)
    kpos = jnp.arange(S)
    scale = Dq ** -0.5
    neg = jnp.finfo(jnp.float32).min

    def one_block(args):
        i, qi = args
        s = jnp.einsum('bqhd,bkhd->bhqk', qi, k).astype(jnp.float32) * scale
        qpos = i * Q_BLOCK + jnp.arange(Q_BLOCK)
        s = jnp.where(kpos[None, :] <= qpos[:, None], s, neg)
        p = jax.nn.softmax(s, axis=-1).astype(v.dtype)
        return jnp.einsum('bhqk,bkhd->bqhd', p, v)

    out = lax.map(one_block, (jnp.arange(nblk), qb))
    return out.transpose(1, 0, 2, 3, 4).reshape(B, S, H * v.shape[-1])

def first_inputs(seed: int = 0) -> dict:
    key = jax.random.key(seed)
    ks = jax.random.split(key, 24)
    f = jnp.float32
    L = DEPTH

    def w(k, shape, fan_in):
        return jax.random.normal(k, shape, f) * (fan_in ** -0.5)

    def gain(k, n):
        return jnp.ones((L, n), f) + 0.05 * jax.random.normal(k, (L, n), f)

    x = jax.random.normal(ks[0], (BATCH, SEQ, D_MODEL), f)
    offset = jax.random.randint(ks[1], (BATCH, 1), 0, 1024, dtype=jnp.int32)
    positions = offset + jnp.arange(SEQ, dtype=jnp.int32)[None, :]
    return {
        "x": x,
        "positions": positions,
        "pre_mix_norm": gain(ks[2], D_MODEL),
        "w_in": w(ks[3], (L, D_MODEL, IN_COLS), D_MODEL),
        "q_norm": gain(ks[4], Q_LORA),
        "w_uq": w(ks[5], (L, Q_LORA, N_HEADS * QK_HEAD), Q_LORA),
        "kv_norm": gain(ks[6], KV_LORA),
        "w_ukv": w(ks[7], (L, KV_LORA, N_HEADS * (QK_NOPE + V_HEAD)), KV_LORA),
        "conv_w": w(ks[8], (L, CONV_K, CONV_CH), CONV_K),
        "conv_b": 0.02 * jax.random.normal(ks[9], (L, CONV_CH), f),
        "conv_ln_g": gain(ks[10], CONV_CH),
        "conv_ln_b": 0.02 * jax.random.normal(ks[11], (L, CONV_CH), f),
        "conv_out_norm": gain(ks[12], CONV_CH),
        "attn_out_norm": gain(ks[13], ATTN_CH),
        "w_out": w(ks[14], (L, MIX_WIDTH, D_MODEL), MIX_WIDTH),
        "post_mix_norm": gain(ks[15], D_MODEL),
        "pre_ffn_norm": gain(ks[16], D_MODEL),
        "w_gate": w(ks[17], (L, D_MODEL, D_FF), D_MODEL),
        "w_up": w(ks[18], (L, D_MODEL, D_FF), D_MODEL),
        "w_down": w(ks[19], (L, D_FF, D_MODEL), D_FF),
        "post_ffn_norm": gain(ks[20], D_MODEL),
    }

def first_block(x, positions, pre_mix_norm, w_in, q_norm, w_uq, kv_norm, w_ukv,
              conv_w, conv_b, conv_ln_g, conv_ln_b, conv_out_norm, attn_out_norm,
              w_out, post_mix_norm, pre_ffn_norm, w_gate, w_up, w_down, post_ffn_norm):
    B, S, _ = x.shape
    cos, sin = rope_tables(positions, x.dtype)
    c1 = 2 * CONV_CH
    c2 = c1 + Q_LORA
    c3 = c2 + KV_LORA
    for l in range(DEPTH):
        h = rmsnorm(x, pre_mix_norm[l])
        z = h @ w_in[l]
        conv_in, q_lat, kv_lat, k_rope = z[..., :c1], z[..., c1:c2], z[..., c2:c3], z[..., c3:]

        a, g = jnp.split(conv_in, 2, axis=-1)
        u = a * jax.nn.sigmoid(g)
        u = causal_depthwise_conv(u, conv_w[l], conv_b[l])
        u = jax.nn.silu(layernorm(u, conv_ln_g[l], conv_ln_b[l]))

        q = (rmsnorm(q_lat, q_norm[l]) @ w_uq[l]).reshape(B, S, N_HEADS, QK_HEAD)
        q_nope, q_pe = q[..., :QK_NOPE], q[..., QK_NOPE:]
        q_pe = apply_rope(q_pe, cos[:, :, None, :], sin[:, :, None, :])
        kv = (rmsnorm(kv_lat, kv_norm[l]) @ w_ukv[l]).reshape(B, S, N_HEADS, QK_NOPE + V_HEAD)
        k_nope, v = kv[..., :QK_NOPE], kv[..., QK_NOPE:]
        k_pe = apply_rope(k_rope, cos, sin)
        k_pe = jnp.broadcast_to(k_pe[:, :, None, :], (B, S, N_HEADS, QK_ROPE))
        q_full = jnp.concatenate([q_nope, q_pe], axis=-1)
        k_full = jnp.concatenate([k_nope, k_pe], axis=-1)
        attn = causal_attention(q_full, k_full, v)

        mix = jnp.concatenate([rmsnorm(u, conv_out_norm[l]),
                               rmsnorm(attn, attn_out_norm[l])], axis=-1) @ w_out[l]
        x = x + rmsnorm(mix, post_mix_norm[l])

        hf = rmsnorm(x, pre_ffn_norm[l])
        ff = (jax.nn.silu(hf @ w_gate[l]) * (hf @ w_up[l])) @ w_down[l]
        x = x + rmsnorm(ff, post_ffn_norm[l])
    return x


POOL_WIDTH = D_MODEL // 2
POOL_WINDOWS = (2, 4, 8, 16)
POOL_GROUP = POOL_WIDTH // len(POOL_WINDOWS)
LRU_WIDTH = D_MODEL // 2
LRU_HEADS = 8
LRU_HEAD_DIM = LRU_WIDTH // LRU_HEADS
CONV_WIDTH = 4
LRU_C = 8.0
MIX_WIDTH_2 = POOL_WIDTH + LRU_WIDTH
IN_PROJ_WIDTH = POOL_WIDTH + 2 * LRU_WIDTH
PEER_HEADS = 8
PEER_N_KEYS = 128
PEER_N_EXPERTS = PEER_N_KEYS * PEER_N_KEYS
PEER_D_KEY = 256
PEER_HALF = PEER_D_KEY // 2
PEER_TOPK = 16
PEER_CHUNK = 128


def rmsnorm_2(x, g):
    xf = x.astype(jnp.float32)
    y = xf * lax.rsqrt(jnp.mean(xf * xf, axis=-1, keepdims=True) + EPS)
    return (y * g.astype(jnp.float32)).astype(x.dtype)

def pool_mixer(u, pool_w, pool_b, pool_scale):
    B, S, _ = u.shape
    uf = u.astype(jnp.float32).reshape(B, S, len(POOL_WINDOWS), POOL_GROUP)
    csum = jnp.cumsum(uf, axis=1)
    pos = jnp.arange(1, S + 1, dtype=jnp.float32)[None, :, None]
    outs = []
    for g, w in enumerate(POOL_WINDOWS):
        c = csum[:, :, g]
        c_prev = jnp.pad(c, ((0, 0), (w, 0), (0, 0)))[:, :S]
        mean = (c - c_prev) / jnp.minimum(pos, float(w))
        outs.append(mean - uf[:, :, g])
    d = jnp.stack(outs, axis=2).astype(u.dtype)
    y = jnp.einsum('bsgi,gij->bsgj', d, pool_w) + pool_b
    return y.reshape(B, S, POOL_WIDTH) * pool_scale

def _lru_combine(left, right):
    a1, b1 = left
    a2, b2 = right
    return a1 * a2, a2 * b1 + b2

def rg_lru_mixer(xb, gate, conv_w, conv_b, gate_a_w, gate_a_b, gate_x_w, gate_x_b, lru_lambda):
    B, S, _ = xb.shape
    xp = jnp.pad(xb, ((0, 0), (CONV_WIDTH - 1, 0), (0, 0)))
    xc = conv_b + xp[:, 0:S] * conv_w[0]
    for k in range(1, CONV_WIDTH):
        xc = xc + xp[:, k:k + S] * conv_w[k]
    xh = xc.reshape(B, S, LRU_HEADS, LRU_HEAD_DIM)
    r = jax.nn.sigmoid(jnp.einsum('bshi,hij->bshj', xh, gate_a_w) + gate_a_b).reshape(B, S, LRU_WIDTH)
    i = jax.nn.sigmoid(jnp.einsum('bshi,hij->bshj', xh, gate_x_w) + gate_x_b).reshape(B, S, LRU_WIDTH)
    log_a = (LRU_C * r.astype(jnp.float32)) * jax.nn.log_sigmoid(lru_lambda.astype(jnp.float32))
    a = jnp.exp(log_a)
    mult = jnp.sqrt(-jnp.expm1(2.0 * log_a))
    b = mult * (i * xc).astype(jnp.float32)
    _, h = lax.associative_scan(_lru_combine, (a, b), axis=1)
    return h.astype(xb.dtype) * jax.nn.gelu(gate)

def peer_ffn(z, peer_wq, keys1, keys2, peer_u, peer_v):
    B, S, D = z.shape
    zt = z.reshape(-1, PEER_CHUNK, D)
    k1 = keys1.astype(jnp.float32)
    k2 = keys2.astype(jnp.float32)

    def chunk(zc):
        q = (zc @ peer_wq).astype(jnp.float32).reshape(PEER_CHUNK, PEER_HEADS, 2, PEER_HALF)
        s1 = jnp.einsum('chd,hkd->chk', q[:, :, 0], k1)
        s2 = jnp.einsum('chd,hkd->chk', q[:, :, 1], k2)
        v1, i1 = lax.top_k(s1, PEER_TOPK)
        v2, i2 = lax.top_k(s2, PEER_TOPK)
        cand = (v1[..., :, None] + v2[..., None, :]).reshape(PEER_CHUNK, PEER_HEADS, PEER_TOPK * PEER_TOPK)
        cand_idx = (i1[..., :, None] * PEER_N_KEYS + i2[..., None, :]).reshape(PEER_CHUNK, PEER_HEADS, PEER_TOPK * PEER_TOPK)
        top_s, top_pos = lax.top_k(cand, PEER_TOPK)
        expert = jnp.take_along_axis(cand_idx, top_pos, axis=-1)
        gate = jax.nn.softmax(top_s, axis=-1)
        u = jnp.take(peer_u, expert, axis=0)
        act = jax.nn.gelu(jnp.einsum('chkd,cd->chk', u, zc))
        v = jnp.take(peer_v, expert, axis=0)
        w = (gate * act.astype(jnp.float32)).astype(zc.dtype)
        return jnp.einsum('chk,chkd->cd', w, v).astype(zc.dtype)

    return lax.map(chunk, zt).reshape(B, S, D)

def second_inputs(seed: int = 0) -> dict:
    key = jax.random.key(seed)
    ks = jax.random.split(key, 24)
    L = DEPTH
    f32 = jnp.float32

    def nrm(k, shape, scale):
        return jax.random.normal(k, shape, f32) * scale

    a0 = jax.random.uniform(ks[12], (L, LRU_WIDTH), f32, 0.9, 0.999) ** (1.0 / LRU_C)
    lru_lambda = jnp.log(a0) - jnp.log1p(-a0)
    return {
        "x": nrm(ks[0], (BATCH, SEQ, D_MODEL), 1.0),
        "norm1_g": 1.0 + nrm(ks[1], (L, D_MODEL), 0.02),
        "w_in": nrm(ks[2], (L, D_MODEL, IN_PROJ_WIDTH), D_MODEL ** -0.5),
        "pool_w": nrm(ks[3], (L, len(POOL_WINDOWS), POOL_GROUP, POOL_GROUP), POOL_GROUP ** -0.5),
        "pool_b": nrm(ks[4], (L, len(POOL_WINDOWS), POOL_GROUP), 0.01),
        "pool_scale": 1.0 + nrm(ks[5], (L, POOL_WIDTH), 0.02),
        "conv_w": nrm(ks[6], (L, CONV_WIDTH, LRU_WIDTH), CONV_WIDTH ** -0.5),
        "conv_b": nrm(ks[7], (L, LRU_WIDTH), 0.01),
        "gate_a_w": nrm(ks[8], (L, LRU_HEADS, LRU_HEAD_DIM, LRU_HEAD_DIM), LRU_HEAD_DIM ** -0.5),
        "gate_a_b": nrm(ks[9], (L, LRU_HEADS, LRU_HEAD_DIM), 0.01),
        "gate_x_w": nrm(ks[10], (L, LRU_HEADS, LRU_HEAD_DIM, LRU_HEAD_DIM), LRU_HEAD_DIM ** -0.5),
        "gate_x_b": nrm(ks[11], (L, LRU_HEADS, LRU_HEAD_DIM), 0.01),
        "lru_lambda": lru_lambda,
        "w_out": nrm(ks[13], (L, MIX_WIDTH_2, D_MODEL), MIX_WIDTH_2 ** -0.5),
        "norm2_g": 1.0 + nrm(ks[14], (L, D_MODEL), 0.02),
        "peer_wq": nrm(ks[15], (L, D_MODEL, PEER_HEADS * PEER_D_KEY), D_MODEL ** -0.5),
        "peer_keys1": nrm(ks[16], (L, PEER_HEADS, PEER_N_KEYS, PEER_HALF), PEER_HALF ** -0.5),
        "peer_keys2": nrm(ks[17], (L, PEER_HEADS, PEER_N_KEYS, PEER_HALF), PEER_HALF ** -0.5),
        "peer_u": nrm(ks[18], (L, PEER_N_EXPERTS, D_MODEL), D_MODEL ** -0.5),
        "peer_v": nrm(ks[19], (L, PEER_N_EXPERTS, D_MODEL), PEER_HEADS ** -0.5),
        "norm_f_g": 1.0 + nrm(ks[20], (D_MODEL,), 0.02),
    }

def second_block(x, norm1_g, w_in, pool_w, pool_b, pool_scale, conv_w, conv_b, gate_a_w, gate_a_b,
              gate_x_w, gate_x_b, lru_lambda, w_out, norm2_g, peer_wq, peer_keys1, peer_keys2,
              peer_u, peer_v, norm_f_g):
    h = x
    for l in range(DEPTH):
        z = rmsnorm_2(h, norm1_g[l])
        proj = z @ w_in[l]
        u_pool = proj[..., :POOL_WIDTH]
        x_lru = proj[..., POOL_WIDTH:POOL_WIDTH + LRU_WIDTH]
        g_lru = proj[..., POOL_WIDTH + LRU_WIDTH:]
        y_pool = pool_mixer(u_pool, pool_w[l], pool_b[l], pool_scale[l])
        y_lru = rg_lru_mixer(x_lru, g_lru, conv_w[l], conv_b[l], gate_a_w[l], gate_a_b[l],
                             gate_x_w[l], gate_x_b[l], lru_lambda[l])
        y = jnp.concatenate([y_pool, y_lru], axis=-1)
        h = h + y @ w_out[l]
        h = h + peer_ffn(rmsnorm_2(h, norm2_g[l]), peer_wq[l], peer_keys1[l], peer_keys2[l],
                         peer_u[l], peer_v[l])
    return rmsnorm_2(h, norm_f_g)


def setup_inputs(seed=0):
    out = dict(first_inputs(seed))
    for name, value in second_inputs(seed + 1).items():
        if name != "x":
            out[name + "_2"] = value
    return out


def reference(
    x, positions, pre_mix_norm, w_in, q_norm, w_uq, kv_norm, w_ukv, conv_w, conv_b, conv_ln_g,
    conv_ln_b, conv_out_norm, attn_out_norm, w_out, post_mix_norm, pre_ffn_norm, w_gate, w_up,
    w_down, post_ffn_norm, norm1_g_2, w_in_2, pool_w_2, pool_b_2, pool_scale_2, conv_w_2,
    conv_b_2, gate_a_w_2, gate_a_b_2, gate_x_w_2, gate_x_b_2, lru_lambda_2, w_out_2, norm2_g_2,
    peer_wq_2, peer_keys1_2, peer_keys2_2, peer_u_2, peer_v_2, norm_f_g_2,
):
    x = first_block(
        x, positions, pre_mix_norm, w_in, q_norm, w_uq, kv_norm, w_ukv, conv_w, conv_b,
        conv_ln_g, conv_ln_b, conv_out_norm, attn_out_norm, w_out, post_mix_norm, pre_ffn_norm,
        w_gate, w_up, w_down, post_ffn_norm,
    )
    return second_block(
        x, norm1_g_2, w_in_2, pool_w_2, pool_b_2, pool_scale_2, conv_w_2, conv_b_2, gate_a_w_2,
        gate_a_b_2, gate_x_w_2, gate_x_b_2, lru_lambda_2, w_out_2, norm2_g_2, peer_wq_2,
        peer_keys1_2, peer_keys2_2, peer_u_2, peer_v_2, norm_f_g_2,
    )


_drawn_inputs = setup_inputs


def setup_inputs(seed=0):
    import zlib

    import numpy as np

    out = dict(_drawn_inputs(seed))
    spreads = {}
    factors = {'conv_ln_b': 3.154,
     'norm1_g_2': 3.928,
     'pool_b_2': 7.617,
     'pool_scale_2': 18.987,
     'conv_b_2': 12.506,
     'gate_a_b_2': 64.0,
     'gate_x_b_2': 50.406,
     'norm2_g_2': 30.272,
     'norm_f_g_2': 7.851}
    for name, (base, spread) in spreads.items():
        noise = np.random.default_rng([zlib.crc32(name.encode()), seed]).standard_normal(out[name].shape)
        drawn = base * np.exp(spread * noise) if base else spread * noise
        out[name] = __import__('jax').numpy.asarray(drawn.astype(out[name].dtype))
    for name, factor in factors.items():
        out[name] = (out[name] * factor).astype(out[name].dtype)
    return out
```

```python
from contextlib import ExitStack

import numpy as np

import concourse.bass as bass
from concourse import mybir

ALU = mybir.AluOpType
ACT = mybir.ActivationFunctionType
AX = mybir.AxisListType
F32 = mybir.dt.float32
I32 = mybir.dt.int32
U32 = mybir.dt.uint32

P = 128
S = 256
TT = S // P
D = 2048
DT = D // P
CONV_CH = 1024
CT = CONV_CH // P
CONV_K = 31
HEADS = 8
NOPE, ROPE, VH = 128, 64, 128
QK = NOPE + ROPE
QLT = 768 // P
KVT = 512 // P
DFF = 5632
FT = DFF // P
EPS = 1e-6
ROPE_THETA = 10000.0
SCALE = float(QK) ** -0.5
MASKED = -1e30
POOL_WINDOWS = (2, 4, 8, 16)
WMAX = max(POOL_WINDOWS)
LRU_C = 8.0
LCONV = 4
PH = 8
NKEY = 128
TOPK = 16
SLOTS = PH * TOPK
NEG = -3.0e38

RING = 4
UNIT = 4096
UCOLS = UNIT // DT
N_IN1, N_UQ, N_UKV, N_OUT, N_GU, N_DOWN, N_IN2 = 14, 4, 2, 8, 44, 32, 12
U_IN1 = 0
U_UQ = U_IN1 + N_IN1
U_UKV = U_UQ + N_UQ
U_OUT1 = U_UKV + N_UKV
U_GU = U_OUT1 + N_OUT
U_DOWN = U_GU + N_GU
U_IN2 = U_DOWN + N_DOWN
U_POOL = U_IN2 + N_IN2
U_GATE = U_POOL + 1
U_OUT2 = U_GATE + 1
U_WQ = U_OUT2 + N_OUT
U_KEY = U_WQ + N_OUT
N_UNITS = U_KEY + 2
DK = FT // 4

NORMS = (("pre", 16), ("q", QLT), ("kv", KVT), ("ln", CT), ("conv", CT), ("attn", 8), ("post", 16),
         ("ffn", 16), ("postf", 16), ("n1", 16), ("n2", 16))
NI = {name: n for n, (name, _) in enumerate(NORMS)}

PARAM_TILES = (
    (("pre_mix_norm", 16), ("q_norm", 6), ("kv_norm", 4), ("conv_b", 8), ("conv_ln_g", 8), ("conv_ln_b", 8),
     ("conv_out_norm", 8), ("attn_out_norm", 8), ("post_mix_norm", 16), ("pre_ffn_norm", 16), ("post_ffn_norm", 16)),
    (("norm1_g_2", 16), ("pool_b_2", 8), ("pool_scale_2", 8), ("conv_b_2", 8), ("gate_a_b_2", 8), ("gate_x_b_2", 8),
     ("lru_lambda_2", 8), ("norm2_g_2", 16), ("conv_w_2", LCONV * 8)),
    (("conv_w_lo", 16 * CT),),
    (("conv_w_hi", (CONV_K - 16) * CT),),
)


def param_columns():
    at, col = {}, 0
    for tile in PARAM_TILES:
        for name, rows in tile:
            at[name] = col
            col += rows
    return at, col


def build(nc, A, out):
    PC, NPARAM = param_columns()
    params = sorted({n for t in PARAM_TILES for n, _ in t})
    n_param_dmas = len(params)

    with ExitStack() as ctx:
        def sb(name, shape, dt=F32):
            return ctx.enter_context(nc.sbuf_tensor(name, shape, dt))

        def sem(name):
            return ctx.enter_context(nc.semaphore(name))

        ring = sb("ring", [P, RING, UNIT])
        res = sb("res", [P, DT, S])
        h = sb("h", [P, DT, S])
        mix = sb("mix", [P, DT, S])
        tmp = sb("tmp", [P, DT, S])
        arena = sb("arena", [P, 16384])
        par = sb("par", [P, NPARAM])
        prow = sb("prow", [P, len(PARAM_TILES), P])
        ident = sb("ident", [P, P])
        ones = sb("ones", [P, P])
        rotT = sb("rotT", [ROPE, ROPE])
        mask = sb("mask", [P, 3, P])
        meansq = sb("meansq", [P, S])
        invms = sb("invms", [P, S])
        rstd = sb("rstd", [P, S])
        small = sb("small", [P, 64])
        halfpi = sb("halfpi", [P, 1])

        def area(start, *shape):
            n = int(np.prod(shape))
            v = arena[:, start:start + n]
            if len(shape) == 2:
                v = v.rearrange("p (a b) -> p a b", a=shape[0])
            if len(shape) == 3:
                v = v.rearrange("p (a b c) -> p a b c", a=shape[0], b=shape[1])
            return v

        CPAD = CONV_K - 1
        xin = area(0, TT, D)
        conv_a = area(0, CT, S)
        conv_u = area(2048, CT, CPAD + S)
        q_lat = area(4336, QLT, S)
        kv_lat = area(5872, KVT, S)
        k_raw = area(6896, S)
        q_nope = area(7152, HEADS, S)
        q_pe = area(9200, HEADS, S)
        k_nope = area(11248, HEADS, S)
        v_tok = area(13296, TT, HEADS * VH)
        k_pe = area(15344, S)
        angle = area(15600, S)
        cosT = area(15856, S)
        sinT = area(16112, S)
        sig = area(7152, 2, 2 * S)
        mean_b = area(9200, S)
        hid = area(0, FT, S)
        silu = area(FT * S, 2, 2 * S)
        LPAD = LCONV - 1
        p_u = area(0, 8, WMAX + S)
        l_x = area(2176, 8, LPAD + S)
        l_gelu = area(4248, 8, S)
        l_xc = area(6296, 8, S)
        l_r = area(8344, 8, S)
        l_i = area(10392, 8, S)
        l_m = area(12440, 8, S)
        win = area(14488, WMAX + S)
        win2 = area(14488 + WMAX + S, WMAX + S)
        edge = area(15032, len(POOL_WINDOWS), WMAX)
        p_d = tmp
        zc = area(0, TT, D)
        acc = area(4096, TT, D)
        sc = area(8192, TT, 16, NKEY)
        keysT = area(12288, 16, NKEY)
        gain_f = tmp[:, 0:8, :].rearrange("p a b -> p (a b)")
        row = ring[:].rearrange("p r (a d) -> p (r a) d", d=D)
        GR = RING * UNIT // D
        top_v = area(14336, TT, 16, TOPK)
        top_i = area(14848, TT, 16, TOPK).bitcast(U32)
        top_f = area(15360, 16, TOPK)
        ctop = area(15616, PH, TOPK)
        cpos = area(15744, PH, TOPK).bitcast(U32)
        cposf = area(15872, 2, PH, TOPK)
        cposi = area(16128, 2, PH, TOPK).bitcast(I32)
        work = tmp[:, 0:8, :].rearrange("p a (b k) -> p (a b) k", k=NKEY)
        iota16 = sb("iota16", [P, TOPK])
        gate = sb("gate", [P, TT, SLOTS])
        expert = sb("expert", [P, TT * SLOTS], I32)
        dots = sb("dots", [P, TT * SLOTS])
        dot_r = sb("dot_r", [P, GR])
        wts = sb("wts", [P, TT * SLOTS])
        w_r = sb("w_r", [P, GR])
        idx_r = sb("idx_r", [P, GR], I32)

        pl = [ctx.enter_context(nc.psum_tensor(f"pl{n}", [P, 512], F32)) for n in range(4)]
        pg = [ctx.enter_context(nc.psum_tensor(f"pg{n}", [P, 512], F32)) for n in range(4)]
        pnorm = pg[3][:, 0:S]

        x_in = sem("x_in")
        par_in = sem("par_in")
        pos_in = sem("pos_in")
        slot_full = [sem(f"slot_full{n}") for n in range(RING)]
        unit_used = sem("unit_used")
        const_ready = sem("const_ready")
        par_T = sem("par_T")
        par_ready = sem("par_ready")
        x_T = sem("x_T")
        res_ready = sem("res_ready")
        norm_sq = sem("norm_sq")
        norm_sum = sem("norm_sum")
        norm_inv = sem("norm_inv")
        norm_rstd = sem("norm_rstd")
        norm_out = sem("norm_out")
        a_ready = sem("a_ready")
        sig_ready = sem("sig_ready")
        u_ready = sem("u_ready")
        lat_ready = sem("lat_ready")
        conv_ready = sem("conv_ready")
        mean_sum = sem("mean_sum")
        centred = sem("centred")
        conv_silu = sem("conv_silu")
        q_ready = sem("q_ready")
        kv_ready = sem("kv_ready")
        freq_done = sem("freq_done")
        trig_arg = sem("trig_arg")
        trig_ready = sem("trig_ready")
        rot_done = sem("rot_done")
        roped = sem("roped")
        s_done = sem("s_done")
        s_ready = sem("s_ready")
        s_max = sem("s_max")
        exp_ready = sem("exp_ready")
        prob_ready = sem("prob_ready")
        pT_done = sem("pT_done")
        pT_ready = sem("pT_ready")
        o_done = sem("o_done")
        o_ready = sem("o_ready")
        out1_ready = sem("out1_ready")
        res1_ready = sem("res1_ready")
        silu_ready = sem("silu_ready")
        hid_ready = sem("hid_ready")
        down_ready = sem("down_ready")
        res2_ready = sem("res2_ready")
        res3_ready = sem("res3_ready")
        in2_ready = sem("in2_ready")
        pool_d = sem("pool_d")
        pool_done = sem("pool_done")
        pool_y = sem("pool_y")
        xc_ready = sem("xc_ready")
        gates_done = sem("gates_done")
        gates_ready = sem("gates_ready")
        lam_exp = sem("lam_exp")
        lam_abs = sem("lam_abs")
        lam_ready = sem("lam_ready")
        decay = sem("decay")
        mult_arg = sem("mult_arg")
        mult_ready = sem("mult_ready")
        lru_y = sem("lru_y")
        out2_ready = sem("out2_ready")
        wq_ready = sem("wq_ready")
        tok_T = sem("tok_T")
        tok_ready = sem("tok_ready")
        key_T = sem("key_T")
        key_ready = sem("key_ready")
        sc_done = sem("sc_done")
        sc_ready = sem("sc_ready")
        sel_max = sem("sel_max")
        sel_exp = sem("sel_exp")
        sel_ready = sem("sel_ready")
        gain_in = sem("gain_in")
        idx_copied = sem("idx_copied")
        pool_step = sem("pool_step")
        row_full = [sem(f"row_full{n}") for n in range(GR)]
        row_used = sem("row_used")
        dot_done = sem("dot_done")
        dot_kept = sem("dot_kept")
        act_ready = sem("act_ready")
        w_copied = sem("w_copied")
        added = sem("added")
        fin_sq = sem("fin_sq")
        fin_inv = sem("fin_inv")
        fin_rstd = sem("fin_rstd")
        fin_out = sem("fin_out")
        stored = sem("stored")
        dve_step = sem("dve_step")
        pool_c = sem("pool_c")

        def slot_count(unit):
            return 16 * (unit // RING + 1)

        def sq_count(n, t4):
            return sum(-(-k // 4) for _, k in NORMS[:n]) + t4 + 1

        def tiles_before(n):
            return sum(k for _, k in NORMS[:n])

        def col(name, t=0, n=1):
            return par[:, PC[name] + t:PC[name] + t + n]

        def conv_tap(k, c):
            return col("conv_w_lo", k * CT + c) if k < 16 else col("conv_w_hi", (k - 16) * CT + c)

        block = ctx.enter_context(nc.Block())

        @block.sync
        def _(sp):
            for t in range(TT):
                sp.dma_start(xin[:, t, :], A["x"][0, t * P:(t + 1) * P, :]).then_inc(x_in, 16)

            def unit(n, src, k, c, free=True):
                if free and n >= RING:
                    sp.wait_ge(unit_used, n - RING + 1)
                dst = ring[:, n % RING, 0:k * c].rearrange("p (k c) -> p k c", k=k)
                sp.dma_start(dst, src).then_inc(slot_full[n % RING], 16)

            def columns(w, c0, c):
                return w[0, :, c0:c0 + c].rearrange("(k p) c -> p k c", p=P)

            for n in range(RING):
                unit(U_IN1 + n, columns(A["w_in"], n * UCOLS, UCOLS), DT, UCOLS)
            for t, tile in enumerate(PARAM_TILES):
                r = 0
                for name, rows in tile:
                    if name == "conv_w_lo":
                        src = A["conv_w"][0, 0:16, :]
                    elif name == "conv_w_hi":
                        src = A["conv_w"][0, 16:CONV_K, :]
                    else:
                        src = A[name][0]
                        if len(src.shape) == 1:
                            src = src.rearrange("(a n) -> a n", a=1)
                    flat = src.rearrange("a n -> (a n)").rearrange("(r c) -> r c", c=P)
                    sp.dma_start(prow[r:r + rows, t, :], flat).then_inc(par_in, 16)
                    r += rows
            sp.dma_start(angle.bitcast(I32), A["positions"].broadcast_to([P, S])).then_inc(pos_in, 16)

            for n in range(RING, N_IN1 - 1):
                unit(U_IN1 + n, columns(A["w_in"], n * UCOLS, UCOLS), DT, UCOLS)
            unit(U_IN1 + N_IN1 - 1, columns(A["w_in"], (N_IN1 - 1) * UCOLS, ROPE), DT, ROPE)
            for n in range(N_UQ):
                unit(U_UQ + n, columns(A["w_uq"], n * 2 * QK, 2 * QK), QLT, 2 * QK)
            for n in range(N_UKV):
                unit(U_UKV + n, columns(A["w_ukv"], n * 1024, 1024), KVT, 1024)

            def stream(first, n_units, parts):
                turn = len(parts)
                with sp.Fori(0, n_units // turn) as i:
                    for j, (src, k, c) in enumerate(parts):
                        n = first + j
                        sp.wait_ge(unit_used, i * turn + (n - RING + 1))
                        dst = ring[:, n % RING, 0:k * c].rearrange("p (k c) -> p k c", k=k)
                        sp.dma_start(dst, src(i)).then_inc(slot_full[n % RING], 16)

            def dyn(w, turn, j, c, k0=0, k=DT):
                def src(i):
                    v = w[0, k0 * P:(k0 + k) * P, bass.ds(i * (turn * c) + j * c, c)]
                    return v.rearrange("(k p) c -> p k c", p=P)
                return (src, k, c)

            stream(U_OUT1, N_OUT, [dyn(A["w_out"], 4, j, UCOLS) for j in range(4)])
            stream(U_GU, N_GU, [dyn(A[w], 2, j, UCOLS) for j in range(2) for w in ("w_gate", "w_up")])
            stream(U_DOWN, N_DOWN, [dyn(A["w_down"], 2, j, UCOLS, u * DK, DK) for j in range(2) for u in range(4)])
            stream(U_IN2, N_IN2, [dyn(A["w_in_2"], 4, j, UCOLS) for j in range(4)])
            sp.wait_ge(unit_used, U_POOL - RING + 1)
            sp.dma_start(ring[:, U_POOL % RING, 0:2048].rearrange("p (g k c) -> p g k c", g=4, k=2),
                         A["pool_w_2"][0].rearrange("g (k p) c -> p g k c", p=P)).then_inc(slot_full[U_POOL % RING], 16)
            sp.wait_ge(unit_used, U_GATE - RING + 1)
            for n, w in enumerate(("gate_a_w_2", "gate_x_w_2")):
                sp.dma_start(ring[:, U_GATE % RING, n * 1024:(n + 1) * 1024].rearrange("p (h c) -> p h c", h=8),
                             A[w][0].rearrange("h p c -> p h c")).then_inc(slot_full[U_GATE % RING], 16)
            stream(U_OUT2, N_OUT, [dyn(A["w_out_2"], 4, j, UCOLS) for j in range(4)])
            stream(U_WQ, N_OUT, [dyn(A["peer_wq_2"], 4, j, UCOLS) for j in range(4)])
            for n, w in enumerate(("peer_keys1_2", "peer_keys2_2")):
                sp.wait_ge(unit_used, U_KEY + n - RING + 1)
                sp.dma_start(ring[:, (U_KEY + n) % RING, 0:1024].rearrange("p (h c) -> p h c", h=PH),
                             A[w][0].rearrange("h p c -> p h c")).then_inc(slot_full[(U_KEY + n) % RING], 16)
            sp.wait_ge(sel_ready, TT)
            sp.dma_start(gain_f, A["norm_f_g_2"].rearrange("(a n) -> a n", a=1).broadcast_to([P, D])).then_inc(gain_in, 16)
            for t in range(TT):
                sp.wait_ge(fin_out, t + 1)
                sp.dma_start(out[0, t * P:(t + 1) * P, :], zc[:, t, :]).then_inc(stored, 16)
            sp.wait_ge(stored, 16 * TT)

        def slot_after(unit):
            return slot_count(unit) + (16 if unit % RING == U_GATE % RING and unit >= U_GATE else 0)

        @block.gpsimd
        def _(pool):
            steps = [0]

            def link(ins):
                steps[0] += 1
                ins.then_inc(pool_c, 1)
                pool.wait_ge(pool_c, steps[0])

            nc.gpsimd.memset(ones[:], 1.0).then_inc(const_ready, 1)
            link(nc.gpsimd.memset(ident[:], 0.0))
            nc.gpsimd.affine_select(out=ident[:], in_=ident[:], compare_op=ALU.not_equal, fill=1.0, base=0,
                                    pattern=[[-1, P]], channel_multiplier=1).then_inc(const_ready, 1)
            link(nc.gpsimd.memset(rotT[:], 0.0))
            HR = ROPE // 2
            link(nc.gpsimd.affine_select(out=rotT[:, 0:HR], in_=rotT[:, 0:HR], compare_op=ALU.not_equal, fill=-1.0,
                                         base=-HR, pattern=[[-1, HR]], channel_multiplier=1))
            nc.gpsimd.affine_select(out=rotT[:, HR:ROPE], in_=rotT[:, HR:ROPE], compare_op=ALU.not_equal, fill=1.0,
                                    base=0, pattern=[[-1, HR]], channel_multiplier=1).then_inc(const_ready, 1)
            link(nc.gpsimd.memset(mask[:], 0.0))
            link(nc.gpsimd.affine_select(out=mask[:, 0, :], in_=mask[:, 0, :], compare_op=ALU.is_ge, fill=MASKED,
                                         base=0, pattern=[[-1, P]], channel_multiplier=1))
            nc.gpsimd.affine_select(out=mask[:, 2, :], in_=mask[:, 2, :], compare_op=ALU.is_ge, fill=MASKED,
                                    base=0, pattern=[[-1, P]], channel_multiplier=1).then_inc(const_ready, 1)
            nc.gpsimd.memset(halfpi[:], float(np.pi / 2)).then_inc(const_ready, 1)
            for k in range(TOPK):
                last = nc.gpsimd.memset(iota16[:, k:k + 1], float(k))
            last.then_inc(const_ready, 1)
            for i in range(HR):
                f = float(np.float32(ROPE_THETA) ** np.float32(-2.0 * i / ROPE))
                last = nc.gpsimd.memset(small[0:1, i:i + 1], f)
                last = nc.gpsimd.memset(small[0:1, HR + i:HR + i + 1], f)
            last.then_inc(const_ready, 1)

            n_pool = [0]
            for table in ("peer_u_2", "peer_v_2"):
                for t in range(TT):
                    base = n_pool[0] * SLOTS
                    n_pool[0] += 1
                    pool.wait_ge(sel_ready, t + 1)
                    with pool.Fori(0, SLOTS // GR) as i:
                        for j in range(GR):
                            pool.wait_ge(row_used, i * GR + (base + j + 1))
                            pool.sem_inc(pool_step, 1)
                            nc.gpsimd.tensor_copy(idx_r[:, j:j + 1], expert[:, bass.ds(i * GR + (t * SLOTS + j), 1)])\
                                .then_inc(idx_copied, 1)
                            pool.wait_ge(idx_copied, i * GR + (base + j + 1))
                            pool.sem_inc(pool_step, 1)
                            nc.gpsimd.indirect_dma_start(row[:, j, :], None, A[table][0],
                                                         bass.IndirectOffsetOnAxis(ap=idx_r[:, j:j + 1], axis=0))\
                                .then_inc(row_full[j], 16)

        @block.tensor
        def _(pe):
            mm = nc.tensor.matmul
            pe.wait_ge(const_ready, 7)
            pe.wait_ge(par_in, 16 * n_param_dmas)
            for t, tile in enumerate(PARAM_TILES):
                rows = sum(r for _, r in tile)
                c = PC[tile[0][0]]
                last = nc.tensor.transpose(pl[0][:, c:c + rows], prow[0:rows, t, :], ident[0:rows, 0:rows])
            last.then_inc(par_T, 1)
            mm(pl[1][:, 0:1], ones[0:1, :], ones[0:1, 0:1], start=True, stop=True)
            mm(pl[1][0:ROPE, 0:1], small[0:1, 0:ROPE], ones[0:1, 0:1], start=True, stop=True).then_inc(freq_done, 1)
            pe.wait_ge(x_in, 16 * TT)
            banks = [pg[0], pg[1], pg[2], pl[2], pl[3], pg[0], pg[1], pg[2]]
            for n, (t, f4) in enumerate((t, f4) for t in range(TT) for f4 in range(4)):
                if n >= 5:
                    pe.wait_ge(res_ready, n - 4)
                for f in range(4):
                    c = (f4 * 4 + f) * P
                    last = nc.tensor.transpose(banks[n][:, f * P:(f + 1) * P], xin[:, t, c:c + P], ident[:])
                last.then_inc(x_T, 1)

            def norm_total(n, sq):
                tiles = NORMS[n][1]
                if n:
                    pe.wait_ge(norm_inv, n)
                for t in range(tiles):
                    if t % 4 == 0:
                        pe.wait_ge(norm_sq, sq_count(n, t // 4))
                    last = mm(pnorm, ones[:], sq[:, t, :], start=(t == 0), stop=(t == tiles - 1))
                last.then_inc(norm_sum, 1)

            def project(bank, slot, k, c, j0, cols, rhs, at=0):
                w = ring[:, slot, 0:k * c].rearrange("p (k c) -> p k c", k=k)
                for t in range(k):
                    last = mm(bank[0:cols, at:at + S], w[:, t, j0:j0 + cols], rhs[:, t, :], start=(t == 0), stop=(t == k - 1))
                return last

            norm_total(NI["pre"], tmp)
            pe.wait_ge(norm_out, tiles_before(1))
            pe.wait_ge(par_ready, 2)
            for n in range(N_IN1):
                u = U_IN1 + n
                pe.wait_ge(slot_full[u % RING], slot_count(u))
                if n >= 4:
                    if n - 4 < 4:
                        pe.wait_ge(a_ready, n - 3)
                    elif n - 4 < 8:
                        pe.wait_ge(sig_ready, n - 7)
                    else:
                        pe.wait_ge(lat_ready, n - 11)
                else:
                    pe.wait_ge(res_ready, 8)
                if n < N_IN1 - 1:
                    project(pl[n % 4], u % RING, DT, UCOLS, 0, P, h, 0)
                    last = project(pl[n % 4], u % RING, DT, UCOLS, P, P, h, S)
                else:
                    last = project(pl[n % 4], u % RING, DT, ROPE, 0, ROPE, h, 0)
                last.then_inc(unit_used, 1)
            norm_total(NI["q"], tmp)
            norm_total(NI["kv"], tmp[:, 6:10, :])
            pe.wait_ge(conv_ready, CT)
            for t in range(CT):
                last = mm(pg[2][:, 0:S], ones[:], conv_a[:, t, :], start=(t == 0), stop=(t == CT - 1))
            last.then_inc(mean_sum, 1)
            pe.wait_ge(norm_out, tiles_before(NI["q"] + 1))
            pe.wait_ge(lat_ready, 6)
            for n in range(N_UQ):
                u = U_UQ + n
                pe.wait_ge(slot_full[u % RING], slot_count(u))
                if n >= 2:
                    pe.wait_ge(q_ready, 2 * (n - 1))
                for a in range(2):
                    project(pl[n], u % RING, QLT, 2 * QK, a * QK, NOPE, q_lat, a * S)
                for a in range(2):
                    last = project(pg[n % 2], u % RING, QLT, 2 * QK, a * QK + NOPE, ROPE, q_lat, a * S)
                last.then_inc(unit_used, 1)
            norm_total(NI["ln"], tmp)
            pe.wait_ge(norm_out, tiles_before(NI["kv"] + 1))
            pe.wait_ge(q_ready, 2 * N_UQ)
            for n in range(N_UKV):
                u = U_UKV + n
                pe.wait_ge(slot_full[u % RING], slot_count(u))
                w = ring[:, u % RING, :].rearrange("p (k h c) -> p k h c", k=KVT, h=4)
                for a in range(4):
                    for t in range(KVT):
                        mm(pl[2 * n + a // 2][:, a % 2 * S:(a % 2 + 1) * S], w[:, t, a, 0:NOPE], kv_lat[:, t, :],
                           start=(t == 0), stop=(t == KVT - 1))
                if n:
                    pe.wait_ge(kv_ready, 4)
                for tt in range(TT):
                    for t in range(KVT):
                        last = mm(pg[tt][:], kv_lat[:, t, tt * P:(tt + 1) * P], w[:, t, :, NOPE:NOPE + VH],
                                  start=(t == 0), stop=(t == KVT - 1))
                last.then_inc(unit_used, 1)
            norm_total(NI["conv"], tmp)
            pe.wait_ge(kv_ready, 8)
            for n in range(4):
                last = mm(pl[n][0:ROPE, :], rotT[:], q_pe[0:ROPE, 2 * n:2 * n + 2, :], start=True, stop=True)
            last = mm(pg[0][0:ROPE, 0:S], rotT[:], k_raw[0:ROPE, :], start=True, stop=True)
            last.then_inc(rot_done, 1)
            pe.wait_ge(roped, 1)

            def scores(hd):
                if hd >= 2:
                    pe.wait_ge(s_ready, hd - 1)
                for qt, at, n in ((0, 0, P), (1, P, S)):
                    q = slice(qt * P, (qt + 1) * P)
                    mm(pl[hd % 2][:, at:at + n], q_nope[:, hd, q], k_nope[:, hd, 0:n], start=True, stop=False)
                    last = mm(pl[hd % 2][:, at:at + n], q_pe[0:ROPE, hd, q], k_pe[0:ROPE, 0:n], start=False, stop=True)
                last.then_inc(s_done, 1)

            prob = tmp[:, 8:12, :].rearrange("p a b -> p (a b)")
            probT = tmp[:, 12:16, :].rearrange("p a b -> p (a b)")
            scores(0)
            for hd in range(HEADS):
                if hd + 1 < HEADS:
                    scores(hd + 1)
                b = hd % 2 * 512
                pe.wait_ge(prob_ready, hd + 1)
                if hd >= 2:
                    pe.wait_ge(pT_ready, hd - 1)
                for n in range(3):
                    last = nc.tensor.transpose(pl[2 + hd % 2][:, n * P:(n + 1) * P], prob[:, b + n * P:b + (n + 1) * P], ident[:])
                last.then_inc(pT_done, 1)
                pe.wait_ge(pT_ready, hd + 1)
                if hd >= 2:
                    pe.wait_ge(o_ready, hd - 1)
                v = slice(hd * VH, (hd + 1) * VH)
                mm(pg[1 + hd % 2][:, 0:S], v_tok[:, 0, v], probT[:, b:b + S], start=True, stop=False, skip_group_check=True)
                mm(pg[1 + hd % 2][:, P:S], v_tok[:, 1, v], probT[:, b + S:b + S + P], start=False, stop=True,
                   skip_group_check=True).then_inc(o_done, 1)
            norm_total(NI["attn"], tmp)

            def stream(first, count, rhs, ready):
                with pe.Fori(0, count // 4) as i:
                    for j in range(4):
                        u = first + j
                        pe.wait_ge(slot_full[u % RING], i * 16 + slot_after(u))
                        pe.wait_ge(ready, i * 4 + (j + 1))
                        project(pl[j], u % RING, DT, UCOLS, 0, P, rhs, 0)
                        project(pl[j], u % RING, DT, UCOLS, P, P, rhs, S).then_inc(unit_used, 1)

            pe.wait_ge(norm_out, tiles_before(NI["attn"] + 1))
            stream(U_OUT1, N_OUT, mix, out1_ready)
            norm_total(NI["post"], mix)
            norm_total(NI["ffn"], tmp)
            pe.wait_ge(norm_out, tiles_before(NI["ffn"] + 1))
            with pe.Fori(0, N_GU // 4) as i:
                for j in range(4):
                    u = U_GU + j
                    pe.wait_ge(slot_full[u % RING], i * 16 + slot_count(u))
                    pe.wait_ge(hid_ready if j % 2 else silu_ready, i * 2 + (j // 2 + 1))
                    project(pl[j], u % RING, DT, UCOLS, 0, P, h, 0)
                    project(pl[j], u % RING, DT, UCOLS, P, P, h, S).then_inc(unit_used, 1)
            pe.wait_ge(hid_ready, 2 + 2 * (N_GU // 4))
            with pe.Fori(0, N_DOWN // 8) as i:
                for j in range(2):
                    pe.wait_ge(down_ready, i * 2 + (j + 1))
                    for n in range(4):
                        u = U_DOWN + 4 * j + n
                        pe.wait_ge(slot_full[u % RING], i * 32 + slot_count(u))
                        w = ring[:, u % RING, 0:DK * UCOLS].rearrange("p (k c) -> p k c", k=DK)
                        for k in range(DK):
                            for f in range(2):
                                last = mm(pl[2 * j + f][:, 0:S], w[:, k, f * P:(f + 1) * P], hid[:, n * DK + k, :],
                                          start=(n == 0 and k == 0), stop=(n == 3 and k == DK - 1))
                        last.then_inc(unit_used, 1)
            norm_total(NI["postf"], mix)
            norm_total(NI["n1"], tmp)
            pe.wait_ge(norm_out, tiles_before(NI["n1"] + 1))
            stream(U_IN2, N_IN2, h, in2_ready)
            pe.wait_ge(slot_full[U_POOL % RING], slot_count(U_POOL))
            pe.wait_ge(in2_ready, 4 + N_IN2)
            w = ring[:, U_POOL % RING, 0:2048].rearrange("p (g k c) -> p g k c", g=4, k=2)
            for g in range(4):
                pe.wait_ge(pool_d, 2 * (g + 1))
                if g >= 3:
                    pe.wait_ge(pool_y, 2 * (g - 2))
                for f in range(2):
                    for k in range(2):
                        last = mm(pg[g % 3][:, f * S:(f + 1) * S], w[:, g, k, f * P:(f + 1) * P], p_d[:, 2 * g + k, :],
                                  start=(k == 0), stop=(k == 1))
                last.then_inc(pool_done, 1)
            pe.wait_ge(pool_done, 4)
            pe.sem_inc(unit_used, 1)
            pe.wait_ge(slot_full[U_GATE % RING], slot_count(U_GATE) + 16)
            w = ring[:, U_GATE % RING, 0:2048].rearrange("p (n h c) -> p n h c", n=2, h=8)
            for hd in range(8):
                pe.wait_ge(xc_ready, hd + 1)
                if hd >= 4:
                    pe.wait_ge(gates_ready, 2 * (hd - 3))
                for n in range(2):
                    last = mm(pl[hd % 4][:, n * S:(n + 1) * S], w[:, n, hd, :], l_xc[:, hd, :], start=True, stop=True)
                last.then_inc(gates_done, 1)
            pe.wait_ge(gates_done, 8)
            pe.sem_inc(unit_used, 1)
            pe.wait_ge(gates_ready, 16)
            pe.wait_ge(pool_y, 8)
            pe.wait_ge(lru_y, CT)
            stream(U_OUT2, N_OUT, mix, out2_ready)
            norm_total(NI["n2"], tmp)
            pe.wait_ge(norm_out, tiles_before(NI["n2"] + 1))
            stream(U_WQ, N_OUT, h, wq_ready)
            banks = [pg[0], pg[1], pg[2], pg[0]]
            for n in range(4):
                u = U_KEY + n // 2
                pe.wait_ge(slot_full[u % RING], slot_after(u))
                if n == 3:
                    pe.wait_ge(key_ready, 1)
                for f in range(4):
                    c = (n % 2 * 4 + f) * P
                    last = nc.tensor.transpose(banks[n][:, f * P:(f + 1) * P], ring[:, u % RING, c:c + P], ident[:])
                last.then_inc(key_T, 1)
            pe.wait_ge(wq_ready, 4 + N_OUT)
            pe.wait_ge(key_ready, 4)
            for n in range(8):
                t, half, h4 = n // 4, n // 2 % 2, n % 2
                if n >= 4:
                    pe.wait_ge(sc_ready, n - 3)
                for f in range(4):
                    hd = h4 * 4 + f
                    last = mm(pl[n % 4][:, f * P:(f + 1) * P], mix[:, 2 * hd + half, t * P:(t + 1) * P],
                              keysT[:, half * 8 + hd, :], start=True, stop=True)
                last.then_inc(sc_done, 1)
            for n in range(16):
                src, t, f4 = (h, res)[n // 8], n // 4 % 2, n % 4
                if n < 3:
                    pe.wait_ge(key_ready, 4)
                else:
                    pe.wait_ge(tok_ready, n - 2)
                for f in range(4):
                    last = nc.tensor.transpose(pg[n % 3][:, f * P:(f + 1) * P], src[:, f4 * 4 + f, t * P:(t + 1) * P], ident[:])
                last.then_inc(tok_T, 1)

        @block.scalar
        def _(act):
            def activation(*a, **k):
                return nc.scalar.activation(*a, **k)

            def copy(o, i):
                return nc.scalar.activation(o, i, ACT.Copy)

            def two(bank):
                return bank[:].rearrange("p (a b) -> p a b", a=2)

            def four(bank):
                return bank[:].rearrange("p (a b) -> p a b", a=4)

            def norm_squares(n, src, sq):
                tiles = NORMS[n][1]
                for t in range(0, tiles, 4):
                    e = min(t + 4, tiles)
                    activation(sq[:, t:e, :], src[:, t:e, :], ACT.Square).then_inc(norm_sq, 1)

            def norm_root(n):
                act.wait_ge(norm_inv, n + 1)
                if n:
                    act.wait_ge(norm_out, tiles_before(n))
                activation(rstd[:], invms[:], ACT.Sqrt).then_inc(norm_rstd, 1)

            act.wait_ge(par_T, 1)
            copy(par[:], pl[0][:, 0:NPARAM]).then_inc(par_ready, 1)
            act.wait_ge(freq_done, 1)
            copy(small[0:ROPE, 32:33], pl[1][0:ROPE, 0:1]).then_inc(par_ready, 1)
            banks = [pg[0], pg[1], pg[2], pl[2], pl[3], pg[0], pg[1], pg[2]]
            for n in range(8):
                act.wait_ge(x_T, n + 1)
                t, f4 = n // 4, n % 4
                copy(res[:, f4 * 4:f4 * 4 + 4, t * P:(t + 1) * P], four(banks[n])).then_inc(res_ready, 1)
            act.wait_ge(res_ready, 8)
            norm_squares(NI["pre"], res, tmp)
            norm_root(NI["pre"])
            for n in range(4):
                act.wait_ge(unit_used, U_IN1 + n + 1)
                copy(conv_a[:, 2 * n:2 * n + 2, :], two(pl[n % 4])).then_inc(a_ready, 1)
            for n in range(4):
                act.wait_ge(unit_used, U_IN1 + 5 + n)
                if n >= 2:
                    act.wait_ge(u_ready, n - 1)
                activation(sig[:, n % 2, :], pl[n % 4][:], ACT.Sigmoid).then_inc(sig_ready, 1)
            for n in range(5):
                act.wait_ge(unit_used, U_IN1 + 9 + n)
                dst = q_lat[:, 2 * n:2 * n + 2, :] if n < 3 else kv_lat[:, 2 * n - 6:2 * n - 4, :]
                copy(dst, two(pl[n % 4])).then_inc(lat_ready, 1)
            act.wait_ge(unit_used, U_IN1 + N_IN1)
            copy(k_raw[0:ROPE, :], pl[1][0:ROPE, 0:S]).then_inc(lat_ready, 1)
            act.wait_ge(lat_ready, 5)
            norm_squares(NI["q"], q_lat, tmp)
            norm_squares(NI["kv"], kv_lat, tmp[:, 6:10, :])
            norm_root(NI["q"])
            norm_root(NI["kv"])
            act.wait_ge(centred, CT)
            act.wait_ge(norm_sum, NI["kv"] + 1)
            norm_squares(NI["ln"], conv_a, tmp)
            for n in range(N_UQ):
                act.wait_ge(unit_used, U_UQ + n + 1)
                if n == 0:
                    act.wait_ge(u_ready, 4)
                    act.wait_ge(centred, CT)
                copy(q_nope[:, 2 * n:2 * n + 2, :], two(pl[n])).then_inc(q_ready, 1)
                copy(q_pe[0:ROPE, 2 * n:2 * n + 2, :], pg[n % 2][0:ROPE, :].rearrange("p (a b) -> p a b", a=2))\
                    .then_inc(q_ready, 1)
            norm_root(NI["ln"])
            for n in range(N_UKV):
                act.wait_ge(unit_used, U_UKV + n + 1)
                for a in range(2):
                    copy(v_tok[:, a, n * 512:(n + 1) * 512], pg[a][:]).then_inc(kv_ready, 1)
                for a in range(2):
                    copy(k_nope[:, 4 * n + 2 * a:4 * n + 2 * a + 2, :], two(pl[2 * n + a])).then_inc(kv_ready, 1)
            act.wait_ge(norm_out, tiles_before(NI["ln"] + 1))
            for c in range(CT):
                activation(mix[:, c, :], conv_a[:, c, :], ACT.Silu, bias=col("conv_ln_b", c)).then_inc(conv_silu, 1)
            act.wait_ge(conv_silu, CT)
            norm_squares(NI["conv"], mix, tmp)
            norm_root(NI["conv"])
            act.wait_ge(trig_arg, 2)
            activation(sinT[0:ROPE, :], sinT[0:ROPE, :], ACT.Sin).then_inc(trig_ready, 1)
            activation(cosT[0:ROPE, :], cosT[0:ROPE, :], ACT.Sin, bias=halfpi[0:ROPE, :], scale=-1.0).then_inc(trig_ready, 1)
            score = tmp[:, 0:4, :].rearrange("p a b -> p (a b)")
            prob = tmp[:, 8:12, :].rearrange("p a b -> p (a b)")
            probT = tmp[:, 12:16, :].rearrange("p a b -> p (a b)")

            def exponentials(hd):
                b = hd % 2 * 512
                act.wait_ge(s_max, hd + 1)
                if hd >= 2:
                    act.wait_ge(pT_done, hd - 1)
                m = 40 + hd % 2 * 4
                activation(prob[:, b:b + P], score[:, b:b + P], ACT.Exp, bias=small[:, m:m + 1],
                           accum_out=small[:, m + 2:m + 3]).then_inc(exp_ready, 1)
                activation(prob[:, b + P:b + 3 * P], score[:, b + P:b + 3 * P], ACT.Exp, bias=small[:, m + 1:m + 2],
                           accum_out=small[:, m + 3:m + 4]).then_inc(exp_ready, 1)

            exponentials(0)
            for hd in range(HEADS):
                if hd + 1 < HEADS:
                    exponentials(hd + 1)
                act.wait_ge(pT_done, hd + 1)
                if hd >= 2:
                    act.wait_ge(o_done, hd - 1)
                copy(probT[:, hd % 2 * 512:hd % 2 * 512 + 3 * P], pl[2 + hd % 2][:, 0:3 * P]).then_inc(pT_ready, 1)
                act.wait_ge(o_done, hd + 1)
                copy(mix[:, 8 + hd, :], pg[1 + hd % 2][:, 0:S]).then_inc(o_ready, 1)
            act.wait_ge(o_ready, HEADS)
            norm_squares(NI["attn"], mix[:, 8:16, :], tmp)
            norm_root(NI["attn"])

            def stream_copy(first, count, ready, dst):
                with act.Fori(0, count // 4) as i:
                    for j in range(4):
                        act.wait_ge(unit_used, i * 4 + (first + j + 1))
                        copy(dst[:, bass.ds(i * 8 + 2 * j, 2), :], two(pl[j])).then_inc(ready, 1)

            act.wait_ge(norm_sum, NI["attn"] + 1)
            act.sem_inc(out1_ready, 4)
            stream_copy(U_OUT1, N_OUT, out1_ready, tmp)
            act.wait_ge(out1_ready, 4 + N_OUT)
            norm_squares(NI["post"], tmp, mix)
            norm_root(NI["post"])
            act.wait_ge(res1_ready, 4)
            norm_squares(NI["ffn"], res, tmp)
            norm_root(NI["ffn"])
            act.sem_inc(silu_ready, 2)
            with act.Fori(0, N_GU // 4) as i:
                for j in range(2):
                    act.wait_ge(unit_used, i * 4 + (U_GU + 2 * j + 1))
                    act.wait_ge(hid_ready, i * 2 + (j + 1))
                    activation(silu[:, j, :], pl[2 * j][:], ACT.Silu).then_inc(silu_ready, 1)
            act.wait_ge(norm_sum, NI["ffn"] + 1)
            act.sem_inc(down_ready, 2)
            with act.Fori(0, N_DOWN // 8) as i:
                for j in range(2):
                    act.wait_ge(unit_used, i * 8 + (U_DOWN + 4 * j + 4))
                    copy(tmp[:, bass.ds(i * 4 + 2 * j, 1), :], pl[2 * j][:, 0:S].unsqueeze(1))
                    copy(tmp[:, bass.ds(i * 4 + (2 * j + 1), 1), :], pl[2 * j + 1][:, 0:S].unsqueeze(1)).then_inc(down_ready, 1)
            act.wait_ge(down_ready, 2 + N_DOWN // 4)
            norm_squares(NI["postf"], tmp, mix)
            norm_root(NI["postf"])
            act.wait_ge(res2_ready, 4)
            norm_squares(NI["n1"], res, tmp)
            norm_root(NI["n1"])
            act.wait_ge(lam_abs, 1)
            activation(small[:, 0:8], small[:, 0:8], ACT.Exp, scale=-1.0).then_inc(lam_exp, 1)
            act.sem_inc(in2_ready, 4)
            for n in range(N_IN2):
                act.wait_ge(unit_used, U_IN2 + n + 1)
                src = two(pl[n % 4])
                t = slice(2 * (n % 4), 2 * (n % 4) + 2)
                if n < 4:
                    copy(p_u[:, t, WMAX:], src).then_inc(in2_ready, 1)
                elif n < 8:
                    copy(l_x[:, t, LPAD:], src).then_inc(in2_ready, 1)
                else:
                    activation(l_gelu[:, t, :], src, ACT.Gelu_apprx_tanh).then_inc(in2_ready, 1)
            for hd in range(8):
                act.wait_ge(gates_done, hd + 1)
                activation(l_r[:, hd, :], pl[hd % 4][:, 0:S], ACT.Sigmoid, bias=col("gate_a_b_2", hd)).then_inc(gates_ready, 1)
                activation(l_i[:, hd, :], pl[hd % 4][:, S:2 * S], ACT.Sigmoid, bias=col("gate_x_b_2", hd)).then_inc(gates_ready, 1)
            act.wait_ge(lam_ready, 1)
            act.wait_ge(gates_ready, 16)
            for hd in range(8):
                activation(l_m[:, hd, :], l_r[:, hd, :], ACT.Tanh, scale=small[:, 16 + hd:17 + hd]).then_inc(decay, 1)
            act.wait_ge(decay, 8)
            for hd in range(8):
                activation(l_r[:, hd, :], l_r[:, hd, :], ACT.Exp, scale=small[:, 8 + hd:9 + hd]).then_inc(decay, 1)
            for hd in range(8):
                act.wait_ge(mult_arg, hd + 1)
                activation(l_m[:, hd, :], l_m[:, hd, :], ACT.Sqrt).then_inc(mult_ready, 1)
            act.wait_ge(pool_done, 4)
            act.sem_inc(out2_ready, 4)
            stream_copy(U_OUT2, N_OUT, out2_ready, tmp)
            act.wait_ge(res3_ready, 1)
            norm_squares(NI["n2"], res, tmp)
            norm_root(NI["n2"])
            act.sem_inc(wq_ready, 4)
            stream_copy(U_WQ, N_OUT, wq_ready, mix)
            banks = [pg[0], pg[1], pg[2], pg[0]]
            for n in range(4):
                act.wait_ge(key_T, n + 1)
                copy(keysT[:, 4 * n:4 * n + 4, :], four(banks[n])).then_inc(key_ready, 1)
            for n in range(8):
                act.wait_ge(sc_done, n + 1)
                t, half, h4 = n // 4, n // 2 % 2, n % 2
                copy(sc[:, t, half * 8 + h4 * 4:half * 8 + h4 * 4 + 4, :], four(pl[n % 4])).then_inc(sc_ready, 1)
            for n in range(16):
                act.wait_ge(tok_T, n + 1)
                dst, t, f4 = (zc, acc)[n // 8], n // 4 % 2, n % 4
                copy(dst[:, t, f4 * 512:(f4 + 1) * 512], pg[n % 3][:]).then_inc(tok_ready, 1)
            for t in range(TT):
                act.wait_ge(sel_max, t + 1)
                activation(gate[:, t, :], gate[:, t, :], ACT.Exp).then_inc(sel_exp, 1)
            for t in range(TT):
                act.wait_ge(dot_kept, (t + 1) * SLOTS // GR)
                d = dots[:, t * SLOTS:(t + 1) * SLOTS]
                activation(d, d, ACT.Gelu_apprx_tanh).then_inc(act_ready, 1)
            for t in range(TT):
                act.wait_ge(added, (t + 1) * SLOTS)
                activation(zc[:, t, :], acc[:, t, :], ACT.Square, accum_out=small[:, 32 + t:33 + t]).then_inc(fin_sq, 1)
                act.wait_ge(fin_inv, t + 1)
                activation(small[:, 36 + t:37 + t], small[:, 34 + t:35 + t], ACT.Sqrt).then_inc(fin_rstd, 1)

        @block.vector
        def _(dve):
            V = nc.vector
            steps = [0]

            def link(ins):
                steps[0] += 1
                ins.then_inc(dve_step, 1)
                dve.wait_ge(dve_step, steps[0])

            def norm_finish(n, src, gain, dst, d):
                tiles = NORMS[n][1]
                dve.wait_ge(norm_sum, n + 1)
                link(V.tensor_scalar(meansq[:], pnorm, 1.0 / d, EPS, ALU.mult, ALU.add))
                if n:
                    dve.wait_ge(norm_rstd, n)
                V.reciprocal(invms[:], meansq[:]).then_inc(norm_inv, 1)
                dve.wait_ge(norm_rstd, n + 1)
                for t in range(tiles):
                    V.scalar_tensor_tensor(dst[:, t, :], src[:, t, :], col(gain, t), rstd[:], ALU.mult, ALU.mult)\
                        .then_inc(norm_out, 1)

            TURN = 2 * np.pi
            T1 = 6.28125
            T2 = float(np.float32(np.round((TURN - T1) * 2.0 ** 21) / 2.0 ** 21))
            T3 = float(np.float32(TURN - T1 - T2))
            MAGIC = 1.5 * 2.0 ** 23
            a_ = angle[0:ROPE, :]
            s_ = sinT[0:ROPE, :]
            c_ = cosT[0:ROPE, :]
            dve.wait_ge(pos_in, 16)
            dve.wait_ge(par_ready, 2)
            link(V.tensor_copy(c_, a_.bitcast(I32)))
            link(V.tensor_scalar(a_, c_, small[0:ROPE, 32:33], None, ALU.mult))
            link(V.tensor_scalar(s_, a_, 1.0 / TURN, None, ALU.mult))
            link(V.tensor_scalar(s_, s_, MAGIC, None, ALU.add))
            link(V.tensor_scalar(s_, s_, MAGIC, None, ALU.subtract))
            for part in (T1, T2, T3):
                link(V.scalar_tensor_tensor(a_, s_, -part, a_, ALU.mult, ALU.add))
            V.tensor_scalar(s_, a_, 3.1415925, -3.1415925, ALU.min, ALU.max).then_inc(trig_arg, 1)
            V.scalar_tensor_tensor(c_, a_, -1.0, a_, ALU.mult, ALU.max).then_inc(trig_arg, 1)
            dve.wait_ge(x_T, 8)
            V.memset(conv_u[:, :, 0:CPAD], 0.0)

            norm_finish(NI["pre"], res, "pre_mix_norm", h, D)
            for n in range(4):
                dve.wait_ge(sig_ready, n + 1)
                dve.wait_ge(a_ready, n + 1)
                V.tensor_tensor(conv_u[:, 2 * n:2 * n + 2, CPAD:], conv_a[:, 2 * n:2 * n + 2, :],
                                sig[:, n % 2, :].rearrange("p (a b) -> p a b", a=2), ALU.mult).then_inc(u_ready, 1)
            dve.wait_ge(u_ready, 4)
            with_tap = 0
            base = steps[0]
            for k in range(CONV_K):
                for c in range(CT):
                    u = conv_u[:, c, k:k + S]
                    if k == 0:
                        ins = V.tensor_scalar(conv_a[:, c, :], u, conv_tap(0, c), col("conv_b", c), ALU.mult, ALU.add)
                    else:
                        dve.wait_ge(dve_step, base + with_tap - CT + 1)
                        ins = V.scalar_tensor_tensor(conv_a[:, c, :], u, conv_tap(k, c), conv_a[:, c, :], ALU.mult, ALU.add)
                    with_tap += 1
                    steps[0] += 1
                    ins.then_inc(dve_step, 1)
                    if k == CONV_K - 1:
                        dve.wait_ge(dve_step, steps[0])
                        dve.sem_inc(conv_ready, 1)
            norm_finish(NI["q"], q_lat, "q_norm", q_lat, QLT * P)
            norm_finish(NI["kv"], kv_lat, "kv_norm", kv_lat, KVT * P)
            dve.wait_ge(mean_sum, 1)
            link(V.tensor_scalar(mean_b, pg[2][:, 0:S], 1.0 / CONV_CH, None, ALU.mult))
            for c in range(CT):
                V.tensor_tensor(conv_a[:, c, :], conv_a[:, c, :], mean_b, ALU.subtract).then_inc(centred, 1)
            dve.wait_ge(centred, CT)
            norm_finish(NI["ln"], conv_a, "conv_ln_g", conv_a, CONV_CH)
            dve.wait_ge(conv_silu, CT)
            norm_finish(NI["conv"], mix, "conv_out_norm", mix, CONV_CH)
            dve.wait_ge(rot_done, 1)
            dve.wait_ge(trig_ready, 2)
            dve.wait_ge(norm_sum, NI["conv"] + 1)
            rot = tmp[0:ROPE, 0:HEADS, :]
            for n in range(4):
                link(V.tensor_tensor(rot[:, 2 * n:2 * n + 2, :], pl[n][0:ROPE, :].rearrange("p (a b) -> p a b", a=2),
                                     s_.unsqueeze(1).broadcast_to([ROPE, 2, S]), ALU.mult))
            link(V.tensor_tensor(q_pe[0:ROPE, :, :], q_pe[0:ROPE, :, :], c_.unsqueeze(1).broadcast_to([ROPE, HEADS, S]), ALU.mult))
            link(V.tensor_tensor(q_pe[0:ROPE, :, :], q_pe[0:ROPE, :, :], rot, ALU.add))
            link(V.tensor_tensor(rot[:, 0, :], pg[0][0:ROPE, 0:S], s_, ALU.mult))
            link(V.tensor_tensor(k_pe[0:ROPE, :], k_raw[0:ROPE, :], c_, ALU.mult))
            V.tensor_tensor(k_pe[0:ROPE, :], k_pe[0:ROPE, :], rot[:, 0, :], ALU.add).then_inc(roped, 1)
            score = tmp[:, 0:4, :].rearrange("p a b -> p (a b)")
            prob = tmp[:, 8:12, :].rearrange("p a b -> p (a b)")
            dve.wait_ge(roped, 1)

            def head_scores(hd):
                b = hd % 2 * 512
                m = 40 + hd % 2 * 4
                dve.wait_ge(s_done, hd + 1)
                if hd >= 2:
                    dve.wait_ge(exp_ready, 2 * (hd - 1))
                V.scalar_tensor_tensor(score[:, b:b + 3 * P], pl[hd % 2][:, 0:3 * P], SCALE,
                                       mask[:].rearrange("p a b -> p (a b)"), ALU.mult, ALU.add).then_inc(s_ready, 1)
                dve.wait_ge(s_ready, hd + 1)
                V.tensor_reduce(small[:, 48:49], score[:, b:b + P], AX.X, ALU.max)
                link(V.tensor_reduce(small[:, 49:50], score[:, b + P:b + 3 * P], AX.X, ALU.max))
                V.tensor_scalar(small[:, m:m + 2], small[:, 48:50], -1.0, None, ALU.mult).then_inc(s_max, 1)

            head_scores(0)
            for hd in range(HEADS):
                if hd + 1 < HEADS:
                    dve.wait_ge(s_max, hd + 1)
                    head_scores(hd + 1)
                b = hd % 2 * 512
                m = 42 + hd % 2 * 4
                dve.wait_ge(exp_ready, 2 * hd + 2)
                r = 52 + hd % 2 * 2
                link(V.reciprocal(small[:, r:r + 2], small[:, m:m + 2]))
                link(V.tensor_scalar(prob[:, b:b + P], prob[:, b:b + P], small[:, r:r + 1], None, ALU.mult))
                V.tensor_scalar(prob[:, b + P:b + 3 * P], prob[:, b + P:b + 3 * P], small[:, r + 1:r + 2], None, ALU.mult)\
                    .then_inc(prob_ready, 1)
            dve.wait_ge(prob_ready, HEADS)
            norm_finish(NI["attn"], mix[:, 8:16, :], "attn_out_norm", mix[:, 8:16, :], 1024)

            def add_residual(ready):
                for t in range(0, DT, 4):
                    V.tensor_tensor(res[:, t:t + 4, :], res[:, t:t + 4, :], tmp[:, t:t + 4, :], ALU.add).then_inc(ready, 1)

            norm_finish(NI["post"], tmp, "post_mix_norm", tmp, D)
            dve.wait_ge(norm_out, tiles_before(NI["post"] + 1))
            add_residual(res1_ready)
            dve.wait_ge(res1_ready, 4)
            norm_finish(NI["ffn"], res, "pre_ffn_norm", h, D)
            dve.sem_inc(hid_ready, 2)
            with dve.Fori(0, N_GU // 4) as i:
                for j in range(2):
                    dve.wait_ge(unit_used, i * 4 + (U_GU + 2 * j + 2))
                    dve.wait_ge(silu_ready, i * 2 + (j + 3))
                    V.tensor_tensor(hid[:, bass.ds(i * 4 + 2 * j, 2), :], silu[:, j, :].rearrange("p (a b) -> p a b", a=2),
                                    pl[2 * j + 1][:].rearrange("p (a b) -> p a b", a=2), ALU.mult).then_inc(hid_ready, 1)
            norm_finish(NI["postf"], tmp, "post_ffn_norm", tmp, D)
            dve.wait_ge(norm_out, tiles_before(NI["postf"] + 1))
            add_residual(res2_ready)
            lam = col("lru_lambda_2", 0, 8)
            V.scalar_tensor_tensor(small[:, 0:8], lam, -1.0, lam, ALU.mult, ALU.max).then_inc(lam_abs, 1)
            dve.wait_ge(res2_ready, 4)
            norm_finish(NI["n1"], res, "norm1_g_2", h, D)
            dve.wait_ge(lam_exp, 1)
            y, s8, s2, ser = small[:, 0:8], small[:, 24:32], small[:, 16:24], small[:, 8:16]
            link(V.tensor_scalar(s2, y, 2.0, None, ALU.add))
            link(V.reciprocal(s2, s2))
            link(V.tensor_tensor(s8, y, s2, ALU.mult))
            link(V.tensor_tensor(s2, s8, s8, ALU.mult))
            TERMS = 9
            link(V.tensor_scalar(ser, s2, 1.0 / (2 * TERMS + 1), 1.0 / (2 * TERMS - 1), ALU.mult, ALU.add))
            for n in range(TERMS - 2, -1, -1):
                link(V.tensor_tensor(ser, ser, s2, ALU.mult))
                link(V.tensor_scalar(ser, ser, 1.0 / (2 * n + 1), None, ALU.add))
            link(V.tensor_tensor(ser, ser, s8, ALU.mult))
            link(V.tensor_scalar(s2, lam, 0.0, None, ALU.min))
            link(V.scalar_tensor_tensor(ser, ser, -2.0, s2, ALU.mult, ALU.add))
            link(V.tensor_scalar(ser, ser, LRU_C, None, ALU.mult))
            V.tensor_scalar(s2, ser, -1.0, None, ALU.mult).then_inc(lam_ready, 1)
            V.memset(p_u[:, :, 0:WMAX], 0.0)
            V.memset(l_x[:, :, 0:LPAD], 0.0)
            for g, w in enumerate(POOL_WINDOWS):
                for n in range(w):
                    V.memset(edge[:, g, n:n + 1], 1.0 / (n + 1))
            link(V.memset(win, 0.0))
            link(V.memset(win2, 0.0))
            n_d = 0
            dve.wait_ge(norm_sum, NI["n1"] + 1)
            for g, w in enumerate(POOL_WINDOWS):
                dve.wait_ge(in2_ready, 4 + g + 1)
                for f in (2 * g, 2 * g + 1):
                    cur, other, step = p_u[:, f, :], win, 1
                    while step < w:
                        link(V.tensor_tensor(other[:, step:], cur[:, step:], cur[:, 0:WMAX + S - step], ALU.add))
                        cur, other, step = other, (win2 if other is win else win), 2 * step
                    V.scalar_tensor_tensor(p_d[:, f, w:], cur[:, WMAX + w:], 1.0 / w, p_u[:, f, WMAX + w:], ALU.mult, ALU.subtract)
                    link(V.tensor_tensor(p_d[:, f, 0:w], cur[:, WMAX:WMAX + w], edge[:, g, 0:w], ALU.mult))
                    link(V.tensor_tensor(p_d[:, f, 0:w], p_d[:, f, 0:w], p_u[:, f, WMAX:WMAX + w], ALU.subtract))
                    dve.sem_inc(pool_d, 1)
            for c in range(8):
                dve.wait_ge(in2_ready, 4 + 4 + c // 2 + 1)
                for k in range(LCONV):
                    src, wk = l_x[:, c, k:k + S], col("conv_w_2", k * 8 + c)
                    if k == 0:
                        ins = V.tensor_scalar(l_xc[:, c, :], src, wk, col("conv_b_2", c), ALU.mult, ALU.add)
                    else:
                        ins = V.scalar_tensor_tensor(l_xc[:, c, :], src, wk, l_xc[:, c, :], ALU.mult, ALU.add)
                    if k < LCONV - 1:
                        link(ins)
                    else:
                        ins.then_inc(xc_ready, 1)
            for g in range(4):
                dve.wait_ge(pool_done, g + 1)
                for f in range(2):
                    t = 2 * g + f
                    V.tensor_scalar(mix[:, t, :], pg[g % 3][:, f * S:(f + 1) * S], col("pool_b_2", t), col("pool_scale_2", t),
                                    ALU.add, ALU.mult).then_inc(pool_y, 1)
            dve.wait_ge(gates_ready, 16)
            dve.wait_ge(xc_ready, 8)
            link(V.tensor_tensor(l_i, l_i, l_xc, ALU.mult))
            for hd in range(8):
                dve.wait_ge(decay, 8 + hd + 1)
                link(V.tensor_tensor(l_xc[:, hd, :], l_r[:, hd, :], l_r[:, hd, :], ALU.mult))
                V.scalar_tensor_tensor(l_m[:, hd, :], l_xc[:, hd, :], 1.0, l_m[:, hd, :], ALU.add, ALU.mult).then_inc(mult_arg, 1)
            for hd in range(8):
                dve.wait_ge(mult_ready, hd + 1)
                link(V.tensor_tensor(l_i[:, hd, :], l_i[:, hd, :], l_m[:, hd, :], ALU.mult))
                link(V.tensor_tensor_scan(l_xc[:, hd, :], l_r[:, hd, :], l_i[:, hd, :], 0.0, ALU.mult, ALU.add))
                V.tensor_tensor(mix[:, 8 + hd, :], l_xc[:, hd, :], l_gelu[:, hd, :], ALU.mult).then_inc(lru_y, 1)
            dve.wait_ge(out2_ready, 4 + N_OUT)
            V.tensor_tensor(res[:], res[:], tmp[:], ALU.add).then_inc(res3_ready, 1)
            dve.wait_ge(res3_ready, 1)
            norm_finish(NI["n2"], res, "norm2_g_2", h, D)

            def wide(ap, axis, shape):
                return ap.unsqueeze(axis).broadcast_to(shape)

            for t in range(TT):
                dve.wait_ge(sc_ready, 4 * (t + 1))
                sets = [(sc[:, t, n, :], work[:, n, :], top_v[:, t, n, :], top_i[:, t, n, :]) for n in range(16)]
                for s, wk, v, ix in sets:
                    last = V.max(v[:, 0:8], s)
                link(last)
                for s, wk, v, ix in sets:
                    V.max_index(ix[:, 0:8], v[:, 0:8], s)
                    last = V.match_replace(wk, v[:, 0:8], s, NEG)
                link(last)
                for s, wk, v, ix in sets:
                    last = V.max(v[:, 8:16], wk)
                link(last)
                for s, wk, v, ix in sets:
                    last = V.max_index(ix[:, 8:16], v[:, 8:16], wk)
                link(last)
                cview = tmp[:, 0:PH, :]
                rest = tmp[:, PH:2 * PH, :]
                for hd in range(PH):
                    last = V.tensor_tensor(cview[:, hd, :].rearrange("p (a b) -> p a b", a=TOPK),
                                           wide(top_v[:, t, hd, :], 2, [P, TOPK, TOPK]),
                                           wide(top_v[:, t, 8 + hd, :], 1, [P, TOPK, TOPK]), ALU.add)
                link(last)
                for hd in range(PH):
                    last = V.max(ctop[:, hd, 0:8], cview[:, hd, :])
                link(last)
                for hd in range(PH):
                    V.max_index(cpos[:, hd, 0:8], ctop[:, hd, 0:8], cview[:, hd, :])
                    last = V.match_replace(rest[:, hd, :], ctop[:, hd, 0:8], cview[:, hd, :], NEG)
                link(last)
                for hd in range(PH):
                    last = V.max(ctop[:, hd, 8:16], rest[:, hd, :])
                link(last)
                for hd in range(PH):
                    last = V.max_index(cpos[:, hd, 8:16], ctop[:, hd, 8:16], rest[:, hd, :])
                link(last)
                ci = cpos[:].bitcast(I32)
                V.tensor_scalar(cposi[:, 0], ci, 4, None, ALU.logical_shift_right)
                link(V.tensor_scalar(cposi[:, 1], ci, 15, None, ALU.bitwise_and))
                V.tensor_copy(cposf[:, 0], cposi[:, 0])
                V.tensor_copy(cposf[:, 1], cposi[:, 1])
                link(V.tensor_copy(top_f[:], top_i[:, t]))
                full = [P, PH, TOPK, TOPK]
                for n in range(2):
                    pick = tmp[:, 8 * n:8 * n + 8, :].rearrange("p h (k j) -> p h k j", k=TOPK)
                    j16 = iota16[:].unsqueeze(1).unsqueeze(1).broadcast_to(full)
                    link(V.tensor_tensor(pick, wide(cposf[:, n], 3, full), j16, ALU.is_equal))
                    link(V.tensor_tensor(pick, pick, wide(top_f[:, 8 * n:8 * n + 8, :], 2, full), ALU.mult))
                    link(V.tensor_reduce(cposf[:, n], pick, AX.X, ALU.add))
                e = expert[:, t * SLOTS:(t + 1) * SLOTS].rearrange("p (h k) -> p h k", h=PH)
                V.scalar_tensor_tensor(e, cposf[:, 0], float(NKEY), cposf[:, 1], ALU.mult, ALU.add).then_inc(sel_ready, 1)
                g3 = gate[:, t, :].rearrange("p (h k) -> p h k", h=PH)
                V.tensor_tensor(g3, ctop[:], ctop[:, :, 0:1].broadcast_to([P, PH, TOPK]), ALU.subtract).then_inc(sel_max, 1)
                dve.wait_ge(sel_exp, t + 1)
                link(V.tensor_reduce(small[:, 0:8], g3, AX.X, ALU.add))
                link(V.reciprocal(small[:, 0:8], small[:, 0:8]))
                link(V.tensor_tensor(g3, g3, wide(small[:, 0:8], 2, [P, PH, TOPK]), ALU.mult))

            dve.wait_ge(tok_ready, 16)
            dve.sem_inc(row_used, GR)
            for t in range(TT):
                n0 = t * SLOTS
                with dve.Fori(0, SLOTS // GR) as i:
                    for j in range(GR):
                        dve.wait_ge(row_full[j], i * 16 + 16 * (t * (SLOTS // GR) + 1))
                        V.tensor_tensor_reduce(row[:, j, :], row[:, j, :], zc[:, t, :], 1.0, 0.0, ALU.mult, ALU.add,
                                               dot_r[:, j:j + 1]).then_inc(dot_done, 1)
                        dve.wait_ge(dot_done, i * GR + (n0 + j + 1))
                        dve.sem_inc(row_used, 1)
                    V.tensor_copy(dots[:, bass.ds(i * GR + n0, GR)], dot_r[:]).then_inc(dot_kept, 1)
                    dve.wait_ge(dot_kept, i + (t * (SLOTS // GR) + 1))
            for t in range(TT):
                dve.wait_ge(act_ready, t + 1)
                w = wts[:, t * SLOTS:(t + 1) * SLOTS]
                link(V.tensor_tensor(w, gate[:, t, :], dots[:, t * SLOTS:(t + 1) * SLOTS], ALU.mult))
            for t in range(TT):
                n0 = t * SLOTS
                with dve.Fori(0, SLOTS // GR) as i:
                    V.tensor_copy(w_r[:], wts[:, bass.ds(i * GR + n0, GR)]).then_inc(w_copied, 1)
                    dve.wait_ge(w_copied, i + (t * (SLOTS // GR) + 1))
                    for j in range(GR):
                        dve.wait_ge(row_full[j], i * 16 + 16 * ((TT + t) * (SLOTS // GR) + 1))
                        V.scalar_tensor_tensor(acc[:, t, :], row[:, j, :], w_r[:, j:j + 1], acc[:, t, :], ALU.mult, ALU.add)\
                            .then_inc(added, 1)
                        dve.wait_ge(added, i * GR + (n0 + j + 1))
                        dve.sem_inc(row_used, 1)
            dve.wait_ge(gain_in, 16)
            for t in range(TT):
                dve.wait_ge(fin_sq, t + 1)
                link(V.tensor_scalar(small[:, 34 + t:35 + t], small[:, 32 + t:33 + t], 1.0 / D, EPS, ALU.mult, ALU.add))
                link(V.reciprocal(small[:, 34 + t:35 + t], small[:, 34 + t:35 + t]))
                dve.sem_inc(fin_inv, 1)
                dve.wait_ge(fin_rstd, t + 1)
                V.scalar_tensor_tensor(zc[:, t, :], acc[:, t, :], small[:, 36 + t:37 + t], gain_f, ALU.mult, ALU.mult)\
                    .then_inc(fin_out, 1)


_INS = ['x', 'positions', 'pre_mix_norm', 'w_in', 'q_norm', 'w_uq', 'kv_norm', 'w_ukv', 'conv_w', 'conv_b', 'conv_ln_g',
        'conv_ln_b', 'conv_out_norm', 'attn_out_norm', 'w_out', 'post_mix_norm', 'pre_ffn_norm', 'w_gate', 'w_up',
        'w_down', 'post_ffn_norm', 'norm1_g_2', 'w_in_2', 'pool_w_2', 'pool_b_2', 'pool_scale_2', 'conv_w_2',
        'conv_b_2', 'gate_a_w_2', 'gate_a_b_2', 'gate_x_w_2', 'gate_x_b_2', 'lru_lambda_2', 'w_out_2', 'norm2_g_2',
        'peer_wq_2', 'peer_keys1_2', 'peer_keys2_2', 'peer_u_2', 'peer_v_2', 'norm_f_g_2']


def kernel(**inputs):
    import concourse.bacc as bacc
    from concourse.bass_utils import run_bass_kernel_spmd

    nc = bacc.Bacc("TRN2", target_bir_lowering=False, num_devices=1)
    arrays, args = {}, {}
    for name in _INS:
        a = np.ascontiguousarray(inputs[name])
        arrays[f"in_{name}"] = a
        args[name] = nc.dram_tensor(f"in_{name}", a.shape, mybir.dt.from_np(a.dtype), kind="ExternalInput").ap()
    out = nc.dram_tensor("out", (1, S, D), F32, kind="ExternalOutput").ap()
    build(nc, args, out)
    r = run_bass_kernel_spmd(nc, [arrays], core_ids=[0])
    return r.results[0]["out"]
```

```python
from contextlib import ExitStack

import numpy as np

import concourse.bass as bass
from concourse import mybir

ALU = mybir.AluOpType
ACT = mybir.ActivationFunctionType
AX = mybir.AxisListType
F32 = mybir.dt.float32
F32R = mybir.dt.float32r
I32 = mybir.dt.int32
U32 = mybir.dt.uint32

P = 128
S = 256
TT = S // P
D = 2048
DT = D // P
CONV_CH = 1024
CT = CONV_CH // P
CONV_K = 31
HEADS = 8
NOPE, ROPE, VH = 128, 64, 128
QK = NOPE + ROPE
QLT = 768 // P
KVT = 512 // P
DFF = 5632
FT = DFF // P
EPS = 1e-6
ROPE_THETA = 10000.0
SCALE = float(QK) ** -0.5
MASKED = -1e30
POOL_WINDOWS = (2, 4, 8, 16)
WMAX = max(POOL_WINDOWS)
LRU_C = 8.0
LCONV = 4
PH = 8
NKEY = 128
TOPK = 16
HSLOTS = TT * TOPK
SLOTS = PH * HSLOTS
GR = 4
NEG = -3.0e38

RING = 4
UNIT = 2048
KU = 8
CG = 256
HCH = 16
CHUNKS = [(c, min(HCH, FT - c)) for c in range(0, FT, HCH)]


def unit_plan():
    seq = [("in1", 26, True), ("kraw", 1, False), ("uq", HEADS, False), ("ukv", HEADS // 2, False), ("out1", 16, True)]
    for j, (_, n) in enumerate(CHUNKS):
        seq += [(f"gu{j}", 2 * n, True), (f"down{j}", 16, True)]
    seq += [("in2a", 16, True), ("gates", 2, False), ("in2b", 8, True), ("pool", 1, False), ("out2", 16, True),
            ("keys", 2, False), ("wq", 16, True)]
    unit, piece, plain, free = {}, {}, {}, []
    n_piece = n_plain = 0
    for name, n, split in seq:
        unit[name], piece[name], plain[name] = len(free), n_piece, n_plain
        for _ in range(n):
            if split:
                n_piece += 2
                free.append((True, n_piece))
            else:
                n_plain += 1
                free.append((False, n_plain))
    return unit, piece, plain, free


UNIT0, PIECE0, PLAIN0, FREE = unit_plan()

NORMS = (("pre", 16), ("q", QLT), ("kv", KVT), ("ln", CT), ("conv", CT), ("attn", 8), ("post", 16),
         ("ffn", 16), ("postf", 16), ("n1", 16), ("n2", 16))
NI = {name: n for n, (name, _) in enumerate(NORMS)}

SPLITS = {"in1": 0, "out1": 1, "ffn": 2, "in2": 3, "out2": 4, "wq": 5}

PARAM_TILES = (
    (("pre_mix_norm", 16), ("q_norm", 6), ("kv_norm", 4), ("conv_b", 8), ("conv_ln_g", 8), ("conv_ln_b", 8),
     ("conv_out_norm", 8), ("attn_out_norm", 8), ("post_mix_norm", 16), ("pre_ffn_norm", 16), ("post_ffn_norm", 16)),
    (("norm1_g_2", 16), ("pool_b_2", 8), ("pool_scale_2", 8), ("conv_b_2", 8), ("gate_a_b_2", 8), ("gate_x_b_2", 8),
     ("lru_lambda_2", 8), ("norm2_g_2", 16), ("conv_w_2", LCONV * 8)),
    (("conv_w_lo", 16 * CT),),
    (("conv_w_hi", (CONV_K - 16) * CT),),
)


def param_columns():
    at, col = {}, 0
    for tile in PARAM_TILES:
        for name, rows in tile:
            at[name] = col
            col += rows
    return at, col


def build(nc, A, out):
    PC, NPARAM = param_columns()
    n_param_dmas = sum(len(t) for t in PARAM_TILES)

    with ExitStack() as ctx:
        def sem(name):
            return ctx.enter_context(nc.semaphore(name))

        base = -(-nc.sbuf_base // 64) * 64
        place = {}
        at = base
        for name, words in (("raw", RING * UNIT), ("whi", 4 * 1024), ("wlo", 4 * 1024), ("xhi", DT * S), ("xlo", DT * S),
                            ("res", DT * S), ("tmp", DT * S), ("mix", DT * S), ("arena", 10240), ("rest", 3200)):
            place[name] = at
            at += words * 4

        def sb(name, region, start, shape, dt=F32):
            return nc.alloc_sbuf_tensor_at(name, shape, dt, offset=place[region] + 4 * start)

        raw = sb("raw", "raw", 0, [P, RING, UNIT])
        whi = sb("whi", "whi", 0, [P, 4, KU, P], F32R)
        wlo = sb("wlo", "wlo", 0, [P, 4, KU, P], F32R)
        xhi = sb("xhi", "xhi", 0, [P, DT, S], F32R)
        xlo = sb("xlo", "xlo", 0, [P, DT, S], F32R)
        res = sb("res", "res", 0, [P, DT, S])
        tmp = sb("tmp", "tmp", 0, [P, DT, S])
        mix = sb("mix", "mix", 0, [P, DT, S])

        r_at = [0]

        def keep(name, shape, dt=F32):
            n = int(np.prod(shape[1:]))
            t = sb(name, "rest", r_at[0], shape, dt)
            r_at[0] += -(-n // 8) * 8
            assert r_at[0] <= 3200
            return t

        par = keep("par", [P, NPARAM])
        ident = keep("ident", [P, P])
        ones = keep("ones", [P, P])
        rotT = keep("rotT", [ROPE, ROPE])
        mask = keep("mask", [P, 3, P])
        meansq = keep("meansq", [P, S])
        invms = keep("invms", [P, S])
        rstd = keep("rstd", [P, S])
        small = keep("small", [P, 64])
        halfpi = keep("halfpi", [P, 1])
        iota16 = keep("iota16", [P, TOPK])
        dot_r = keep("dot_r", [P, GR])
        idx_r = keep("idx_r", [P, GR], I32)
        w_r = keep("w_r", [P, HSLOTS])
        gate = keep("gate", [P, SLOTS])
        expert = keep("expert", [P, SLOTS], I32)
        dots = keep("dots", [P, SLOTS])

        CPAD = CONV_K - 1
        prow = sb("prow", "tmp", 0, [P, len(PARAM_TILES), P])
        xin = sb("xin", "mix", 0, [P, TT, D])
        conv_a = sb("conv_a", "arena", 0, [P, CT, S])
        conv_u = sb("conv_u", "arena", 2048, [P, CT, CPAD + S])
        q_lat = sb("q_lat", "arena", 4336, [P, QLT, S])
        kv_lat = sb("kv_lat", "arena", 5872, [P, KVT, S])
        k_raw = sb("k_raw", "arena", 6896, [P, S])
        sig = sb("sig", "arena", 7152, [P, 2, 2, S])
        mean_b = sb("mean_b", "arena", 8176, [P, S])
        angle = sb("angle", "arena", 8432, [P, S])
        cosT = sb("cosT", "arena", 8688, [P, S])
        sinT = sb("sinT", "arena", 8944, [P, S])
        k_pe = sb("k_pe", "arena", 9200, [P, S])
        q_nope = sb("q_nope", "xhi", 0, [P, HEADS, S])
        q_pe = sb("q_pe", "xhi", 2048, [P, HEADS, S])
        k_nope = sb("k_nope", "xlo", 0, [P, HEADS, S])
        v_tok = sb("v_tok", "xlo", 2048, [P, TT, HEADS * VH])
        hhi = sb("hhi", "arena", 0, [P, HCH, S], F32R)
        hlo = sb("hlo", "arena", HCH * S, [P, HCH, S], F32R)
        silu = sb("silu", "arena", 2 * HCH * S, [P, 2, S])
        hid = sb("hid", "arena", 2 * HCH * S + 2 * S, [P, 2, S])
        LPAD = LCONV - 1
        p_u = sb("p_u", "arena", 0, [P, 8, WMAX + S])
        l_x = sb("l_x", "arena", 2176, [P, 8, LPAD + S])
        l_i = sb("l_i", "arena", 2176, [P, 8, S])
        l_gelu = sb("l_gelu", "arena", 4248, [P, 8, S])
        l_xc = sb("l_xc", "arena", 6296, [P, 8, S])
        win = sb("win", "arena", 8344, [P, WMAX + S])
        win2 = sb("win2", "arena", 8616, [P, WMAX + S])
        edge = sb("edge", "arena", 8888, [P, len(POOL_WINDOWS), WMAX])
        p_d = tmp[:, 0:8, :]
        l_m = tmp[:, 8:16, :]
        l_r = mix[:, 8:16, :]
        zc = sb("zc", "arena", 0, [P, TT, D])
        acc = sb("acc", "arena", TT * D, [P, TT, D])
        keysT = sb("keysT", "arena", 2 * TT * D, [P, 2 * PH, NKEY])
        row = [sb(f"row{n}", ("res", "tmp")[n // 2], n % 2 * D, [P, D]) for n in range(GR)]
        qh = sb("qh", "mix", 0, [P, 2, 2, S])
        sc = sb("sc", "mix", 1024, [P, 2, 4, NKEY])
        work = sb("work", "mix", 2048, [P, 4, NKEY])
        cand = sb("cand", "mix", 2560, [P, TT, TOPK * TOPK])
        cand2 = sb("cand2", "mix", 3072, [P, TT, TOPK * TOPK])
        top_v = sb("top_v", "mix", 3584, [P, 4, TOPK])
        top_i = sb("top_i", "mix", 3648, [P, 4, TOPK], U32)
        top_f = sb("top_f", "mix", 3712, [P, 4, TOPK])
        ctop = sb("ctop", "mix", 3776, [P, TT, TOPK])
        cpos = sb("cpos", "mix", 3808, [P, TT, TOPK], U32)
        cposi = sb("cposi", "mix", 3840, [P, 2, TT, TOPK], I32)
        cposf = sb("cposf", "mix", 3904, [P, 2, TT, TOPK])
        gain_f = sb("gain_f", "raw", 0, [P, D])

        pl = [ctx.enter_context(nc.psum_tensor(f"pl{n}", [P, 512], F32)) for n in range(4)]
        pg = [ctx.enter_context(nc.psum_tensor(f"pg{n}", [P, 512], F32)) for n in range(4)]
        pnorm = pg[3][:, 0:S]

        x_in = sem("x_in")
        par_in = sem("par_in")
        pos_in = sem("pos_in")
        slot_full = [sem(f"slot_full{n}") for n in range(RING)]
        w_hi = sem("w_hi")
        w_lo = sem("w_lo")
        piece_used = sem("piece_used")
        plain_used = sem("plain_used")
        x_hi = sem("x_hi")
        x_lo = sem("x_lo")
        const_ready = sem("const_ready")
        par_T = sem("par_T")
        par_ready = sem("par_ready")
        x_T = sem("x_T")
        res_ready = sem("res_ready")
        norm_sq = sem("norm_sq")
        norm_sum = sem("norm_sum")
        norm_inv = sem("norm_inv")
        norm_rstd = sem("norm_rstd")
        norm_out = sem("norm_out")
        in1_ready = sem("in1_ready")
        u_ready = sem("u_ready")
        conv_step = sem("conv_step")
        mean_sum = sem("mean_sum")
        centred = sem("centred")
        conv_silu = sem("conv_silu")
        q_ready = sem("q_ready")
        kv_ready = sem("kv_ready")
        freq_done = sem("freq_done")
        trig_arg = sem("trig_arg")
        trig_ready = sem("trig_ready")
        rot_done = sem("rot_done")
        roped = sem("roped")
        s_done = sem("s_done")
        s_ready = sem("s_ready")
        s_max = sem("s_max")
        exp_ready = sem("exp_ready")
        prob_ready = sem("prob_ready")
        pT_done = sem("pT_done")
        pT_ready = sem("pT_ready")
        o_done = sem("o_done")
        o_ready = sem("o_ready")
        out1_ready = sem("out1_ready")
        res1_ready = sem("res1_ready")
        silu_ready = sem("silu_ready")
        mul_ready = sem("mul_ready")
        hid_hi = sem("hid_hi")
        hid_lo = sem("hid_lo")
        down_ready = sem("down_ready")
        res2_ready = sem("res2_ready")
        in2_ready = sem("in2_ready")
        pool_d = sem("pool_d")
        pool_done = sem("pool_done")
        pool_y = sem("pool_y")
        xc_ready = sem("xc_ready")
        gates_done = sem("gates_done")
        gates_ready = sem("gates_ready")
        lam_abs = sem("lam_abs")
        lam_exp = sem("lam_exp")
        lam_ready = sem("lam_ready")
        decay = sem("decay")
        mult_arg = sem("mult_arg")
        mult_ready = sem("mult_ready")
        lru_y = sem("lru_y")
        out2_ready = sem("out2_ready")
        res3_ready = sem("res3_ready")
        tok_T = sem("tok_T")
        tok_z = sem("tok_z")
        tok_r = sem("tok_r")
        key_T = sem("key_T")
        key_ready = sem("key_ready")
        wq_ready = sem("wq_ready")
        sc_done = sem("sc_done")
        sc_ready = sem("sc_ready")
        sel_max = sem("sel_max")
        sel_exp = sem("sel_exp")
        sel_ready = sem("sel_ready")
        gain_in = sem("gain_in")
        idx_copied = sem("idx_copied")
        pool_step = sem("pool_step")
        row_full = [sem(f"row_full{n}") for n in range(GR)]
        row_used = sem("row_used")
        dot_done = sem("dot_done")
        dot_kept = sem("dot_kept")
        act_ready = sem("act_ready")
        w_copied = sem("w_copied")
        added = sem("added")
        fin_sq = sem("fin_sq")
        fin_inv = sem("fin_inv")
        fin_rstd = sem("fin_rstd")
        fin_out = sem("fin_out")
        stored = sem("stored")
        dve_step = sem("dve_step")
        const_step = sem("const_step")

        def landed(unit):
            return 16 * (unit // RING + 1)

        def sq_count(n, t4):
            return sum(-(-k // 4) for _, k in NORMS[:n]) + t4 + 1

        def tiles_before(n):
            return sum(k for _, k in NORMS[:n])

        def col(name, t=0, n=1):
            return par[:, PC[name] + t:PC[name] + t + n]

        def conv_tap(k, c):
            return col("conv_w_lo", k * CT + c) if k < 16 else col("conv_w_hi", (k - 16) * CT + c)

        def plain(unit, *shape):
            n = int(np.prod(shape))
            v = raw[:, unit % RING, 0:n]
            if len(shape) == 2:
                return v.rearrange("p (a b) -> p a b", a=shape[0])
            return v.rearrange("p (a b c) -> p a b c", a=shape[0], b=shape[1])

        IN1_COLS = [c for j in range(4) for c in (j * CG, CONV_CH + j * CG)] + [2 * CONV_CH + j * CG for j in range(5)]
        IN2_COLS = [CONV_CH + j * CG for j in range(4)] + [j * CG for j in range(4)] + [2 * CONV_CH + j * CG for j in range(4)]

        block = ctx.enter_context(nc.Block())

        @block.sync
        def _(sp):
            for t in range(TT):
                sp.dma_start(xin[:, t, :], A["x"][0, t * P:(t + 1) * P, :]).then_inc(x_in, 16)

            def slot_free(unit, i=None, step=0):
                if unit < RING:
                    return
                split, count = FREE[unit - RING]
                s = w_lo if split else plain_used
                if i is None:
                    sp.wait_ge(s, count)
                else:
                    sp.wait_ge(s, i * step + (count - step))

            def split_unit(unit, src, k=KU):
                dst = raw[:, unit % RING, 0:k * CG].rearrange("p (k c) -> p k c", k=k)
                sp.dma_start(dst, src).then_inc(slot_full[unit % RING], 16)

            def block_of(w, k0, k, cols, c=CG):
                return w[0, k0 * P:(k0 + k) * P, cols:cols + c].rearrange("(k p) c -> p k c", p=P)

            def group(unit, w, cols):
                for half in range(2):
                    slot_free(unit + half)
                    split_unit(unit + half, block_of(w, half * KU, KU, cols))

            def groups(unit, n, parts):
                for j, (w, cols, step, k0, k) in enumerate(parts):
                    for half in range(2):
                        u = unit + 2 * j + half
                        slot_free(u)
                        split_unit(u, block_of(w, k0 + half * k, k, cols), k)
                with sp.Fori(1, n) as i:
                    for j, (w, cols, step, k0, k) in enumerate(parts):
                        for half in range(2):
                            u = unit + 2 * j + half
                            slot_free(u + RING, i, 8)
                            src = w[0, (k0 + half * k) * P:(k0 + (half + 1) * k) * P, bass.ds(i * step + cols, CG)]
                            split_unit(u, src.rearrange("(k p) c -> p k c", p=P), k)

            for n in range(2):
                group(UNIT0["in1"] + 2 * n, A["w_in"], IN1_COLS[n])
            for t, tile in enumerate(PARAM_TILES):
                r = 0
                for name, rows in tile:
                    if name == "conv_w_lo":
                        src = A["conv_w"][0, 0:16, :]
                    elif name == "conv_w_hi":
                        src = A["conv_w"][0, 16:CONV_K, :]
                    else:
                        src = A[name][0]
                        if len(src.shape) == 1:
                            src = src.rearrange("(a n) -> a n", a=1)
                    flat = src.rearrange("a n -> (a n)").rearrange("(r c) -> r c", c=P)
                    sp.dma_start(prow[r:r + rows, t, :], flat).then_inc(par_in, 16)
                    r += rows
            sp.dma_start(angle[:].bitcast(I32), A["positions"].broadcast_to([P, S])).then_inc(pos_in, 16)
            for n in range(2, len(IN1_COLS)):
                group(UNIT0["in1"] + 2 * n, A["w_in"], IN1_COLS[n])
            u = UNIT0["kraw"]
            slot_free(u)
            c = 2 * CONV_CH + (QLT + KVT) * P
            sp.dma_start(plain(u, DT, ROPE), block_of(A["w_in"], 0, DT, c, ROPE)).then_inc(slot_full[u % RING], 16)
            for hd in range(HEADS):
                u = UNIT0["uq"] + hd
                slot_free(u)
                sp.dma_start(plain(u, QLT, QK), block_of(A["w_uq"], 0, QLT, hd * QK, QK)).then_inc(slot_full[u % RING], 16)
            for n in range(HEADS // 2):
                u = UNIT0["ukv"] + n
                c = 2 * (NOPE + VH)
                slot_free(u)
                sp.dma_start(plain(u, KVT, c), block_of(A["w_ukv"], 0, KVT, n * c, c)).then_inc(slot_full[u % RING], 16)
            groups(UNIT0["out1"], 4, [(A["w_out"], j * CG, 2 * CG, 0, KU) for j in range(2)])
            for j, (t0, n) in enumerate(CHUNKS):
                groups(UNIT0[f"gu{j}"], n // 2, [(A[w], t0 * P, CG, 0, KU) for w in ("w_gate", "w_up")])
                groups(UNIT0[f"down{j}"], 4, [(A["w_down"], a * CG, 2 * CG, t0, n // 2) for a in range(2)])
            for n in range(8):
                group(UNIT0["in2a"] + 2 * n, A["w_in_2"], IN2_COLS[n])
            for n, w in enumerate(("gate_a_w_2", "gate_x_w_2")):
                u = UNIT0["gates"] + n
                slot_free(u)
                sp.dma_start(plain(u, 8, P), A[w][0].rearrange("h p c -> p h c")).then_inc(slot_full[u % RING], 16)
            for n in range(8, 12):
                group(UNIT0["in2b"] + 2 * (n - 8), A["w_in_2"], IN2_COLS[n])
            u = UNIT0["pool"]
            slot_free(u)
            sp.dma_start(plain(u, 4, 2, 2 * P), A["pool_w_2"][0].rearrange("g (k p) c -> p g k c", p=P)).then_inc(slot_full[u % RING], 16)
            groups(UNIT0["out2"], 4, [(A["w_out_2"], j * CG, 2 * CG, 0, KU) for j in range(2)])
            for n, w in enumerate(("peer_keys1_2", "peer_keys2_2")):
                u = UNIT0["keys"] + n
                slot_free(u)
                sp.dma_start(plain(u, PH, P), A[w][0].rearrange("h p c -> p h c")).then_inc(slot_full[u % RING], 16)
            groups(UNIT0["wq"], 4, [(A["peer_wq_2"], j * CG, 2 * CG, 0, KU) for j in range(2)])
            sp.wait_ge(w_lo, FREE[-1][1])
            sp.dma_start(gain_f[:], A["norm_f_g_2"].rearrange("(a n) -> a n", a=1).broadcast_to([P, D])).then_inc(gain_in, 16)
            for t in range(TT):
                sp.wait_ge(fin_out, t + 1)
                sp.dma_start(out[0, t * P:(t + 1) * P, :], zc[:, t, :]).then_inc(stored, 16)
            sp.wait_ge(stored, 16 * TT)

        @block.gpsimd
        def _(pool):
            steps = [0]

            def link(ins):
                steps[0] += 1
                ins.then_inc(const_step, 1)
                pool.wait_ge(const_step, steps[0])

            nc.gpsimd.memset(ones[:], 1.0).then_inc(const_ready, 1)
            link(nc.gpsimd.memset(ident[:], 0.0))
            nc.gpsimd.affine_select(out=ident[:], in_=ident[:], compare_op=ALU.not_equal, fill=1.0, base=0,
                                    pattern=[[-1, P]], channel_multiplier=1).then_inc(const_ready, 1)
            HR = ROPE // 2
            link(nc.gpsimd.memset(rotT[:], 0.0))
            link(nc.gpsimd.affine_select(out=rotT[:, 0:HR], in_=rotT[:, 0:HR], compare_op=ALU.not_equal, fill=-1.0,
                                         base=-HR, pattern=[[-1, HR]], channel_multiplier=1))
            nc.gpsimd.affine_select(out=rotT[:, HR:ROPE], in_=rotT[:, HR:ROPE], compare_op=ALU.not_equal, fill=1.0,
                                    base=0, pattern=[[-1, HR]], channel_multiplier=1).then_inc(const_ready, 1)
            for i in range(HR):
                f = float(np.float32(ROPE_THETA) ** np.float32(-2.0 * i / ROPE))
                nc.gpsimd.memset(small[0:1, i:i + 1], f)
                last = nc.gpsimd.memset(small[0:1, HR + i:HR + i + 1], f)
            last.then_inc(const_ready, 1)
            link(nc.gpsimd.memset(mask[:], 0.0))
            link(nc.gpsimd.affine_select(out=mask[:, 0, :], in_=mask[:, 0, :], compare_op=ALU.is_ge, fill=MASKED,
                                         base=0, pattern=[[-1, P]], channel_multiplier=1))
            nc.gpsimd.affine_select(out=mask[:, 2, :], in_=mask[:, 2, :], compare_op=ALU.is_ge, fill=MASKED,
                                    base=0, pattern=[[-1, P]], channel_multiplier=1).then_inc(const_ready, 1)
            nc.gpsimd.memset(halfpi[:], float(np.pi / 2)).then_inc(const_ready, 1)
            for k in range(TOPK):
                last = nc.gpsimd.memset(iota16[:, k:k + 1], float(k))
            last.then_inc(const_ready, 1)

            for n, table in enumerate(("peer_u_2", "peer_v_2")):
                with pool.Fori(0, PH) as hd:
                    if n == 0:
                        pool.wait_ge(sel_ready, hd + 1)
                        pool.sem_inc(pool_step, 1)
                    for j in range(HSLOTS):
                        done = n * SLOTS + j
                        pool.wait_ge(row_used, hd * HSLOTS + (done + 1))
                        pool.sem_inc(pool_step, 1)
                        nc.gpsimd.tensor_copy(idx_r[:, j % GR:j % GR + 1], expert[:, bass.ds(hd * HSLOTS + j, 1)])\
                            .then_inc(idx_copied, 1)
                        pool.wait_ge(idx_copied, hd * HSLOTS + (done + 1))
                        pool.sem_inc(pool_step, 1)
                        nc.gpsimd.indirect_dma_start(row[j % GR][:], None, A[table][0],
                                                     bass.IndirectOffsetOnAxis(ap=idx_r[:, j % GR:j % GR + 1], axis=0))\
                            .then_inc(row_full[j % GR], 16)

        @block.tensor
        def _(pe):
            mm = nc.tensor.matmul
            pe.wait_ge(const_ready, 4)
            pe.wait_ge(par_in, 16 * n_param_dmas)
            for t, tile in enumerate(PARAM_TILES):
                rows = sum(r for _, r in tile)
                c = PC[tile[0][0]]
                last = nc.tensor.transpose(pl[0][:, c:c + rows], prow[0:rows, t, :], ident[0:rows, 0:rows])
            last.then_inc(par_T, 1)
            mm(pl[1][0:ROPE, 0:1], small[0:1, 0:ROPE], ones[0:1, 0:1], start=True, stop=True).then_inc(freq_done, 1)
            pe.wait_ge(x_in, 16 * TT)
            banks = [pg[0], pg[1], pg[2], pl[2], pl[3], pg[0], pg[1], pg[2]]
            for n, (t, f4) in enumerate((t, f4) for t in range(TT) for f4 in range(4)):
                if n >= 5:
                    pe.wait_ge(res_ready, n - 4)
                for f in range(4):
                    c = (f4 * 4 + f) * P
                    last = nc.tensor.transpose(banks[n][:, f * P:(f + 1) * P], xin[:, t, c:c + P], ident[:])
                last.then_inc(x_T, 1)

            def norm_total(n, sq):
                tiles = NORMS[n][1]
                if n:
                    pe.wait_ge(norm_inv, n)
                for t in range(tiles):
                    if t % 4 == 0:
                        pe.wait_ge(norm_sq, sq_count(n, t // 4))
                    last = mm(pnorm, ones[:], sq[:, t, :], start=(t == 0), stop=(t == tiles - 1))
                last.then_inc(norm_sum, 1)

            def group(piece, banks, xh=xhi, xl=xlo, k=KU, i=None, step=0):
                for half in range(2):
                    for f in range(2):
                        n = piece + 2 * half + f
                        pe.wait_ge(w_hi, n + 1 if i is None else i * step + (n + 1))
                        for t in range(k):
                            w, x = whi[:, n % 4, t, :], half * k + t
                            mm(banks[f][:, 0:S], w, xh[:, x, :], start=(half == 0 and t == 0), stop=False)
                            mm(banks[f][:, 0:S], w, xl[:, x, :], start=False, stop=False)
                        pe.wait_ge(w_lo, n + 1 if i is None else i * step + (n + 1))
                        for t in range(k):
                            last = mm(banks[f][:, 0:S], wlo[:, n % 4, t, :], xh[:, half * k + t, :], start=False,
                                      stop=(half == 1 and t == k - 1))
                        last.then_inc(piece_used, 1)

            PAIRS = (pl[0:2], pl[2:4])

            def layer(piece, turns, ready, done=0, **k):
                with pe.Fori(0, turns) as i:
                    for j in range(2):
                        pe.wait_ge(ready, i * 2 + (done + j + 1))
                        group(piece + 4 * j, PAIRS[j], i=i, step=8, **k)

            def inputs(name):
                pe.wait_ge(x_lo, 4 * (SPLITS[name] + 1))

            norm_total(NI["pre"], tmp)
            inputs("in1")
            pe.wait_ge(par_ready, 2)
            layer(PIECE0["in1"], 6, in1_ready)
            pe.wait_ge(in1_ready, 13)
            group(PIECE0["in1"] + 48, PAIRS[0])
            u = UNIT0["kraw"]
            pe.wait_ge(slot_full[u % RING], landed(u))
            pe.wait_ge(in1_ready, 14)
            for t in range(DT):
                last = mm(pl[2][0:ROPE, 0:S], plain(u, DT, ROPE)[:, t, :], mix[:, t, :], start=(t == 0), stop=(t == DT - 1))
            last.then_inc(plain_used, 1)
            norm_total(NI["q"], tmp)
            norm_total(NI["kv"], tmp[:, 6:10, :])
            pe.wait_ge(norm_out, tiles_before(NI["q"] + 1))
            pe.wait_ge(in1_ready, 16)
            for hd in range(HEADS):
                u = UNIT0["uq"] + hd
                n, at = hd // 2, hd % 2 * S
                pe.wait_ge(slot_full[u % RING], landed(u))
                if n >= 2 and hd % 2 == 0:
                    pe.wait_ge(q_ready, 2 * (n - 1))
                w = plain(u, QLT, QK)
                for t in range(QLT):
                    mm(pl[n][:, at:at + S], w[:, t, 0:NOPE], q_lat[:, t, :], start=(t == 0), stop=(t == QLT - 1))
                for t in range(QLT):
                    last = mm(pg[n % 2][0:ROPE, at:at + S], w[:, t, NOPE:QK], q_lat[:, t, :], start=(t == 0), stop=(t == QLT - 1))
                last.then_inc(plain_used, 1)
            pe.wait_ge(norm_out, tiles_before(NI["kv"] + 1))
            pe.wait_ge(q_ready, HEADS)
            for n in range(HEADS // 2):
                u = UNIT0["ukv"] + n
                pe.wait_ge(slot_full[u % RING], landed(u))
                w = plain(u, KVT, 2, NOPE + VH)
                for a in range(2):
                    for t in range(KVT):
                        mm(pl[n][:, a * S:(a + 1) * S], w[:, t, a, 0:NOPE], kv_lat[:, t, :], start=(t == 0), stop=(t == KVT - 1))
                if n == 2:
                    pe.wait_ge(kv_ready, 4)
                for tt in range(TT):
                    for t in range(KVT):
                        last = mm(pg[tt][:, n % 2 * S:(n % 2 + 1) * S], kv_lat[:, t, tt * P:(tt + 1) * P],
                                  w[:, t, :, NOPE:NOPE + VH], start=(t == 0), stop=(t == KVT - 1))
                last.then_inc(plain_used, 1)
            pe.wait_ge(kv_ready, 8)
            for n in range(4):
                mm(pl[n][0:ROPE, :], rotT[:], q_pe[0:ROPE, 2 * n:2 * n + 2, :], start=True, stop=True)
            mm(pg[0][0:ROPE, 0:S], rotT[:], k_raw[0:ROPE, :], start=True, stop=True).then_inc(rot_done, 1)
            pe.wait_ge(conv_step, CONV_K * CT)
            for t in range(CT):
                last = mm(pg[2][:, 0:S], ones[:], conv_a[:, t, :], start=(t == 0), stop=(t == CT - 1))
            last.then_inc(mean_sum, 1)
            norm_total(NI["ln"], tmp[:, 0:8, :])
            pe.wait_ge(roped, 1)

            def scores(hd):
                if hd >= 2:
                    pe.wait_ge(s_ready, hd - 1)
                for qt, at, n in ((0, 0, P), (1, P, S)):
                    q = slice(qt * P, (qt + 1) * P)
                    mm(pl[hd % 2][:, at:at + n], q_nope[:, hd, q], k_nope[:, hd, 0:n], start=True, stop=False)
                    last = mm(pl[hd % 2][:, at:at + n], q_pe[0:ROPE, hd, q], k_pe[0:ROPE, 0:n], start=False, stop=True)
                last.then_inc(s_done, 1)

            prob = tmp[:, 8:12, :].rearrange("p a b -> p (a b)")
            probT = tmp[:, 12:16, :].rearrange("p a b -> p (a b)")
            scores(0)
            for hd in range(HEADS):
                if hd + 1 < HEADS:
                    scores(hd + 1)
                if hd == 1:
                    norm_total(NI["conv"], conv_a)
                b = hd % 2 * 512
                pe.wait_ge(prob_ready, hd + 1)
                if hd >= 2:
                    pe.wait_ge(pT_ready, hd - 1)
                for n in range(3):
                    last = nc.tensor.transpose(pl[2 + hd % 2][:, n * P:(n + 1) * P], prob[:, b + n * P:b + (n + 1) * P], ident[:])
                last.then_inc(pT_done, 1)
                pe.wait_ge(pT_ready, hd + 1)
                if hd >= 2:
                    pe.wait_ge(o_ready, hd - 1)
                v = slice(hd * VH, (hd + 1) * VH)
                mm(pg[1 + hd % 2][:, 0:S], v_tok[:, 0, v], probT[:, b:b + S], start=True, stop=False, skip_group_check=True)
                mm(pg[1 + hd % 2][:, P:S], v_tok[:, 1, v], probT[:, b + S:b + S + P], start=False, stop=True,
                   skip_group_check=True).then_inc(o_done, 1)
            norm_total(NI["attn"], tmp)
            inputs("out1")
            layer(PIECE0["out1"], 4, out1_ready)
            norm_total(NI["post"], mix)
            norm_total(NI["ffn"], tmp)
            inputs("ffn")
            pairs = 0
            for c, (t0, n) in enumerate(CHUNKS):
                if c:
                    pe.wait_ge(down_ready, 2 + 8 * c)
                with pe.Fori(0, n // 2) as i:
                    pe.wait_ge(silu_ready, i + (pairs + 1))
                    group(PIECE0[f"gu{c}"], PAIRS[0], i=i, step=8)
                    pe.wait_ge(mul_ready, i + (pairs + 1))
                    group(PIECE0[f"gu{c}"] + 4, PAIRS[1], i=i, step=8)
                pairs += n // 2
                pe.wait_ge(hid_lo, pairs + 1)
                layer(PIECE0[f"down{c}"], 4, down_ready, 8 * c, xh=hhi, xl=hlo, k=n // 2)
            norm_total(NI["postf"], mix)
            norm_total(NI["n1"], tmp)
            inputs("in2")
            layer(PIECE0["in2a"], 4, in2_ready)
            for n in range(2):
                u = UNIT0["gates"] + n
                pe.wait_ge(slot_full[u % RING], landed(u))
            for hd in range(8):
                pe.wait_ge(xc_ready, hd + 1)
                if hd >= 3:
                    pe.wait_ge(gates_ready, 2 * (hd - 2))
                for n in range(2):
                    last = mm(pg[hd % 3][:, n * S:(n + 1) * S], plain(UNIT0["gates"] + n, 8, P)[:, hd, :], l_xc[:, hd, :],
                              start=True, stop=True)
                last.then_inc(gates_done, 1)
            pe.wait_ge(gates_done, 8)
            pe.sem_inc(plain_used, 2)
            layer(PIECE0["in2b"], 2, in2_ready, 8)
            u = UNIT0["pool"]
            pe.wait_ge(slot_full[u % RING], landed(u))
            pe.wait_ge(gates_ready, 16)
            w = plain(u, 4, 2, 2 * P)
            for g in range(4):
                pe.wait_ge(pool_d, 2 * (g + 1))
                if g >= 3:
                    pe.wait_ge(pool_y, 2 * (g - 2))
                for f in range(2):
                    for k in range(2):
                        last = mm(pg[g % 3][:, f * S:(f + 1) * S], w[:, g, k, f * P:(f + 1) * P], p_d[:, 2 * g + k, :],
                                  start=(k == 0), stop=(k == 1))
                last.then_inc(pool_done, 1)
            pe.wait_ge(pool_done, 4)
            pe.sem_inc(plain_used, 1)
            inputs("out2")
            layer(PIECE0["out2"], 4, out2_ready)
            pe.wait_ge(pool_y, 8)
            for n in range(4):
                u = UNIT0["keys"] + n // 2
                pe.wait_ge(slot_full[u % RING], landed(u))
                if n == 3:
                    pe.wait_ge(key_ready, 1)
                for f in range(4):
                    last = nc.tensor.transpose(pg[n % 3][:, f * P:(f + 1) * P], plain(u, PH, P)[:, n % 2 * 4 + f, :], ident[:])
                last.then_inc(key_T, 1)
            pe.wait_ge(key_T, 4)
            pe.sem_inc(plain_used, 2)
            norm_total(NI["n2"], mix)
            pe.wait_ge(key_ready, 4)
            for n in range(16):
                src, t, f4 = (res, tmp)[n // 8], n // 4 % 2, n % 4
                if n >= 3:
                    pe.wait_ge(*((tok_r, n - 2) if n - 3 < 8 else (tok_z, n - 10)))
                if n >= 8:
                    pe.wait_ge(norm_out, tiles_before(NI["n2"]) + 4 * f4 + 4)
                for f in range(4):
                    last = nc.tensor.transpose(pg[n % 3][:, f * P:(f + 1) * P], src[:, f4 * 4 + f, t * P:(t + 1) * P], ident[:])
                last.then_inc(tok_T, 1)
            inputs("wq")

            def peer_scores(n):
                pe.wait_ge(wq_ready, 2 + n + 1)
                if n >= 2:
                    pe.wait_ge(sc_ready, n - 1)
                elif n == 0:
                    pe.wait_ge(tok_z, 8)
                for m in range(4):
                    t, half = m // 2, m % 2
                    last = mm(pg[n % 2][:, m * P:(m + 1) * P], qh[:, n % 2, half, t * P:(t + 1) * P],
                              keysT[:, half * PH + n, :], start=True, stop=True)
                last.then_inc(sc_done, 1)

            for n in range(PH):
                pe.wait_ge(wq_ready, n + 1)
                group(PIECE0["wq"] + 4 * n, PAIRS[n % 2])
                if n >= 1:
                    peer_scores(n - 1)
            peer_scores(PH - 1)

        @block.scalar
        def _(act):
            activation = nc.scalar.activation

            def copy(o, i):
                return nc.scalar.activation(o, i, ACT.Copy)

            def four(bank):
                return bank[:].rearrange("p (a b) -> p a b", a=4)

            def two(bank):
                return bank[:].rearrange("p (a b) -> p a b", a=2)

            def norm_squares(n, src, sq):
                tiles = NORMS[n][1]
                for t in range(0, tiles, 4):
                    e = min(t + 4, tiles)
                    activation(sq[:, t:e, :], src[:, t:e, :], ACT.Square).then_inc(norm_sq, 1)

            def norm_root(n):
                act.wait_ge(norm_inv, n + 1)
                if n:
                    act.wait_ge(norm_out, tiles_before(n))
                activation(rstd[:], invms[:], ACT.Sqrt).then_inc(norm_rstd, 1)

            def weights_hi(unit, piece, k=KU, i=None, step=0):
                for half in range(2):
                    u = unit + half
                    act.wait_ge(slot_full[u % RING], landed(u) if i is None else i * (2 * step) + landed(u))
                    w = raw[:, u % RING, 0:k * CG].rearrange("p (k f c) -> p k f c", k=k, f=2)
                    for f in range(2):
                        n = piece + 2 * half + f
                        if n >= 4:
                            act.wait_ge(piece_used, n - 3 if i is None else i * step + (n - 3))
                        copy(whi[:, n % 4, 0:k, :], w[:, :, f, :]).then_inc(w_hi, 1)

            def input_hi(name, src, n):
                for t in range(0, DT, 4):
                    act.wait_ge(norm_out, tiles_before(n) + t + 4)
                    copy(xhi[:, t:t + 4, :], src[:, t:t + 4, :]).then_inc(x_hi, 1)

            act.wait_ge(par_T, 1)
            copy(par[:], pl[0][:, 0:NPARAM]).then_inc(par_ready, 1)
            act.wait_ge(freq_done, 1)
            copy(small[0:ROPE, 32:33], pl[1][0:ROPE, 0:1]).then_inc(par_ready, 1)
            banks = [pg[0], pg[1], pg[2], pl[2], pl[3], pg[0], pg[1], pg[2]]
            for n in range(8):
                act.wait_ge(x_T, n + 1)
                t, f4 = n // 4, n % 4
                copy(res[:, f4 * 4:f4 * 4 + 4, t * P:(t + 1) * P], four(banks[n])).then_inc(res_ready, 1)
            act.wait_ge(res_ready, 8)
            norm_squares(NI["pre"], res, tmp)
            weights_hi(UNIT0["in1"], PIECE0["in1"])
            norm_root(NI["pre"])
            input_hi("in1", mix, NI["pre"])
            act.sem_inc(in1_ready, 2)

            def in1_out(g):
                act.wait_ge(piece_used, PIECE0["in1"] + 4 * (g + 1))
                a, b = PAIRS[g % 2]
                if g < 8:
                    j = g // 2
                    if g % 2 == 0:
                        dst, fn = conv_a[:, 2 * j:2 * j + 2, :], ACT.Copy
                    else:
                        dst, fn = sig[:, j % 2], ACT.Sigmoid
                        if j >= 2:
                            act.wait_ge(u_ready, j - 1)
                else:
                    j = g - 8
                    dst, fn = (q_lat[:, 2 * j:2 * j + 2, :] if j < 3 else kv_lat[:, 2 * j - 6:2 * j - 4, :]), ACT.Copy
                activation(dst[:, 0, :], a[:, 0:S], fn)
                activation(dst[:, 1, :], b[:, 0:S], fn).then_inc(in1_ready, 1)

            PAIRS = (pl[0:2], pl[2:4])
            for g in range(1, len(IN1_COLS)):
                weights_hi(UNIT0["in1"] + 2 * g, PIECE0["in1"] + 4 * g)
                in1_out(g - 1)
            in1_out(len(IN1_COLS) - 1)
            act.wait_ge(plain_used, PLAIN0["kraw"] + 1)
            copy(k_raw[0:ROPE, :], pl[2][0:ROPE, 0:S]).then_inc(in1_ready, 1)
            act.wait_ge(in1_ready, 15)
            norm_squares(NI["q"], q_lat, tmp)
            norm_squares(NI["kv"], kv_lat, tmp[:, 6:10, :])
            norm_root(NI["q"])
            norm_root(NI["kv"])
            for n in range(HEADS // 2):
                act.wait_ge(plain_used, PLAIN0["uq"] + 2 * n + 2)
                copy(q_nope[:, 2 * n:2 * n + 2, :], two(pl[n])).then_inc(q_ready, 1)
                copy(q_pe[0:ROPE, 2 * n:2 * n + 2, :], pg[n % 2][0:ROPE, :].rearrange("p (a b) -> p a b", a=2))\
                    .then_inc(q_ready, 1)
            for n in range(HEADS // 2):
                act.wait_ge(plain_used, PLAIN0["ukv"] + n + 1)
                copy(k_nope[:, 2 * n:2 * n + 2, :], two(pl[n])).then_inc(kv_ready, 1)
                if n % 2:
                    for a in range(2):
                        copy(v_tok[:, a, n // 2 * 512:(n // 2 + 1) * 512], pg[a][:]).then_inc(kv_ready, 1)
            act.wait_ge(centred, CT)
            act.wait_ge(norm_sum, NI["kv"] + 1)
            norm_squares(NI["ln"], conv_a, tmp)
            act.wait_ge(const_ready, 7)
            act.wait_ge(trig_arg, 2)
            activation(sinT[0:ROPE, :], sinT[0:ROPE, :], ACT.Sin).then_inc(trig_ready, 1)
            activation(cosT[0:ROPE, :], cosT[0:ROPE, :], ACT.Sin, bias=halfpi[0:ROPE, :], scale=-1.0).then_inc(trig_ready, 1)
            norm_root(NI["ln"])
            act.wait_ge(norm_out, tiles_before(NI["ln"] + 1))
            for c in range(CT):
                activation(mix[:, c, :], conv_a[:, c, :], ACT.Silu, bias=col("conv_ln_b", c)).then_inc(conv_silu, 1)
            act.wait_ge(conv_silu, CT)
            norm_squares(NI["conv"], mix, conv_a)
            score = tmp[:, 0:4, :].rearrange("p a b -> p (a b)")
            prob = tmp[:, 8:12, :].rearrange("p a b -> p (a b)")
            probT = tmp[:, 12:16, :].rearrange("p a b -> p (a b)")

            def exponentials(hd):
                b = hd % 2 * 512
                act.wait_ge(s_max, hd + 1)
                if hd >= 2:
                    act.wait_ge(pT_done, hd - 1)
                m = 40 + hd % 2 * 4
                activation(prob[:, b:b + P], score[:, b:b + P], ACT.Exp, bias=small[:, m:m + 1],
                           accum_out=small[:, m + 2:m + 3]).then_inc(exp_ready, 1)
                activation(prob[:, b + P:b + 3 * P], score[:, b + P:b + 3 * P], ACT.Exp, bias=small[:, m + 1:m + 2],
                           accum_out=small[:, m + 3:m + 4]).then_inc(exp_ready, 1)

            exponentials(0)
            for hd in range(HEADS):
                if hd + 1 < HEADS:
                    exponentials(hd + 1)
                if hd == 1:
                    norm_root(NI["conv"])
                act.wait_ge(pT_done, hd + 1)
                if hd >= 2:
                    act.wait_ge(o_done, hd - 1)
                copy(probT[:, hd % 2 * 512:hd % 2 * 512 + 3 * P], pl[2 + hd % 2][:, 0:3 * P]).then_inc(pT_ready, 1)
                act.wait_ge(o_done, hd + 1)
                copy(mix[:, 8 + hd, :], pg[1 + hd % 2][:, 0:S]).then_inc(o_ready, 1)
            act.wait_ge(o_ready, HEADS)
            norm_squares(NI["attn"], mix[:, 8:16, :], tmp)
            weights_hi(UNIT0["out1"], PIECE0["out1"])
            norm_root(NI["attn"])
            act.wait_ge(norm_out, tiles_before(NI["attn"] + 1))
            for t in range(0, DT, 4):
                copy(xhi[:, t:t + 4, :], mix[:, t:t + 4, :]).then_inc(x_hi, 1)

            def layer(name, turns, ready, dst):
                u, n = UNIT0[name], PIECE0[name]
                act.sem_inc(ready, 2)

                def out(g, i=None):
                    act.wait_ge(piece_used, n + 4 * (g + 1) if i is None else i * 8 + (n + 4 * (g + 1)))
                    for f in range(2):
                        t = 2 * g + f
                        d = dst[:, t, :] if i is None else dst[:, bass.ds(i * 4 + t, 1), :].rearrange("p a b -> p (a b)")
                        last = copy(d, PAIRS[g % 2][f][:, 0:S])
                    last.then_inc(ready, 1)

                weights_hi(u + 2, n + 4)
                out(0)
                with act.Fori(1, turns) as i:
                    weights_hi(u, n, i=i, step=8)
                    out(-1, i)
                    weights_hi(u + 2, n + 4, i=i, step=8)
                    out(0, i)
                out(2 * turns - 1)

            layer("out1", 4, out1_ready, tmp)
            act.wait_ge(out1_ready, 2 + 8)
            norm_squares(NI["post"], tmp, mix)
            weights_hi(UNIT0["gu0"], PIECE0["gu0"])
            norm_root(NI["post"])
            act.wait_ge(res1_ready, 4)
            norm_squares(NI["ffn"], res, tmp)
            norm_root(NI["ffn"])
            input_hi("ffn", mix, NI["ffn"])
            act.sem_inc(silu_ready, 1)
            pairs = 0
            for c, (t0, n) in enumerate(CHUNKS):
                u, pc = UNIT0[f"gu{c}"], PIECE0[f"gu{c}"]

                def gate_out(i=None):
                    act.wait_ge(piece_used, pc + 4 if i is None else i * 8 + (pc + 4))
                    k = pairs + 1
                    act.wait_ge(mul_ready, k if i is None else i + k)
                    activation(silu[:, 0, :], pl[0][:, 0:S], ACT.Silu)
                    activation(silu[:, 1, :], pl[1][:, 0:S], ACT.Silu).then_inc(silu_ready, 1)

                def hidden_hi(at, i=None):
                    act.wait_ge(mul_ready, pairs + at + 2 if i is None else i + (pairs + at + 2))
                    d = hhi[:, 2 * at:2 * at + 2, :] if i is None else hhi[:, bass.ds(i * 2 + 2 * at, 2), :]
                    copy(d, hid[:]).then_inc(hid_hi, 1)

                weights_hi(u + 2, pc + 4)
                gate_out()
                with act.Fori(1, n // 2) as i:
                    weights_hi(u, pc, i=i, step=8)
                    hidden_hi(-1, i)
                    weights_hi(u + 2, pc + 4, i=i, step=8)
                    gate_out(i)
                ud, pd, k = UNIT0[f"down{c}"], PIECE0[f"down{c}"], n // 2
                weights_hi(ud, pd, k)
                hidden_hi(n // 2 - 1)
                weights_hi(ud + 2, pd + 4, k)
                with act.Fori(1, 4) as i:
                    weights_hi(ud, pd, k, i=i, step=8)
                    weights_hi(ud + 2, pd + 4, k, i=i, step=8)
                pairs += n // 2
                if c + 1 < len(CHUNKS):
                    weights_hi(UNIT0[f"gu{c + 1}"], PIECE0[f"gu{c + 1}"])
            act.wait_ge(down_ready, 2 + 8 * len(CHUNKS))
            norm_squares(NI["postf"], tmp, mix)
            weights_hi(UNIT0["in2a"], PIECE0["in2a"])
            norm_root(NI["postf"])
            act.wait_ge(res2_ready, 4)
            norm_squares(NI["n1"], res, tmp)
            norm_root(NI["n1"])
            input_hi("in2", mix, NI["n1"])
            act.wait_ge(lam_abs, 1)
            activation(small[:, 0:8], small[:, 0:8], ACT.Exp, scale=-1.0).then_inc(lam_exp, 1)
            act.sem_inc(in2_ready, 2)
            pc = PIECE0["in2a"]

            def in2_hi(g):
                name, j = ("in2a", g) if g < 8 else ("in2b", g - 8)
                weights_hi(UNIT0[name] + 2 * j, PIECE0[name] + 4 * j)

            def in2_out(g):
                act.wait_ge(piece_used, pc + 4 * (g + 1))
                t = slice(2 * (g % 4), 2 * (g % 4) + 2)
                dst = (l_x[:, t, LPAD:], p_u[:, t, WMAX:], l_gelu[:, t, :])[g // 4]
                fn = (ACT.Copy, ACT.Copy, ACT.Gelu_apprx_tanh)[g // 4]
                for f in range(2):
                    last = activation(dst[:, f, :], PAIRS[g % 2][f][:, 0:S], fn)
                last.then_inc(in2_ready, 1)

            for g in range(1, 9):
                in2_hi(g)
                in2_out(g - 1)
            act.wait_ge(x_lo, 4 * (SPLITS["in2"] + 1))
            for hd in range(8):
                act.wait_ge(gates_done, hd + 1)
                if hd == 0:
                    act.wait_ge(xc_ready, 8)
                activation(l_r[:, hd, :], pg[hd % 3][:, 0:S], ACT.Sigmoid, bias=col("gate_a_b_2", hd)).then_inc(gates_ready, 1)
                activation(l_i[:, hd, :], pg[hd % 3][:, S:2 * S], ACT.Sigmoid, bias=col("gate_x_b_2", hd)).then_inc(gates_ready, 1)
            in2_hi(9)
            in2_out(8)
            act.wait_ge(lam_ready, 1)
            act.wait_ge(gates_ready, 16)
            for hd in range(8):
                activation(l_m[:, hd, :], l_r[:, hd, :], ACT.Tanh, scale=small[:, 16 + hd:17 + hd]).then_inc(decay, 1)
            act.wait_ge(decay, 8)
            for hd in range(8):
                activation(l_r[:, hd, :], l_r[:, hd, :], ACT.Exp, scale=small[:, 8 + hd:9 + hd]).then_inc(decay, 1)
            in2_hi(10)
            in2_out(9)
            for hd in range(8):
                act.wait_ge(mult_arg, hd + 1)
                activation(l_m[:, hd, :], l_m[:, hd, :], ACT.Sqrt).then_inc(mult_ready, 1)
            in2_hi(11)
            in2_out(10)
            in2_out(11)
            weights_hi(UNIT0["out2"], PIECE0["out2"])
            for t in range(0, DT, 4):
                act.wait_ge(*((pool_y, t + 4) if t < 8 else (lru_y, t - 4)))
                copy(xhi[:, t:t + 4, :], mix[:, t:t + 4, :]).then_inc(x_hi, 1)
            layer("out2", 4, out2_ready, tmp)
            for n in range(4):
                act.wait_ge(key_T, n + 1)
                copy(keysT[:, 4 * n:4 * n + 4, :], four(pg[n % 3])).then_inc(key_ready, 1)
            act.wait_ge(res3_ready, 4)
            norm_squares(NI["n2"], res, mix)
            weights_hi(UNIT0["wq"], PIECE0["wq"])
            norm_root(NI["n2"])
            input_hi("wq", tmp, NI["n2"])
            for n in range(8):
                act.wait_ge(tok_T, 8 + n + 1)
                t, f4 = n // 4, n % 4
                copy(zc[:, t, f4 * 512:(f4 + 1) * 512], pg[(8 + n) % 3][:]).then_inc(tok_z, 1)
            act.sem_inc(wq_ready, 2)

            def queries(n):
                act.wait_ge(piece_used, PIECE0["wq"] + 4 * (n + 1))
                if n >= 2:
                    act.wait_ge(sc_done, n - 1)
                for half in range(2):
                    last = copy(qh[:, n % 2, half, :], PAIRS[n % 2][half][:, 0:S])
                last.then_inc(wq_ready, 1)

            def score_copy(n):
                act.wait_ge(sc_done, n + 1)
                if n >= 2:
                    act.wait_ge(sel_max, n - 1)
                copy(sc[:, n % 2], four(pg[n % 2])).then_inc(sc_ready, 1)

            def gate_exp(n):
                act.wait_ge(sel_max, n + 1)
                g = gate[:, n * HSLOTS:(n + 1) * HSLOTS]
                activation(g, g, ACT.Exp).then_inc(sel_exp, 1)

            for n in range(PH + 3):
                if 1 <= n < PH:
                    weights_hi(UNIT0["wq"] + 2 * n, PIECE0["wq"] + 4 * n)
                if 1 <= n <= PH:
                    queries(n - 1)
                if 2 <= n <= PH + 1:
                    score_copy(n - 2)
                if n >= 3:
                    gate_exp(n - 3)
            for n in range(PH):
                act.wait_ge(dot_kept, (n + 1) * HSLOTS // GR)
                d = dots[:, n * HSLOTS:(n + 1) * HSLOTS]
                activation(d, d, ACT.Gelu_apprx_tanh).then_inc(act_ready, 1)
            for t in range(TT):
                act.wait_ge(added, SLOTS)
                activation(zc[:, t, :], acc[:, t, :], ACT.Square, accum_out=small[:, 32 + t:33 + t]).then_inc(fin_sq, 1)
                act.wait_ge(fin_inv, t + 1)
                activation(small[:, 36 + t:37 + t], small[:, 34 + t:35 + t], ACT.Sqrt).then_inc(fin_rstd, 1)

        @block.vector
        def _(dve):
            V = nc.vector
            steps = [0]

            def link(ins):
                steps[0] += 1
                ins.then_inc(dve_step, 1)
                dve.wait_ge(dve_step, steps[0])

            def norm_finish(n, src, gain, dst, d):
                tiles = NORMS[n][1]
                dve.wait_ge(norm_sum, n + 1)
                link(V.tensor_scalar(meansq[:], pnorm, 1.0 / d, EPS, ALU.mult, ALU.add))
                if n:
                    dve.wait_ge(norm_rstd, n)
                V.reciprocal(invms[:], meansq[:]).then_inc(norm_inv, 1)
                dve.wait_ge(norm_rstd, n + 1)
                for t in range(tiles):
                    V.scalar_tensor_tensor(dst[:, t, :], src[:, t, :], col(gain, t), rstd[:], ALU.mult, ALU.mult)\
                        .then_inc(norm_out, 1)

            def weights_lo(unit, piece, k=KU, i=None, step=0, between=None):
                for half in range(2):
                    u = unit + half
                    w = raw[:, u % RING, 0:k * CG].rearrange("p (k f c) -> p k f c", k=k, f=2)
                    for f in range(2):
                        n = piece + 2 * half + f
                        dve.wait_ge(w_hi, n + 1 if i is None else i * step + (n + 1))
                        V.tensor_tensor(wlo[:, n % 4, 0:k, :], w[:, :, f, :], whi[:, n % 4, 0:k, :].bitcast(F32), ALU.subtract)\
                            .then_inc(w_lo, 1)
                        if between:
                            between()

            def input_lo(name, src):
                for t in range(0, DT, 4):
                    dve.wait_ge(x_hi, 4 * SPLITS[name] + t // 4 + 1)
                    V.tensor_tensor(xlo[:, t:t + 4, :], src[:, t:t + 4, :], xhi[:, t:t + 4, :].bitcast(F32), ALU.subtract)\
                        .then_inc(x_lo, 1)

            TURN = 2 * np.pi
            T1 = 6.28125
            T2 = float(np.float32(np.round((TURN - T1) * 2.0 ** 21) / 2.0 ** 21))
            T3 = float(np.float32(TURN - T1 - T2))
            MAGIC = 1.5 * 2.0 ** 23
            a_ = angle[0:ROPE, :]
            s_ = sinT[0:ROPE, :]
            c_ = cosT[0:ROPE, :]
            dve.wait_ge(pos_in, 16)
            dve.wait_ge(par_ready, 2)
            link(V.tensor_copy(c_, a_.bitcast(I32)))
            link(V.tensor_scalar(a_, c_, small[0:ROPE, 32:33], None, ALU.mult))
            link(V.tensor_scalar(s_, a_, 1.0 / TURN, None, ALU.mult))
            link(V.tensor_scalar(s_, s_, MAGIC, None, ALU.add))
            link(V.tensor_scalar(s_, s_, MAGIC, None, ALU.subtract))
            for part in (T1, T2, T3):
                link(V.scalar_tensor_tensor(a_, s_, -part, a_, ALU.mult, ALU.add))
            V.tensor_scalar(s_, a_, 3.1415925, -3.1415925, ALU.min, ALU.max).then_inc(trig_arg, 1)
            V.scalar_tensor_tensor(c_, a_, -1.0, a_, ALU.mult, ALU.max).then_inc(trig_arg, 1)
            V.memset(conv_u[:, :, 0:CPAD], 0.0)

            weights_lo(UNIT0["in1"], PIECE0["in1"])
            dve.wait_ge(x_T, 8)
            norm_finish(NI["pre"], res, "pre_mix_norm", mix, D)
            input_lo("in1", mix)

            taps = []
            n_taps = [0]

            def add_taps(n):
                for k, c in taps[n_taps[0]:n_taps[0] + n]:
                    u = conv_u[:, c, k:k + S]
                    if k == 0:
                        ins = V.tensor_scalar(conv_a[:, c, :], u, conv_tap(0, c), col("conv_b", c), ALU.mult, ALU.add)
                    else:
                        dve.wait_ge(conv_step, n_taps[0] - 1)
                        ins = V.scalar_tensor_tensor(conv_a[:, c, :], u, conv_tap(k, c), conv_a[:, c, :], ALU.mult, ALU.add)
                    ins.then_inc(conv_step, 1)
                    n_taps[0] += 1

            for g in range(1, len(IN1_COLS)):
                weights_lo(UNIT0["in1"] + 2 * g, PIECE0["in1"] + 4 * g, between=lambda: add_taps(4))
                if g % 2 == 0 and g <= 8:
                    j = g // 2 - 1
                    dve.wait_ge(in1_ready, 2 + g)
                    V.tensor_tensor(conv_u[:, 2 * j:2 * j + 2, CPAD:], conv_a[:, 2 * j:2 * j + 2, :], sig[:, j % 2], ALU.mult)\
                        .then_inc(u_ready, 1)
                    dve.wait_ge(u_ready, j + 1)
                    taps += [(k, c) for k in range(CONV_K) for c in (2 * j, 2 * j + 1)]
            norm_finish(NI["q"], q_lat, "q_norm", q_lat, QLT * P)
            norm_finish(NI["kv"], kv_lat, "kv_norm", kv_lat, KVT * P)
            add_taps(len(taps))
            dve.wait_ge(mean_sum, 1)
            link(V.tensor_scalar(mean_b[:], pg[2][:, 0:S], 1.0 / CONV_CH, None, ALU.mult))
            for c in range(CT):
                V.tensor_tensor(conv_a[:, c, :], conv_a[:, c, :], mean_b[:], ALU.subtract).then_inc(centred, 1)
            dve.wait_ge(centred, CT)
            norm_finish(NI["ln"], conv_a, "conv_ln_g", conv_a, CONV_CH)
            dve.wait_ge(rot_done, 1)
            dve.wait_ge(trig_ready, 2)
            rot = tmp[0:ROPE, 0:HEADS, :]
            for n in range(4):
                last = V.tensor_tensor(rot[:, 2 * n:2 * n + 2, :], pl[n][0:ROPE, :].rearrange("p (a b) -> p a b", a=2),
                                       s_.unsqueeze(1).broadcast_to([ROPE, 2, S]), ALU.mult)
            link(V.tensor_tensor(q_pe[0:ROPE, :, :], q_pe[0:ROPE, :, :], c_.unsqueeze(1).broadcast_to([ROPE, HEADS, S]), ALU.mult))
            link(V.tensor_tensor(q_pe[0:ROPE, :, :], q_pe[0:ROPE, :, :], rot, ALU.add))
            V.tensor_tensor(k_pe[0:ROPE, :], k_raw[0:ROPE, :], c_, ALU.mult)
            link(V.tensor_tensor(rot[:, 0, :], pg[0][0:ROPE, 0:S], s_, ALU.mult))
            V.tensor_tensor(k_pe[0:ROPE, :], k_pe[0:ROPE, :], rot[:, 0, :], ALU.add).then_inc(roped, 1)
            score = tmp[:, 0:4, :].rearrange("p a b -> p (a b)")
            prob = tmp[:, 8:12, :].rearrange("p a b -> p (a b)")
            dve.wait_ge(roped, 1)
            dve.wait_ge(const_ready, 7)

            def head_scores(hd):
                b = hd % 2 * 512
                m = 40 + hd % 2 * 4
                dve.wait_ge(s_done, hd + 1)
                if hd >= 2:
                    dve.wait_ge(exp_ready, 2 * (hd - 1))
                V.scalar_tensor_tensor(score[:, b:b + 3 * P], pl[hd % 2][:, 0:3 * P], SCALE,
                                       mask[:].rearrange("p a b -> p (a b)"), ALU.mult, ALU.add).then_inc(s_ready, 1)
                dve.wait_ge(s_ready, hd + 1)
                V.tensor_reduce(small[:, 48:49], score[:, b:b + P], AX.X, ALU.max)
                link(V.tensor_reduce(small[:, 49:50], score[:, b + P:b + 3 * P], AX.X, ALU.max))
                V.tensor_scalar(small[:, m:m + 2], small[:, 48:50], -1.0, None, ALU.mult).then_inc(s_max, 1)

            head_scores(0)
            for hd in range(HEADS):
                if hd + 1 < HEADS:
                    dve.wait_ge(s_max, hd + 1)
                    head_scores(hd + 1)
                if hd == 1:
                    norm_finish(NI["conv"], mix, "conv_out_norm", mix, CONV_CH)
                b = hd % 2 * 512
                m = 42 + hd % 2 * 4
                r = 52 + hd % 2 * 2
                dve.wait_ge(exp_ready, 2 * hd + 2)
                link(V.reciprocal(small[:, r:r + 2], small[:, m:m + 2]))
                link(V.tensor_scalar(prob[:, b:b + P], prob[:, b:b + P], small[:, r:r + 1], None, ALU.mult))
                V.tensor_scalar(prob[:, b + P:b + 3 * P], prob[:, b + P:b + 3 * P], small[:, r + 1:r + 2], None, ALU.mult)\
                    .then_inc(prob_ready, 1)
            weights_lo(UNIT0["out1"], PIECE0["out1"])
            norm_finish(NI["attn"], mix[:, 8:16, :], "attn_out_norm", mix[:, 8:16, :], HEADS * VH)
            input_lo("out1", mix)

            def layer(name, turns):
                u, n = UNIT0[name], PIECE0[name]
                weights_lo(u + 2, n + 4)
                with dve.Fori(1, turns) as i:
                    weights_lo(u, n, i=i, step=8)
                    weights_lo(u + 2, n + 4, i=i, step=8)

            def add_residual(ready):
                for t in range(0, DT, 4):
                    V.tensor_tensor(res[:, t:t + 4, :], res[:, t:t + 4, :], tmp[:, t:t + 4, :], ALU.add).then_inc(ready, 1)

            layer("out1", 4)
            weights_lo(UNIT0["gu0"], PIECE0["gu0"])
            norm_finish(NI["post"], tmp, "post_mix_norm", tmp, D)
            dve.wait_ge(norm_out, tiles_before(NI["post"] + 1))
            add_residual(res1_ready)
            dve.wait_ge(res1_ready, 4)
            norm_finish(NI["ffn"], res, "pre_ffn_norm", mix, D)
            input_lo("ffn", mix)
            dve.sem_inc(mul_ready, 1)
            dve.sem_inc(down_ready, 2)
            pairs = 0
            for c, (t0, n) in enumerate(CHUNKS):
                u, pc = UNIT0[f"gu{c}"], PIECE0[f"gu{c}"]

                def multiply(at, i=None):
                    k = pairs + at
                    dve.wait_ge(piece_used, pc + 8 * at + 8 if i is None else i * 8 + (pc + 8 * at + 8))
                    dve.wait_ge(silu_ready, k + 2 if i is None else i + (k + 2))
                    dve.wait_ge(hid_lo, k + 1 if i is None else i + (k + 1))
                    for f in range(2):
                        last = V.tensor_tensor(hid[:, f, :], silu[:, f, :], pl[2 + f][:, 0:S], ALU.mult)
                    last.then_inc(mul_ready, 1)

                def hidden_lo(at, i=None):
                    k = pairs + at
                    dve.wait_ge(hid_hi, k + 1 if i is None else i + (k + 1))
                    if i is None:
                        d, s = hlo[:, 2 * at:2 * at + 2, :], hhi[:, 2 * at:2 * at + 2, :]
                    else:
                        d, s = hlo[:, bass.ds(i * 2 + 2 * at, 2), :], hhi[:, bass.ds(i * 2 + 2 * at, 2), :]
                    V.tensor_tensor(d, hid[:], s.bitcast(F32), ALU.subtract).then_inc(hid_lo, 1)

                if c == 0:
                    dve.sem_inc(hid_lo, 1)
                weights_lo(u + 2, pc + 4)
                with dve.Fori(1, n // 2) as i:
                    weights_lo(u, pc, i=i, step=8)
                    multiply(-1, i)
                    weights_lo(u + 2, pc + 4, i=i, step=8)
                    hidden_lo(-1, i)
                ud, pd, k = UNIT0[f"down{c}"], PIECE0[f"down{c}"], n // 2
                weights_lo(ud, pd, k)
                multiply(n // 2 - 1)
                hidden_lo(n // 2 - 1)

                def down_out(g, i=None):
                    dve.wait_ge(piece_used, pd + 4 * (g + 1) if i is None else i * 8 + (pd + 4 * (g + 1)))
                    for f in range(2):
                        t = 2 * g + f
                        d = tmp[:, t, :] if i is None else tmp[:, bass.ds(i * 4 + t, 1), :].rearrange("p a b -> p (a b)")
                        bank = pl[2 * (g % 2) + f][:, 0:S]
                        last = V.tensor_copy(d, bank) if c == 0 else V.tensor_tensor(d, d, bank, ALU.add)
                    last.then_inc(down_ready, 1)

                weights_lo(ud + 2, pd + 4, k)
                down_out(0)
                with dve.Fori(1, 4) as i:
                    weights_lo(ud, pd, k, i=i, step=8)
                    down_out(-1, i)
                    weights_lo(ud + 2, pd + 4, k, i=i, step=8)
                    down_out(0, i)
                pairs += n // 2
                if c + 1 < len(CHUNKS):
                    weights_lo(UNIT0[f"gu{c + 1}"], PIECE0[f"gu{c + 1}"])
                down_out(7)
            weights_lo(UNIT0["in2a"], PIECE0["in2a"])
            norm_finish(NI["postf"], tmp, "post_ffn_norm", tmp, D)
            dve.wait_ge(norm_out, tiles_before(NI["postf"] + 1))
            add_residual(res2_ready)
            lam = col("lru_lambda_2", 0, 8)
            V.scalar_tensor_tensor(small[:, 0:8], lam, -1.0, lam, ALU.mult, ALU.max).then_inc(lam_abs, 1)
            dve.wait_ge(res2_ready, 4)
            norm_finish(NI["n1"], res, "norm1_g_2", mix, D)
            input_lo("in2", mix)
            V.memset(p_u[:, :, 0:WMAX], 0.0)
            V.memset(l_x[:, :, 0:LPAD], 0.0)
            for g, w in enumerate(POOL_WINDOWS):
                for n in range(w):
                    V.memset(edge[:, g, n:n + 1], 1.0 / (n + 1))
            link(V.memset(win[:], 0.0))
            link(V.memset(win2[:], 0.0))

            def in2_lo(g):
                name, j = ("in2a", g) if g < 8 else ("in2b", g - 8)
                weights_lo(UNIT0[name] + 2 * j, PIECE0[name] + 4 * j)

            in2_lo(1)
            dve.wait_ge(lam_exp, 1)
            y, s8, s2, ser = small[:, 0:8], small[:, 24:32], small[:, 16:24], small[:, 8:16]
            link(V.tensor_scalar(s2, y, 2.0, None, ALU.add))
            link(V.reciprocal(s2, s2))
            link(V.tensor_tensor(s8, y, s2, ALU.mult))
            link(V.tensor_tensor(s2, s8, s8, ALU.mult))
            TERMS = 9
            link(V.tensor_scalar(ser, s2, 1.0 / (2 * TERMS + 1), 1.0 / (2 * TERMS - 1), ALU.mult, ALU.add))
            for n in range(TERMS - 2, -1, -1):
                link(V.tensor_tensor(ser, ser, s2, ALU.mult))
                link(V.tensor_scalar(ser, ser, 1.0 / (2 * n + 1), None, ALU.add))
            link(V.tensor_tensor(ser, ser, s8, ALU.mult))
            link(V.tensor_scalar(s2, lam, 0.0, None, ALU.min))
            link(V.scalar_tensor_tensor(ser, ser, -2.0, s2, ALU.mult, ALU.add))
            link(V.tensor_scalar(ser, ser, LRU_C, None, ALU.mult))
            V.tensor_scalar(s2, ser, -1.0, None, ALU.mult).then_inc(lam_ready, 1)

            def short_conv(c):
                dve.wait_ge(in2_ready, 2 + c // 2 + 1)
                for k in range(LCONV):
                    src, wk = l_x[:, c, k:k + S], col("conv_w_2", k * 8 + c)
                    if k == 0:
                        ins = V.tensor_scalar(l_xc[:, c, :], src, wk, col("conv_b_2", c), ALU.mult, ALU.add)
                    else:
                        ins = V.scalar_tensor_tensor(l_xc[:, c, :], src, wk, l_xc[:, c, :], ALU.mult, ALU.add)
                    if k < LCONV - 1:
                        link(ins)
                    else:
                        ins.then_inc(xc_ready, 1)

            def pool_group(g):
                w = POOL_WINDOWS[g]
                dve.wait_ge(in2_ready, 2 + 4 + g + 1)
                for f in (2 * g, 2 * g + 1):
                    cur, other, step = p_u[:, f, :], win[:], 1
                    while step < w:
                        link(V.tensor_tensor(other[:, step:], cur[:, step:], cur[:, 0:WMAX + S - step], ALU.add))
                        cur, other, step = other, (win if step % 4 == 2 or step == 2 else win2)[:], 2 * step
                    V.scalar_tensor_tensor(p_d[:, f, w:], cur[:, WMAX + w:], 1.0 / w, p_u[:, f, WMAX + w:], ALU.mult, ALU.subtract)
                    link(V.tensor_tensor(p_d[:, f, 0:w], cur[:, WMAX:WMAX + w], edge[:, g, 0:w], ALU.mult))
                    link(V.tensor_tensor(p_d[:, f, 0:w], p_d[:, f, 0:w], p_u[:, f, WMAX:WMAX + w], ALU.subtract))
                    dve.sem_inc(pool_d, 1)

            for g in range(2, 9):
                in2_lo(g)
                if g <= 5:
                    short_conv(2 * g - 4)
                    short_conv(2 * g - 3)
                else:
                    pool_group(g - 6)
            dve.wait_ge(gates_ready, 16)
            V.tensor_tensor(l_i[:], l_i[:], l_xc[:], ALU.mult)
            in2_lo(9)
            pool_group(3)
            for hd in range(8):
                dve.wait_ge(decay, 8 + hd + 1)
                link(V.tensor_tensor(l_xc[:, hd, :], l_r[:, hd, :], l_r[:, hd, :], ALU.mult))
                V.scalar_tensor_tensor(l_m[:, hd, :], l_xc[:, hd, :], 1.0, l_m[:, hd, :], ALU.add, ALU.mult).then_inc(mult_arg, 1)
            in2_lo(10)
            for hd in range(8):
                dve.wait_ge(mult_ready, hd + 1)
                link(V.tensor_tensor(l_i[:, hd, :], l_i[:, hd, :], l_m[:, hd, :], ALU.mult))
                link(V.tensor_tensor_scan(l_xc[:, hd, :], l_r[:, hd, :], l_i[:, hd, :], 0.0, ALU.mult, ALU.add))
            in2_lo(11)
            weights_lo(UNIT0["out2"], PIECE0["out2"])
            for g in range(4):
                dve.wait_ge(pool_done, g + 1)
                for f in range(2):
                    t = 2 * g + f
                    V.tensor_scalar(mix[:, t, :], pg[g % 3][:, f * S:(f + 1) * S], col("pool_b_2", t), col("pool_scale_2", t),
                                    ALU.add, ALU.mult).then_inc(pool_y, 1)
            for hd in range(8):
                if hd % 2 == 0:
                    dve.wait_ge(in2_ready, 2 + 8 + hd // 2 + 1)
                V.tensor_tensor(mix[:, 8 + hd, :], l_xc[:, hd, :], l_gelu[:, hd, :], ALU.mult).then_inc(lru_y, 1)
            input_lo("out2", mix)
            layer("out2", 4)
            dve.wait_ge(out2_ready, 2 + 8)
            add_residual(res3_ready)
            weights_lo(UNIT0["wq"], PIECE0["wq"])
            norm_finish(NI["n2"], res, "norm2_g_2", tmp, D)
            for n in range(8):
                dve.wait_ge(tok_T, n + 1)
                t, f4 = n // 4, n % 4
                V.tensor_copy(acc[:, t, f4 * 512:(f4 + 1) * 512], pg[n % 3][:]).then_inc(tok_r, 1)
            input_lo("wq", tmp)

            def wide(ap, axis, shape):
                return ap.unsqueeze(axis).broadcast_to(shape)

            def best(sets):
                for s, rest, v, ix in sets:
                    last = V.max(v[:, 0:8], s)
                link(last)
                for s, rest, v, ix in sets:
                    V.max_index(ix[:, 0:8], v[:, 0:8], s)
                    last = V.match_replace(rest, v[:, 0:8], s, NEG)
                link(last)
                for s, rest, v, ix in sets:
                    last = V.max(v[:, 8:16], rest)
                link(last)
                for s, rest, v, ix in sets:
                    last = V.max_index(ix[:, 8:16], v[:, 8:16], rest)
                link(last)

            def choose(n):
                dve.wait_ge(sc_ready, n + 1)
                best([(sc[:, n % 2, m, :], work[:, m, :], top_v[:, m, :], top_i[:, m, :]) for m in range(4)])
                for t in range(TT):
                    last = V.tensor_tensor(cand[:, t, :].rearrange("p (a b) -> p a b", a=TOPK),
                                           wide(top_v[:, 2 * t, :], 2, [P, TOPK, TOPK]),
                                           wide(top_v[:, 2 * t + 1, :], 1, [P, TOPK, TOPK]), ALU.add)
                link(last)
                best([(cand[:, t, :], cand2[:, t, :], ctop[:, t, :], cpos[:, t, :]) for t in range(TT)])
                g3 = gate[:, n * HSLOTS:(n + 1) * HSLOTS].rearrange("p (t k) -> p t k", t=TT)
                V.tensor_tensor(g3, ctop[:], ctop[:, :, 0:1].broadcast_to([P, TT, TOPK]), ALU.subtract).then_inc(sel_max, 1)
                ci = cpos[:].bitcast(I32)
                V.tensor_scalar(cposi[:, 0], ci, 4, None, ALU.logical_shift_right)
                link(V.tensor_scalar(cposi[:, 1], ci, 15, None, ALU.bitwise_and))
                V.tensor_copy(cposf[:], cposi[:])
                link(V.tensor_copy(top_f[:], top_i[:]))
                full = [P, TT, TOPK, TOPK]
                j16 = iota16[:].unsqueeze(1).unsqueeze(1).broadcast_to(full)
                picks = [c_[:].rearrange("p t (k j) -> p t k j", k=TOPK) for c_ in (cand, cand2)]
                for half in range(2):
                    last = V.tensor_tensor(picks[half], wide(cposf[:, half], 3, full), j16, ALU.is_equal)
                link(last)
                keys = top_f[:].rearrange("p (t h) j -> p h t j", t=TT)
                for half in range(2):
                    last = V.tensor_tensor(picks[half], picks[half], wide(keys[:, half], 2, full), ALU.mult)
                link(last)
                for half in range(2):
                    last = V.tensor_reduce(cposf[:, half], picks[half], AX.X, ALU.add)
                link(last)
                e = expert[:, n * HSLOTS:(n + 1) * HSLOTS].rearrange("p (t k) -> p t k", t=TT)
                V.scalar_tensor_tensor(e, cposf[:, 0], float(NKEY), cposf[:, 1], ALU.mult, ALU.add).then_inc(sel_ready, 1)
                dve.wait_ge(sel_ready, n + 1)

            def products(n):
                for t in range(TT):
                    turns = TOPK // GR
                    first = (n * TT + t) * turns
                    with dve.Fori(0, turns) as i:
                        for j in range(GR):
                            dve.wait_ge(row_full[j], i * 16 + 16 * (first + 1))
                            V.tensor_tensor_reduce(row[j][:], row[j][:], zc[:, t, :], 1.0, 0.0, ALU.mult, ALU.add,
                                                   dot_r[:, j:j + 1]).then_inc(dot_done, 1)
                            dve.wait_ge(dot_done, i * GR + (first * GR + j + 1))
                            dve.sem_inc(row_used, 1)
                        V.tensor_copy(dots[:, bass.ds(i * GR + first * GR, GR)], dot_r[:]).then_inc(dot_kept, 1)
                        dve.wait_ge(dot_kept, i + (first + 1))

            def query_lo(n):
                weights_lo(UNIT0["wq"] + 2 * n, PIECE0["wq"] + 4 * n)

            query_lo(1)
            query_lo(2)
            choose(0)
            query_lo(3)
            choose(1)
            dve.wait_ge(tok_z, 8)
            dve.wait_ge(tok_r, 8)
            dve.wait_ge(x_lo, 4 * (SPLITS["wq"] + 1))
            dve.sem_inc(row_used, GR)
            for n in range(PH):
                products(n)
                if n + 4 < PH:
                    query_lo(n + 4)
                if n + 2 < PH:
                    choose(n + 2)
                if n == PH - 2:
                    dve.wait_ge(sel_exp, PH)
                    g3 = gate[:].rearrange("p (s k) -> p s k", k=TOPK)
                    link(V.tensor_reduce(small[:, 0:PH * TT], g3, AX.X, ALU.add))
                    link(V.reciprocal(small[:, 0:PH * TT], small[:, 0:PH * TT]))
                    link(V.tensor_tensor(g3, g3, wide(small[:, 0:PH * TT], 2, [P, PH * TT, TOPK]), ALU.mult))
            dve.wait_ge(act_ready, PH)
            link(V.tensor_tensor(dots[:], gate[:], dots[:], ALU.mult))
            with dve.Fori(0, PH) as n:
                V.tensor_copy(w_r[:], dots[:, bass.ds(n * HSLOTS, HSLOTS)]).then_inc(w_copied, 1)
                dve.wait_ge(w_copied, n + 1)
                for j in range(HSLOTS):
                    t = j // TOPK
                    dve.wait_ge(row_full[j % GR], n * (16 * HSLOTS // GR) + 16 * (SLOTS // GR + j // GR + 1))
                    V.scalar_tensor_tensor(acc[:, t, :], row[j % GR][:], w_r[:, j:j + 1], acc[:, t, :], ALU.mult, ALU.add)\
                        .then_inc(added, 1)
                    dve.wait_ge(added, n * HSLOTS + (j + 1))
                    dve.sem_inc(row_used, 1)
            dve.wait_ge(gain_in, 16)
            for t in range(TT):
                dve.wait_ge(fin_sq, t + 1)
                link(V.tensor_scalar(small[:, 34 + t:35 + t], small[:, 32 + t:33 + t], 1.0 / D, EPS, ALU.mult, ALU.add))
                link(V.reciprocal(small[:, 34 + t:35 + t], small[:, 34 + t:35 + t]))
                dve.sem_inc(fin_inv, 1)
                dve.wait_ge(fin_rstd, t + 1)
                V.scalar_tensor_tensor(zc[:, t, :], acc[:, t, :], small[:, 36 + t:37 + t], gain_f[:], ALU.mult, ALU.mult)\
                    .then_inc(fin_out, 1)


_INS = ['x', 'positions', 'pre_mix_norm', 'w_in', 'q_norm', 'w_uq', 'kv_norm', 'w_ukv', 'conv_w', 'conv_b', 'conv_ln_g',
        'conv_ln_b', 'conv_out_norm', 'attn_out_norm', 'w_out', 'post_mix_norm', 'pre_ffn_norm', 'w_gate', 'w_up',
        'w_down', 'post_ffn_norm', 'norm1_g_2', 'w_in_2', 'pool_w_2', 'pool_b_2', 'pool_scale_2', 'conv_w_2',
        'conv_b_2', 'gate_a_w_2', 'gate_a_b_2', 'gate_x_w_2', 'gate_x_b_2', 'lru_lambda_2', 'w_out_2', 'norm2_g_2',
        'peer_wq_2', 'peer_keys1_2', 'peer_keys2_2', 'peer_u_2', 'peer_v_2', 'norm_f_g_2']


def kernel(**inputs):
    import concourse.bacc as bacc
    from concourse.bass_utils import run_bass_kernel_spmd

    nc = bacc.Bacc("TRN2", target_bir_lowering=False, num_devices=1)
    arrays, args = {}, {}
    for name in _INS:
        a = np.ascontiguousarray(inputs[name])
        arrays[f"in_{name}"] = a
        args[name] = nc.dram_tensor(f"in_{name}", a.shape, mybir.dt.from_np(a.dtype), kind="ExternalInput").ap()
    out = nc.dram_tensor("out", (1, S, D), F32, kind="ExternalOutput").ap()
    build(nc, args, out)
    r = run_bass_kernel_spmd(nc, [arrays], core_ids=[0])
    return r.results[0]["out"]
```

```python
from contextlib import ExitStack

import numpy as np

import concourse.bass as bass
from concourse import mybir

ALU = mybir.AluOpType
ACT = mybir.ActivationFunctionType
AX = mybir.AxisListType
F32 = mybir.dt.float32
F32R = mybir.dt.float32r
I32 = mybir.dt.int32
U32 = mybir.dt.uint32

P = 128
S = 256
TT = S // P
D = 2048
DT = D // P
CONV_CH = 1024
CT = CONV_CH // P
CONV_K = 31
HEADS = 8
NOPE, ROPE, VH = 128, 64, 128
QK = NOPE + ROPE
QLT = 768 // P
KVT = 512 // P
DFF = 5632
FT = DFF // P
EPS = 1e-6
ROPE_THETA = 10000.0
SCALE = float(QK) ** -0.5
MASKED = -1e30
POOL_WINDOWS = (2, 4, 8, 16)
WMAX = max(POOL_WINDOWS)
LRU_C = 8.0
LCONV = 4
PH = 8
NKEY = 128
TOPK = 16
HSLOTS = TT * TOPK
SLOTS = PH * HSLOTS
GR = 4
NEG = -3.0e38

RING = 4
UNIT = 2048
KU = 8
CG = 256
HCH = 16
CHUNKS = [(c, min(HCH, FT - c)) for c in range(0, FT, HCH)]


def unit_plan():
    seq = [("in1", 26, True), ("kraw", 1, False), ("uq", HEADS, False), ("ukv", HEADS // 2, False), ("out1", 16, True)]
    for j, (_, n) in enumerate(CHUNKS):
        seq += [(f"gu{j}", 2 * n, True), (f"down{j}", 16, True)]
    seq += [("in2a", 16, True), ("gates", 2, False), ("in2b", 6, True), ("pool", 1, False), ("in2c", 2, True),
            ("out2", 16, True), ("keys", 2, False), ("wq", 16, True)]
    unit, piece, plain, free, loads = {}, {}, {}, [], []
    n_piece = n_plain = 0
    for name, n, split in seq:
        unit[name], piece[name], plain[name] = len(free), n_piece, n_plain
        for _ in range(n):
            loads.append({"kraw": 2, "uq": 4}.get(name, 1) + (loads[-RING] if len(loads) >= RING else 0))
            if split:
                n_piece += 2
                free.append((True, n_piece))
            else:
                n_plain += 1
                free.append((False, n_plain))
    return unit, piece, plain, free, loads


UNIT0, PIECE0, PLAIN0, FREE, LOADS = unit_plan()

NORMS = (("q", QLT), ("kv", KVT), ("ln", CT), ("conv", CT), ("attn", 8), ("post", 16),
         ("ffn", 16), ("postf", 16), ("n1", 16), ("n2", 16))
NI = {name: n for n, (name, _) in enumerate(NORMS)}
WIDE = ("post", "ffn", "postf", "n1", "n2")
LATE = ("ffn", "n1", "n2")
POOL_LO = {"post": "gu0", "postf": "in2a"}

SPLITS = {"in1": 0, "out1": 1, "ffn": 2, "in2": 3, "out2": 4}

PARAM_TILES = (
    (("pre_mix_norm", 16), ("q_norm", 6), ("kv_norm", 4), ("conv_b", 8), ("conv_ln_g", 8), ("conv_ln_b", 8),
     ("conv_out_norm", 8), ("attn_out_norm", 8), ("post_mix_norm", 16), ("pre_ffn_norm", 16), ("post_ffn_norm", 16)),
    (("norm1_g_2", 16), ("pool_b_2", 8), ("pool_scale_2", 8), ("conv_b_2", 8), ("gate_a_b_2", 8), ("gate_x_b_2", 8),
     ("lru_lambda_2", 8), ("norm2_g_2", 16), ("conv_w_2", LCONV * 8)),
    (("conv_w_lo", 16 * CT),),
    (("conv_w_hi", (CONV_K - 16) * CT),),
)


def param_columns():
    at, col = {}, 0
    for tile in PARAM_TILES:
        for name, rows in tile:
            at[name] = col
            col += rows
    return at, col


def build(nc, A, out):
    PC, NPARAM = param_columns()
    n_param_dmas = sum(len(t) for t in PARAM_TILES)

    with ExitStack() as ctx:
        def sem(name):
            return ctx.enter_context(nc.semaphore(name))

        base = -(-nc.sbuf_base // 64) * 64
        place = {}
        at = base
        for name, words in (("raw", RING * UNIT), ("whi", 4 * 1024), ("wlo", 4 * 1024), ("xhi", DT * S), ("xlo", DT * S),
                            ("res", DT * S), ("tmp", DT * S), ("mix", DT * S), ("arena", 10240), ("rest", 4736)):
            place[name] = at
            at += words * 4

        def sb(name, region, start, shape, dt=F32):
            return nc.alloc_sbuf_tensor_at(name, shape, dt, offset=place[region] + 4 * start)

        raw = sb("raw", "raw", 0, [P, RING, UNIT])
        whi = sb("whi", "whi", 0, [P, 4, KU, P], F32R)
        wlo = sb("wlo", "wlo", 0, [P, 4, KU, P], F32R)
        xhi = sb("xhi", "xhi", 0, [P, DT, S], F32R)
        xlo = sb("xlo", "xlo", 0, [P, DT, S], F32R)
        res = sb("res", "res", 0, [P, DT, S])
        tmp = sb("tmp", "tmp", 0, [P, DT, S])
        mix = sb("mix", "mix", 0, [P, DT, S])

        r_at = [0]

        def keep(name, shape, dt=F32):
            n = int(np.prod(shape[1:]))
            t = sb(name, "rest", r_at[0], shape, dt)
            r_at[0] += -(-n // 8) * 8
            assert r_at[0] <= 4736
            return t

        par = keep("par", [P, NPARAM])
        ident = keep("ident", [P, P])
        ones = keep("ones", [P, P])
        rotT = keep("rotT", [P, P])
        freq_row = keep("freq_row", [1, P])
        mask = keep("mask", [P, 3, P])
        meansq = keep("meansq", [P, S])
        invms = keep("invms", [P, S])
        rstd = keep("rstd", [P, S])
        small = keep("small", [P, 64])
        x_stat = keep("x_stat", [P, 6])
        halfpi = keep("halfpi", [P, 1])
        iota16 = keep("iota16", [P, TOPK])
        idx_r = keep("idx_r", [P, GR], I32)
        w_r = keep("w_r", [P, HSLOTS])
        gate = keep("gate", [P, SLOTS])
        expert = keep("expert", [P, SLOTS], I32)
        dots = keep("dots", [P, SLOTS])
        sq_sum = keep("sq_sum", [P, 2, S])
        sq_r = keep("sq_r", [P, 2, 2, S])

        CPAD = CONV_K - 1
        prow = sb("prow", "tmp", 0, [P, len(PARAM_TILES), P])
        xin = sb("xin", "mix", 0, [P, TT, D])
        xn = sb("xn", "arena", 0, [P, TT, D])
        xsq = sb("xsq", "xlo", 0, [P, TT, D])
        conv_a = sb("conv_a", "arena", 0, [P, CT, S])
        conv_u = sb("conv_u", "arena", 2048, [P, CT, CPAD + S])
        q_lat = sb("q_lat", "arena", 4336, [P, QLT, S])
        kv_lat = sb("kv_lat", "arena", 5872, [P, KVT, S])
        k_raw = sb("k_raw", "arena", 6896, [P, S])
        sig = sb("sig", "arena", 7152, [P, 2, 2, S])
        mean_b = sb("mean_b", "arena", 8176, [P, S])
        angle = sb("angle", "arena", 8432, [P, S])
        cosT = sb("cosT", "arena", 8688, [P, S])
        sinT = sb("sinT", "arena", 8944, [P, S])
        k_pe = sb("k_pe", "arena", 9200, [P, S])
        q_nope = sb("q_nope", "xhi", 0, [P, HEADS, S])
        q_pe = sb("q_pe", "xhi", 2048, [P, HEADS // 2, S])
        k_nope = sb("k_nope", "xlo", 0, [P, HEADS, S])
        v_tok = sb("v_tok", "xlo", 2048, [P, TT, HEADS * VH])
        hhi = sb("hhi", "arena", 0, [P, HCH, S], F32R)
        hlo = sb("hlo", "arena", HCH * S, [P, HCH, S], F32R)
        silu = sb("silu", "arena", 2 * HCH * S, [P, 2, S])
        hid = sb("hid", "arena", 2 * HCH * S + 2 * S, [P, 2, S])
        LPAD = LCONV - 1
        p_u = sb("p_u", "arena", 0, [P, 8, WMAX + S])
        l_x = sb("l_x", "arena", 2176, [P, 8, LPAD + S])
        l_i = sb("l_i", "arena", 2176, [P, 8, S])
        l_gelu = sb("l_gelu", "arena", 4248, [P, 8, S])
        l_xc = sb("l_xc", "arena", 6296, [P, 8, S])
        win = sb("win", "arena", 8344, [P, WMAX + S])
        win2 = sb("win2", "arena", 8616, [P, WMAX + S])
        edge = sb("edge", "arena", 8888, [P, len(POOL_WINDOWS), WMAX])
        p_d = tmp[:, 0:8, :]
        l_m = tmp[:, 8:16, :]
        l_r = mix[:, 8:16, :]
        zc = sb("zc", "arena", 0, [P, TT, D])
        acc = sb("acc", "arena", TT * D, [P, TT, D])
        keysT = sb("keysT", "arena", 2 * TT * D, [P, 2 * PH, NKEY])
        zhi = sb("zhi", "tmp", 0, [P, DT, S], F32R)
        zlo = sb("zlo", "mix", 0, [P, DT, S], F32R)
        row = [sb(f"row{n}", ("res", "xlo")[n // 2], n % 2 * D, [P, D]) for n in range(GR)]
        qh = sb("qh", "xhi", 0, [P, 2, 2, S])
        sc = sb("sc", "xhi", 1024, [P, 2, 4, NKEY])
        work = sb("work", "xhi", 2048, [P, 4, NKEY])
        cand = sb("cand", "xhi", 2560, [P, TT, TOPK * TOPK])
        cand2 = sb("cand2", "xhi", 3072, [P, TT, TOPK * TOPK])
        top_v = sb("top_v", "xhi", 3584, [P, 4, TOPK])
        top_i = sb("top_i", "xhi", 3648, [P, 4, TOPK], U32)
        top_f = sb("top_f", "xhi", 3712, [P, 4, TOPK])
        ctop = sb("ctop", "xhi", 3776, [P, TT, TOPK])
        cpos = sb("cpos", "xhi", 3808, [P, TT, TOPK], U32)
        cposi = sb("cposi", "xhi", 3840, [P, 2, TT, TOPK], I32)
        cposf = sb("cposf", "xhi", 3904, [P, 2, TT, TOPK])
        gain_f = sb("gain_f", "raw", 0, [P, D])

        pl = [ctx.enter_context(nc.psum_tensor(f"pl{n}", [P, 512], F32)) for n in range(4)]
        pg = [ctx.enter_context(nc.psum_tensor(f"pg{n}", [P, 512], F32)) for n in range(4)]
        pnorm = pg[3][:, 0:S]

        x_in = [sem(f"x_in{t}") for t in range(TT)]
        par_in = sem("par_in")
        pos_in = sem("pos_in")
        slot_full = [sem(f"slot_full{n}") for n in range(RING)]
        w_hi = sem("w_hi")
        w_lo = sem("w_lo")
        piece_used = sem("piece_used")
        plain_used = sem("plain_used")
        x_hi = sem("x_hi")
        x_lo = sem("x_lo")
        const_ready = sem("const_ready")
        par_T = sem("par_T")
        par_ready = sem("par_ready")
        x_T = sem("x_T")
        x_sq = sem("x_sq")
        x_inv = sem("x_inv")
        x_rstd = sem("x_rstd")
        x_norm = sem("x_norm")
        xn_T = sem("xn_T")
        xn_ready = sem("xn_ready")
        res_ready = sem("res_ready")
        norm_sq = sem("norm_sq")
        sq_added = sem("sq_added")
        norm_sum = sem("norm_sum")
        norm_inv = sem("norm_inv")
        norm_rstd = sem("norm_rstd")
        norm_out = sem("norm_out")
        in1_ready = sem("in1_ready")
        u_ready = sem("u_ready")
        conv_step = sem("conv_step")
        mean_sum = sem("mean_sum")
        centred = sem("centred")
        conv_silu = sem("conv_silu")
        q_ready = sem("q_ready")
        kv_ready = sem("kv_ready")
        freq_done = sem("freq_done")
        trig_arg = sem("trig_arg")
        trig_ready = sem("trig_ready")
        rot_done = sem("rot_done")
        rot_read = sem("rot_read")
        roped = sem("roped")
        s_done = sem("s_done")
        s_ready = sem("s_ready")
        s_max = sem("s_max")
        exp_ready = sem("exp_ready")
        prob_ready = sem("prob_ready")
        pT_done = sem("pT_done")
        pT_ready = sem("pT_ready")
        o_done = sem("o_done")
        o_ready = sem("o_ready")
        gate_scaled = sem("gate_scaled")
        silu_scaled = sem("silu_scaled")
        gelu_ready = sem("gelu_ready")
        z_scaled = sem("z_scaled")
        z_hi = sem("z_hi")
        z_lo = sem("z_lo")
        zgain_in = sem("zgain_in")
        rstd_T = sem("rstd_T")
        rstd_tok = sem("rstd_tok")
        out1_ready = sem("out1_ready")
        res1_ready = sem("res1_ready")
        silu_ready = sem("silu_ready")
        mul_ready = sem("mul_ready")
        hid_hi = sem("hid_hi")
        hid_lo = sem("hid_lo")
        down_ready = sem("down_ready")
        res2_ready = sem("res2_ready")
        in2_ready = sem("in2_ready")
        pool_d = sem("pool_d")
        pool_done = sem("pool_done")
        pool_y = sem("pool_y")
        xc_ready = sem("xc_ready")
        gates_done = sem("gates_done")
        gates_ready = sem("gates_ready")
        lam_abs = sem("lam_abs")
        lam_exp = sem("lam_exp")
        lam_ready = sem("lam_ready")
        decay = sem("decay")
        mult_arg = sem("mult_arg")
        mult_ready = sem("mult_ready")
        lru_y = sem("lru_y")
        out2_ready = sem("out2_ready")
        tok_T = sem("tok_T")
        tok_r = sem("tok_r")
        key_T = sem("key_T")
        key_ready = sem("key_ready")
        wq_ready = sem("wq_ready")
        sc_done = sem("sc_done")
        sc_ready = sem("sc_ready")
        sel_max = sem("sel_max")
        sel_exp = sem("sel_exp")
        sel_ready = sem("sel_ready")
        gain_in = sem("gain_in")
        idx_copied = sem("idx_copied")
        pool_step = sem("pool_step")
        row_full = [sem(f"row_full{n}") for n in range(GR)]
        row_used = sem("row_used")
        act_ready = sem("act_ready")
        w_copied = sem("w_copied")
        fin_sq = sem("fin_sq")
        fin_inv = sem("fin_inv")
        fin_rstd = sem("fin_rstd")
        fin_out = sem("fin_out")
        stored = sem("stored")
        dve_step = sem("dve_step")
        const_step = sem("const_step")

        def landed(unit):
            return 16 * LOADS[unit]

        def sq_count(n, t4):
            return sum(8 if m in WIDE else -(-k // 4) for m, k in NORMS[:n]) + t4 + 1

        def tiles_before(n):
            return sum(k for m, k in NORMS[:n] if m not in LATE)

        def two_tiles(a, g, i=None):
            return a[:, 2 * g:2 * g + 2, :] if i is None else a[:, bass.ds(i * 4 + 2 * g, 2), :]

        def col(name, t=0, n=1):
            return par[:, PC[name] + t:PC[name] + t + n]

        def conv_tap(k, c):
            return col("conv_w_lo", k * CT + c) if k < 16 else col("conv_w_hi", (k - 16) * CT + c)

        def plain(unit, *shape):
            n = int(np.prod(shape))
            v = raw[:, unit % RING, 0:n]
            if len(shape) == 2:
                return v.rearrange("p (a b) -> p a b", a=shape[0])
            return v.rearrange("p (a b c) -> p a b c", a=shape[0], b=shape[1])

        IN1_COLS = [c for j in range(4) for c in (j * CG, CONV_CH + j * CG)] + [2 * CONV_CH + j * CG for j in range(5)]
        IN2_COLS = [CONV_CH + j * CG for j in range(4)] + [j * CG for j in range(4)] + [2 * CONV_CH + j * CG for j in range(4)]

        def in2_unit(g):
            name, first = ("in2a", 0) if g < 8 else ("in2b", 8) if g < 11 else ("in2c", 11)
            return UNIT0[name] + 2 * (g - first)

        block = ctx.enter_context(nc.Block())

        @block.sync
        def _(sp):
            for t in range(TT):
                sp.dma_start(xin[:, t, :], A["x"][0, t * P:(t + 1) * P, :]).then_inc(x_in[t], 16)

            def slot_free(unit, i=None, step=0):
                if unit < RING:
                    return
                split, count = FREE[unit - RING]
                s = w_lo if split else plain_used
                if i is None:
                    sp.wait_ge(s, count)
                else:
                    sp.wait_ge(s, i * step + (count - step))

            def split_unit(unit, src, k=KU):
                dst = raw[:, unit % RING, 0:k * CG].rearrange("p (k c) -> p k c", k=k)
                sp.dma_start(dst, src).then_inc(slot_full[unit % RING], 16)

            def block_of(w, k0, k, cols, c=CG):
                return w[0, k0 * P:(k0 + k) * P, cols:cols + c].rearrange("(k p) c -> p k c", p=P)

            def group(unit, w, cols):
                for half in range(2):
                    slot_free(unit + half)
                    split_unit(unit + half, block_of(w, half * KU, KU, cols))

            def groups(unit, n, parts, halves_first=False):
                for m in range(4):
                    j, half = (m % 2, m // 2) if halves_first else (m // 2, m % 2)
                    w, cols, step, k0, k = parts[j]
                    slot_free(unit + m)
                    split_unit(unit + m, block_of(w, k0 + half * k, k, cols), k)
                with sp.Fori(1, n) as i:
                    for j, (w, cols, step, k0, k) in enumerate(parts):
                        for half in range(2):
                            u = unit + 2 * j + half
                            slot_free(u + RING, i, 8)
                            src = w[0, (k0 + half * k) * P:(k0 + (half + 1) * k) * P, bass.ds(i * step + cols, CG)]
                            split_unit(u, src.rearrange("(k p) c -> p k c", p=P), k)

            for t, tile in enumerate(PARAM_TILES):
                r = 0
                for name, rows in tile:
                    if name == "conv_w_lo":
                        src = A["conv_w"][0, 0:16, :]
                    elif name == "conv_w_hi":
                        src = A["conv_w"][0, 16:CONV_K, :]
                    else:
                        src = A[name][0]
                        if len(src.shape) == 1:
                            src = src.rearrange("(a n) -> a n", a=1)
                    flat = src.rearrange("a n -> (a n)").rearrange("(r c) -> r c", c=P)
                    sp.dma_start(prow[r:r + rows, t, :], flat).then_inc(par_in, 16)
                    r += rows
            for n in range(2):
                group(UNIT0["in1"] + 2 * n, A["w_in"], IN1_COLS[n])
            sp.dma_start(angle[:].bitcast(I32), A["positions"].broadcast_to([P, S])).then_inc(pos_in, 16)
            for n in range(2, len(IN1_COLS)):
                group(UNIT0["in1"] + 2 * n, A["w_in"], IN1_COLS[n])
            u = UNIT0["kraw"]
            slot_free(u)
            c = 2 * CONV_CH + (QLT + KVT) * P
            for a in range(2):
                sp.dma_start(plain(u, DT, 2, ROPE)[:, :, a, :], block_of(A["w_in"], 0, DT, c, ROPE))\
                    .then_inc(slot_full[u % RING], 16)
            for m in range(HEADS):
                u, n, half = UNIT0["uq"] + m, m // 2, m % 2
                slot_free(u)
                w = plain(u, QLT // 2, 2 * QK)
                for a in range(2):
                    for at, c, m in ((a * NOPE, 0, NOPE), (2 * NOPE + a * ROPE, NOPE, ROPE)):
                        src = block_of(A["w_uq"], half * QLT // 2, QLT // 2, (2 * n + a) * QK + c, m)
                        sp.dma_start(w[:, :, at:at + m], src).then_inc(slot_full[u % RING], 16)
            for n in range(HEADS // 2):
                u = UNIT0["ukv"] + n
                c = 2 * (NOPE + VH)
                slot_free(u)
                sp.dma_start(plain(u, KVT, c), block_of(A["w_ukv"], 0, KVT, n * c, c)).then_inc(slot_full[u % RING], 16)
            groups(UNIT0["out1"], 4, [(A["w_out"], j * CG, 2 * CG, 0, KU) for j in range(2)], True)
            for j, (t0, n) in enumerate(CHUNKS):
                groups(UNIT0[f"gu{j}"], n // 2, [(A[w], t0 * P, CG, 0, KU) for w in ("w_gate", "w_up")], j == 0)
                groups(UNIT0[f"down{j}"], 4, [(A["w_down"], a * CG, 2 * CG, t0, n // 2) for a in range(2)])
            for m in range(4):
                u = UNIT0["in2a"] + m
                slot_free(u)
                split_unit(u, block_of(A["w_in_2"], m // 2 * KU, KU, IN2_COLS[m % 2]))
            for n in range(2, 8):
                group(UNIT0["in2a"] + 2 * n, A["w_in_2"], IN2_COLS[n])
            for n, w in enumerate(("gate_a_w_2", "gate_x_w_2")):
                u = UNIT0["gates"] + n
                slot_free(u)
                sp.dma_start(plain(u, 8, P), A[w][0].rearrange("h p c -> p h c")).then_inc(slot_full[u % RING], 16)
            for n in range(8, 12):
                if n == 11:
                    u = UNIT0["pool"]
                    slot_free(u)
                    sp.dma_start(plain(u, 4, 2, 2 * P), A["pool_w_2"][0].rearrange("g (k p) c -> p g k c", p=P))\
                        .then_inc(slot_full[u % RING], 16)
                group(in2_unit(n), A["w_in_2"], IN2_COLS[n])
            groups(UNIT0["out2"], 4, [(A["w_out_2"], j * CG, 2 * CG, 0, KU) for j in range(2)])
            for n, w in enumerate(("peer_keys1_2", "peer_keys2_2")):
                u = UNIT0["keys"] + n
                slot_free(u)
                sp.dma_start(plain(u, PH, P), A[w][0].rearrange("h p c -> p h c")).then_inc(slot_full[u % RING], 16)
            sp.wait_ge(lru_y, 8)
            for t in range(TT):
                sp.dma_start(zc[:, t, :], A["norm2_g_2"].broadcast_to([P, D])).then_inc(zgain_in, 16)
            groups(UNIT0["wq"], 4, [(A["peer_wq_2"], j * CG, 2 * CG, 0, KU) for j in range(2)])
            sp.wait_ge(w_lo, FREE[-1][1])
            sp.dma_start(gain_f[:], A["norm_f_g_2"].rearrange("(a n) -> a n", a=1).broadcast_to([P, D])).then_inc(gain_in, 16)
            for t in range(TT):
                for half in range(2):
                    c = slice(half * D // 2, (half + 1) * D // 2)
                    sp.wait_ge(fin_out, 2 * t + half + 1)
                    sp.dma_start(out[0, t * P:(t + 1) * P, c], zc[:, t, c]).then_inc(stored, 16)
            sp.wait_ge(stored, 2 * 16 * TT)

        @block.gpsimd
        def _(pool):
            steps = [0]

            def link(ins):
                steps[0] += 1
                ins.then_inc(const_step, 1)
                pool.wait_ge(const_step, steps[0])

            nc.gpsimd.memset(ones[:], 1.0).then_inc(const_ready, 1)
            link(nc.gpsimd.memset(ident[:], 0.0))
            nc.gpsimd.affine_select(out=ident[:], in_=ident[:], compare_op=ALU.not_equal, fill=1.0, base=0,
                                    pattern=[[-1, P]], channel_multiplier=1).then_inc(const_ready, 1)
            HR = ROPE // 2
            link(nc.gpsimd.memset(rotT[:], 0.0))
            for c in range(0, P, HR):
                second = c // HR % 2
                cols = rotT[:, c:c + HR]
                last = nc.gpsimd.affine_select(out=cols, in_=cols, compare_op=ALU.not_equal, fill=1.0 if second else -1.0,
                                               base=HR - c if second else -HR - c, pattern=[[-1, HR]], channel_multiplier=1)
            last.then_inc(const_ready, 1)
            for i in range(HR):
                f = float(np.float32(ROPE_THETA) ** np.float32(-2.0 * i / ROPE))
                last = nc.gpsimd.memset(freq_row[0:1, :].rearrange("p (a b) -> p a b", b=HR)[:, :, i:i + 1], f)
            last.then_inc(const_ready, 1)
            link(nc.gpsimd.memset(mask[:], 0.0))
            link(nc.gpsimd.affine_select(out=mask[:, 0, :], in_=mask[:, 0, :], compare_op=ALU.is_ge, fill=MASKED,
                                         base=0, pattern=[[-1, P]], channel_multiplier=1))
            nc.gpsimd.affine_select(out=mask[:, 2, :], in_=mask[:, 2, :], compare_op=ALU.is_ge, fill=MASKED,
                                    base=0, pattern=[[-1, P]], channel_multiplier=1).then_inc(const_ready, 1)
            nc.gpsimd.memset(halfpi[:], float(np.pi / 2)).then_inc(const_ready, 1)
            for k in range(TOPK):
                last = nc.gpsimd.memset(iota16[:, k:k + 1], float(k))
            last.then_inc(const_ready, 1)

            for m, name in enumerate(WIDE):
                sq = {"post": mix, "ffn": tmp, "postf": mix, "n1": tmp}.get(name)
                n = sq_count(NI[name], -1)
                if m:
                    pool.wait_ge(norm_sum, NI[WIDE[m - 1]] + 1)
                pool.wait_ge(norm_sq, n + 2)
                a, b = (sq_r[:, 0], sq_r[:, 1]) if sq is None else (sq[:, 0:2, :], sq[:, 2:4, :])
                nc.gpsimd.tensor_tensor(sq_sum[:], a, b, ALU.add).then_inc(sq_added, 1)
                pool.wait_ge(sq_added, 7 * m + 1)
                with pool.Fori(1, 4) as i:
                    for j in range(2):
                        pool.wait_ge(norm_sq, i * 2 + (n + j + 1))
                        pool.sem_inc(pool_step, 1)
                        a = sq_r[:, j] if sq is None else two_tiles(sq, j, i)
                        nc.gpsimd.tensor_tensor(sq_sum[:], sq_sum[:], a, ALU.add).then_inc(sq_added, 1)
                        pool.wait_ge(sq_added, i * 2 + (7 * m + j))
                        pool.sem_inc(pool_step, 1)
                if name in POOL_LO:
                    u, n = UNIT0[POOL_LO[name]], PIECE0[POOL_LO[name]]
                    for q in range(4):
                        w = raw[:, (u + q // 2) % RING, 0:KU * CG].rearrange("p (k f c) -> p k f c", k=KU, f=2)
                        pool.wait_ge(w_hi, n + q + 1)
                        nc.gpsimd.tensor_tensor(wlo[:, (n + q) % 4], w[:, :, q % 2, :], whi[:, (n + q) % 4].bitcast(F32),
                                                ALU.subtract).then_inc(w_lo, 1)

            for n, table in enumerate(("peer_u_2", "peer_v_2")):
                with pool.Fori(0, PH) as hd:
                    for j in range(HSLOTS):
                        done = n * SLOTS + j
                        if n == 0 and j % TOPK == 0:
                            pool.wait_ge(sel_ready, hd * TT + (j // TOPK + 1))
                            pool.sem_inc(pool_step, 1)
                        pool.wait_ge(row_used, hd * HSLOTS + (done + 1))
                        pool.sem_inc(pool_step, 1)
                        nc.gpsimd.tensor_copy(idx_r[:, j % GR:j % GR + 1], expert[:, bass.ds(hd * HSLOTS + j, 1)])\
                            .then_inc(idx_copied, 1)
                        pool.wait_ge(idx_copied, hd * HSLOTS + (done + 1))
                        pool.sem_inc(pool_step, 1)
                        nc.gpsimd.indirect_dma_start(row[j % GR][:], None, A[table][0],
                                                     bass.IndirectOffsetOnAxis(ap=idx_r[:, j % GR:j % GR + 1], axis=0))\
                            .then_inc(row_full[j % GR], 16)

        @block.tensor
        def _(pe):
            mm = nc.tensor.matmul
            pe.wait_ge(const_ready, 2)
            def x_tiles(src, t, f4, bank):
                for f in range(4):
                    c = (f4 * 4 + f) * P
                    last = nc.tensor.transpose(bank[:, f * P:(f + 1) * P], src[:, t, c:c + P], ident[:])
                return last

            for n in range(8):
                t, f4 = n // 4, n % 4
                pe.wait_ge(x_in[t], 16)
                if n >= 3:
                    pe.wait_ge(res_ready, n - 2)
                x_tiles(xin, t, f4, pg[n % 3]).then_inc(x_T, 1)
            pe.wait_ge(par_in, 16 * n_param_dmas)
            for t, tile in enumerate(PARAM_TILES):
                rows = sum(r for _, r in tile)
                c = PC[tile[0][0]]
                last = nc.tensor.transpose(pl[0][:, c:c + rows], prow[0:rows, t, :], ident[0:rows, 0:rows])
            last.then_inc(par_T, 1)
            for n in range(8):
                t, f4 = n // 4, n % 4
                pe.wait_ge(x_norm, t + 1)
                if n >= 3:
                    pe.wait_ge(xn_ready, n - 2)
                x_tiles(xn, t, f4, pl[1 + n % 3]).then_inc(xn_T, 1)

            def norm_total(n, sq):
                tiles = NORMS[n][1]
                if n:
                    pe.wait_ge(norm_inv, n)
                for t in range(tiles):
                    if t % 4 == 0:
                        pe.wait_ge(norm_sq, sq_count(n, t // 4))
                    last = mm(pnorm, ones[:], sq[:, t, :], start=(t == 0), stop=(t == tiles - 1))
                last.then_inc(norm_sum, 1)

            def wide_total(name):
                n = NI[name]
                pe.wait_ge(norm_inv, n)
                pe.wait_ge(sq_added, 7 * (WIDE.index(name) + 1))
                mm(pnorm, ones[:], sq_sum[:, 0, :], start=True, stop=False)
                mm(pnorm, ones[:], sq_sum[:, 1, :], start=False, stop=True).then_inc(norm_sum, 1)

            def half_group(first, half, banks, xh=xhi, xl=xlo, k=KU, i=None, step=0, arriving=None):
                for f in range(2):
                    n = first + f
                    pe.wait_ge(w_hi, n + 1 if i is None else i * step + (n + 1))
                    for t in range(k):
                        w, x = whi[:, n % 4, t, :], half * k + t
                        if arriving and f == 0 and t % 4 == 0:
                            pe.wait_ge(x_lo, 4 * SPLITS[arriving] + x // 4 + 1)
                        mm(banks[f][:, 0:S], w, xh[:, x, :], start=(half == 0 and t == 0), stop=False)
                        mm(banks[f][:, 0:S], w, xl[:, x, :], start=False, stop=False)
                    pe.wait_ge(w_lo, n + 1 if i is None else i * step + (n + 1))
                    for t in range(k):
                        last = mm(banks[f][:, 0:S], wlo[:, n % 4, t, :], xh[:, half * k + t, :], start=False,
                                  stop=(half == 1 and t == k - 1))
                    last.then_inc(piece_used, 1)

            def group(piece, banks, rest=None, **k):
                half_group(piece, 0, banks, **k)
                if rest:
                    pe.wait_ge(*rest)
                half_group(piece + 2, 1, banks, **k)

            PAIRS = (pl[0:2], pl[2:4])

            def two_groups(piece, arriving, norm):
                half_group(piece, 0, PAIRS[0], arriving=arriving)
                half_group(piece + 2, 0, PAIRS[1])
                norm()
                half_group(piece + 4, 1, PAIRS[0], arriving=arriving)
                half_group(piece + 6, 1, PAIRS[1])

            def layer(piece, turns, ready, done=0, first=0, **k):
                with pe.Fori(first, turns) as i:
                    for j in range(2):
                        pe.wait_ge(ready, i * 2 + (done + j + 1))
                        group(piece + 4 * j, PAIRS[j], i=i, step=8, **k)

            pe.wait_ge(par_ready, 1)
            pe.wait_ge(xn_ready, 8)
            for j in range(2):
                pe.wait_ge(in1_ready, j + 1)
                group(PIECE0["in1"] + 4 * j, PAIRS[j], arriving="in1")
            pe.wait_ge(const_ready, 4)
            mm(pg[0][:, 0:1], freq_row[0:1, :], ones[0:1, 0:1], start=True, stop=True).then_inc(freq_done, 1)
            layer(PIECE0["in1"], 6, in1_ready, first=1)
            pe.wait_ge(in1_ready, 13)
            group(PIECE0["in1"] + 48, PAIRS[0])
            u = UNIT0["kraw"]
            pe.wait_ge(slot_full[u % RING], landed(u))
            pe.wait_ge(in1_ready, 14)
            for t in range(DT):
                last = mm(pl[2][:, 0:S], plain(u, DT, 2 * ROPE)[:, t, :], mix[:, t, :], start=(t == 0), stop=(t == DT - 1))
            last.then_inc(plain_used, 1)
            norm_total(NI["q"], tmp)
            norm_total(NI["kv"], tmp[:, 6:10, :])
            pe.wait_ge(norm_out, tiles_before(NI["q"] + 1))
            pe.wait_ge(in1_ready, 16)
            for n in range(HEADS // 2):
                if n >= 2:
                    pe.wait_ge(q_ready, 2 * (n - 1))
                for half in range(2):
                    u = UNIT0["uq"] + 2 * n + half
                    pe.wait_ge(slot_full[u % RING], landed(u))
                    w = plain(u, QLT // 2, 2 * QK)
                    for t in range(QLT // 2):
                        k = half * QLT // 2 + t
                        for a in range(2):
                            mm(pl[2 * (n % 2) + a][:, 0:S], w[:, t, a * NOPE:(a + 1) * NOPE], q_lat[:, k, :],
                               start=(k == 0), stop=(k == QLT - 1))
                        last = mm(pg[n % 2][:, 0:S], w[:, t, 2 * NOPE:], q_lat[:, k, :], start=(k == 0), stop=(k == QLT - 1))
                    last.then_inc(plain_used, 1)
            pe.wait_ge(q_ready, HEADS)
            for n in range(2):
                mm(pl[n][:], rotT[:], q_pe[:, 2 * n:2 * n + 2, :], start=True, stop=True)
            mm(pg[0][:, 0:S], rotT[:], k_raw[:], start=True, stop=True).then_inc(rot_done, 1)
            pe.wait_ge(conv_step, CONV_K * CT)
            for t in range(CT):
                last = mm(pg[2][:, 0:S], ones[:], conv_a[:, t, :], start=(t == 0), stop=(t == CT - 1))
            last.then_inc(mean_sum, 1)
            pe.wait_ge(norm_out, tiles_before(NI["kv"] + 1))
            pe.wait_ge(rot_read, 1)
            for n in range(HEADS // 2):
                u = UNIT0["ukv"] + n
                pe.wait_ge(slot_full[u % RING], landed(u))
                w = plain(u, KVT, 2, NOPE + VH)
                for a in range(2):
                    for t in range(KVT):
                        mm(pl[n][:, a * S:(a + 1) * S], w[:, t, a, 0:NOPE], kv_lat[:, t, :], start=(t == 0), stop=(t == KVT - 1))
                if n == 2:
                    pe.wait_ge(kv_ready, 4)
                for tt in range(TT):
                    for t in range(KVT):
                        last = mm(pg[tt][:, n % 2 * S:(n % 2 + 1) * S], kv_lat[:, t, tt * P:(tt + 1) * P],
                                  w[:, t, :, NOPE:NOPE + VH], start=(t == 0), stop=(t == KVT - 1))
                last.then_inc(plain_used, 1)
                if n == 1:
                    norm_total(NI["ln"], tmp[:, 0:8, :])
            pe.wait_ge(roped, 1)
            pe.wait_ge(kv_ready, 8)

            def scores(hd):
                if hd >= 2:
                    pe.wait_ge(s_ready, hd - 1)
                for qt, at, n in ((0, 0, P), (1, P, S)):
                    q = slice(qt * P, (qt + 1) * P)
                    mm(pl[hd % 2][:, at:at + n], q_nope[:, hd, q], k_nope[:, hd, 0:n], start=True, stop=False)
                    r = slice(hd % 2 * ROPE, (hd % 2 + 1) * ROPE)
                    last = mm(pl[hd % 2][:, at:at + n], q_pe[r, hd // 2, q], k_pe[r, 0:n], start=False, stop=True)
                last.then_inc(s_done, 1)

            prob = tmp[:, 8:12, :].rearrange("p a b -> p (a b)")
            probT = tmp[:, 12:16, :].rearrange("p a b -> p (a b)")
            scores(0)
            scores(1)
            for hd in range(HEADS):
                b = hd % 2 * 512
                pe.wait_ge(prob_ready, hd + 1)
                if hd >= 2:
                    pe.wait_ge(pT_ready, hd - 1)
                for n in range(3):
                    last = nc.tensor.transpose(pl[2 + hd % 2][:, n * P:(n + 1) * P], prob[:, b + n * P:b + (n + 1) * P], ident[:])
                last.then_inc(pT_done, 1)
                if hd + 2 < HEADS:
                    scores(hd + 2)
                pe.wait_ge(pT_ready, hd + 1)
                if hd >= 2:
                    pe.wait_ge(o_ready, hd - 1)
                v = slice(hd * VH, (hd + 1) * VH)
                mm(pg[1 + hd % 2][:, 0:S], v_tok[:, 0, v], probT[:, b:b + S], start=True, stop=False, skip_group_check=True)
                mm(pg[1 + hd % 2][:, P:S], v_tok[:, 1, v], probT[:, b + S:b + S + P], start=False, stop=True,
                   skip_group_check=True).then_inc(o_done, 1)
                if hd == 1:
                    norm_total(NI["conv"], conv_a)
            half_group(PIECE0["out1"], 0, PAIRS[0], arriving="out1")
            norm_total(NI["attn"], tmp)
            half_group(PIECE0["out1"] + 2, 0, PAIRS[1])
            half_group(PIECE0["out1"] + 4, 1, PAIRS[0], arriving="out1")
            half_group(PIECE0["out1"] + 6, 1, PAIRS[1])
            layer(PIECE0["out1"], 4, out1_ready, first=1)
            wide_total("post")
            pairs = 0
            for c, (t0, n) in enumerate(CHUNKS):
                def gates_ups(i):
                    k = pairs + 1
                    pe.wait_ge(gate_scaled, i + k)
                    if c:
                        pe.wait_ge(down_ready, 1 + 8 * c)
                    group(PIECE0[f"gu{c}"], PAIRS[0], i=i, step=8)
                    pe.wait_ge(mul_ready, i + k)
                    if c:
                        pe.wait_ge(down_ready, 2 + 8 * c)
                    group(PIECE0[f"gu{c}"] + 4, PAIRS[1], i=i, step=8)

                if c == 0:
                    pe.wait_ge(gate_scaled, 1)
                    pe.wait_ge(mul_ready, 1)
                    two_groups(PIECE0["gu0"], "ffn", lambda: wide_total("ffn"))
                with pe.Fori(c == 0, n // 2) as i:
                    gates_ups(i)
                pairs += n // 2
                pe.wait_ge(gate_scaled, pairs + 1)
                pe.wait_ge(hid_lo, pairs - n // 4 + 1)
                layer(PIECE0[f"down{c}"], 4, down_ready, 8 * c, xh=hhi, xl=hlo, k=n // 2, rest=(hid_lo, pairs + 1))
            wide_total("postf")
            pe.wait_ge(in2_ready, 2)
            two_groups(PIECE0["in2a"], "in2", lambda: wide_total("n1"))
            layer(PIECE0["in2a"], 4, in2_ready, first=1)
            for n in range(2):
                u = UNIT0["gates"] + n
                pe.wait_ge(slot_full[u % RING], landed(u))
            for hd in range(8):
                pe.wait_ge(xc_ready, hd + 1)
                if hd >= 3:
                    pe.wait_ge(gates_ready, 2 * (hd - 2))
                for n in range(2):
                    last = mm(pg[hd % 3][:, n * S:(n + 1) * S], plain(UNIT0["gates"] + n, 8, P)[:, hd, :], l_xc[:, hd, :],
                              start=True, stop=True)
                last.then_inc(gates_done, 1)
            pe.wait_ge(gates_done, 8)
            pe.sem_inc(plain_used, 2)
            layer(PIECE0["in2b"], 1, in2_ready, 8)
            pe.wait_ge(in2_ready, 11)
            group(PIECE0["in2b"] + 8, PAIRS[0])
            u = UNIT0["pool"]
            pe.wait_ge(slot_full[u % RING], landed(u))
            pe.wait_ge(gates_ready, 16)
            w = plain(u, 4, 2, 2 * P)
            for g in range(4):
                pe.wait_ge(pool_d, 2 * (g + 1))
                if g >= 3:
                    pe.wait_ge(pool_y, 2 * (g - 2))
                for f in range(2):
                    for k in range(2):
                        last = mm(pg[g % 3][:, f * S:(f + 1) * S], w[:, g, k, f * P:(f + 1) * P], p_d[:, 2 * g + k, :],
                                  start=(k == 0), stop=(k == 1))
                last.then_inc(pool_done, 1)
            pe.wait_ge(pool_done, 4)
            pe.sem_inc(plain_used, 1)
            pe.wait_ge(in2_ready, 12)
            group(PIECE0["in2b"] + 12, PAIRS[1])
            for j in range(2):
                pe.wait_ge(out2_ready, j + 1)
                group(PIECE0["out2"] + 4 * j, PAIRS[j], arriving="out2")
            layer(PIECE0["out2"], 4, out2_ready, first=1)
            pe.wait_ge(pool_y, 8)
            for n in range(4):
                u = UNIT0["keys"] + n // 2
                pe.wait_ge(slot_full[u % RING], landed(u))
                if n == 3:
                    pe.wait_ge(key_ready, 1)
                for f in range(4):
                    last = nc.tensor.transpose(pg[n % 3][:, f * P:(f + 1) * P], plain(u, PH, P)[:, n % 2 * 4 + f, :], ident[:])
                last.then_inc(key_T, 1)
            pe.wait_ge(key_T, 4)
            pe.sem_inc(plain_used, 2)
            wide_total("n2")
            pe.wait_ge(z_lo, 8)

            def peer_scores(j, i=None):
                pe.wait_ge(wq_ready, j + 3 if i is None else i * 2 + (j + 3))
                if i is not None:
                    pe.wait_ge(sc_ready, i * 2 + (j - 1))
                for m in range(4):
                    t, half = m // 2, m % 2
                    n = half * PH + j
                    keys = keysT[:, n, :] if i is None else keysT[:, bass.ds(i * 2 + n, 1), :].rearrange("p a b -> p (a b)")
                    last = mm(pg[j][:, m * P:(m + 1) * P], qh[:, j, half, t * P:(t + 1) * P], keys, start=True, stop=True)
                last.then_inc(sc_done, 1)

            pe.wait_ge(wq_ready, 1)
            group(PIECE0["wq"], PAIRS[0], xh=zhi, xl=zlo)
            pe.wait_ge(key_ready, 4)
            peer_scores(0)
            for t in range(TT):
                last = nc.tensor.transpose(pl[2][:, t * P:(t + 1) * P], rstd[:, t * P:(t + 1) * P], ident[:])
            last.then_inc(rstd_T, 1)
            for m in range(8):
                t, f4 = m // 4, m % 4
                if m >= 2:
                    pe.wait_ge(tok_r, m - 1)
                for f in range(4):
                    last = nc.tensor.transpose(pg[1 + m % 2][:, f * P:(f + 1) * P],
                                               res[:, f4 * 4 + f, t * P:(t + 1) * P], ident[:])
                last.then_inc(tok_T, 1)
            pe.wait_ge(rstd_tok, 1)
            pe.wait_ge(wq_ready, 2)
            group(PIECE0["wq"] + 4, PAIRS[1], xh=zhi, xl=zlo)
            pe.wait_ge(tok_r, 8)
            peer_scores(1)
            with pe.Fori(1, PH // 2) as i:
                for j in range(2):
                    pe.wait_ge(wq_ready, i * 2 + (j + 1))
                    group(PIECE0["wq"] + 4 * j, PAIRS[j], xh=zhi, xl=zlo, i=i, step=8)
                    peer_scores(j, i)

        @block.scalar
        def _(act):
            activation = nc.scalar.activation

            def copy(o, i):
                return nc.scalar.activation(o, i, ACT.Copy)

            def four(bank):
                return bank[:].rearrange("p (a b) -> p a b", a=4)

            def two(bank):
                return bank[:].rearrange("p (a b) -> p a b", a=2)

            def norm_squares(n, src, sq):
                tiles = NORMS[n][1]
                for t in range(0, tiles, 4):
                    e = min(t + 4, tiles)
                    activation(sq[:, t:e, :], src[:, t:e, :], ACT.Square).then_inc(norm_sq, 1)

            def norm_root(n):
                act.wait_ge(norm_inv, n + 1)
                if n:
                    act.wait_ge(norm_out, tiles_before(n))
                activation(rstd[:], invms[:], ACT.Sqrt).then_inc(norm_rstd, 1)

            def weights_hi(unit, piece, k=KU, i=None, step=0, halves=(0, 1)):
                for half in halves:
                    u = unit + half
                    act.wait_ge(slot_full[u % RING], landed(u) if i is None else i * (2 * step) + landed(u))
                    w = raw[:, u % RING, 0:k * CG].rearrange("p (k f c) -> p k f c", k=k, f=2)
                    for f in range(2):
                        n = piece + 2 * half + f
                        if n >= 4:
                            act.wait_ge(piece_used, n - 3 if i is None else i * step + (n - 3))
                        copy(whi[:, n % 4, 0:k, :], w[:, :, f, :]).then_inc(w_hi, 1)

            def input_hi(ready, gain):
                for t4 in range(0, DT, 4):
                    act.wait_ge(ready, t4 // 4 + 1)
                    for t in range(t4, t4 + 4):
                        last = activation(xhi[:, t, :], res[:, t, :], ACT.Copy, scale=col(gain, t))
                    last.then_inc(x_hi, 1)
                    for t in (t4, t4 + 2):
                        activation(tmp[:, t:t + 2, :], res[:, t:t + 2, :], ACT.Square).then_inc(norm_sq, 1)

            for t in range(TT):
                act.wait_ge(x_in[t], 16)
                activation(xsq[:, t, :], xin[:, t, :], ACT.Square, accum_out=x_stat[:, t:t + 1]).then_inc(x_sq, 1)
                for f4 in range(4):
                    n = 4 * t + f4
                    act.wait_ge(x_T, n + 1)
                    copy(res[:, f4 * 4:f4 * 4 + 4, t * P:(t + 1) * P], four(pg[n % 3])).then_inc(res_ready, 1)
                    if f4 == 1:
                        act.wait_ge(x_inv, t + 1)
                        activation(x_stat[:, 4 + t:5 + t], x_stat[:, 2 + t:3 + t], ACT.Sqrt).then_inc(x_rstd, 1)
            act.wait_ge(par_T, 1)
            copy(par[:], pl[0][:, 0:NPARAM]).then_inc(par_ready, 1)
            weights_hi(UNIT0["in1"], PIECE0["in1"], halves=(0,))
            for t in range(0, DT, 4):
                act.wait_ge(xn_ready, 4 + t // 4 + 1)
                copy(xhi[:, t:t + 4, :], mix[:, t:t + 4, :]).then_inc(x_hi, 1)
            weights_hi(UNIT0["in1"], PIECE0["in1"], halves=(1,))

            def in1_out(g):
                act.wait_ge(piece_used, PIECE0["in1"] + 4 * (g + 1))
                a, b = PAIRS[g % 2]
                if g < 8:
                    j = g // 2
                    if g % 2 == 0:
                        dst, fn = conv_a[:, 2 * j:2 * j + 2, :], ACT.Copy
                    else:
                        dst, fn = sig[:, j % 2], ACT.Sigmoid
                        if j >= 2:
                            act.wait_ge(u_ready, j - 1)
                else:
                    j = g - 8
                    dst, fn = (q_lat[:, 2 * j:2 * j + 2, :] if j < 3 else kv_lat[:, 2 * j - 6:2 * j - 4, :]), ACT.Copy
                activation(dst[:, 0, :], a[:, 0:S], fn)
                activation(dst[:, 1, :], b[:, 0:S], fn).then_inc(in1_ready, 1)

            PAIRS = (pl[0:2], pl[2:4])
            for g in range(1, len(IN1_COLS)):
                weights_hi(UNIT0["in1"] + 2 * g, PIECE0["in1"] + 4 * g)
                in1_out(g - 1)
                if g == 2:
                    act.wait_ge(freq_done, 1)
                    copy(small[:, 32:33], pg[0][:, 0:1]).then_inc(par_ready, 1)
            in1_out(len(IN1_COLS) - 1)
            act.wait_ge(in1_ready, 15)
            norm_squares(NI["q"], q_lat, tmp)
            norm_squares(NI["kv"], kv_lat, tmp[:, 6:10, :])
            act.wait_ge(plain_used, PLAIN0["kraw"] + 1)
            copy(k_raw[:], pl[2][:, 0:S]).then_inc(in1_ready, 1)
            norm_root(NI["q"])
            norm_root(NI["kv"])
            act.wait_ge(const_ready, 7)
            act.wait_ge(trig_arg, 2)
            activation(sinT[:], sinT[:], ACT.Sin).then_inc(trig_ready, 1)
            activation(cosT[:], cosT[:], ACT.Sin, bias=halfpi[:], scale=-1.0).then_inc(trig_ready, 1)
            for n in range(HEADS // 2):
                act.wait_ge(plain_used, PLAIN0["uq"] + 2 * n + 2)
                for a in range(2):
                    last = copy(q_nope[:, 2 * n + a, :], pl[2 * (n % 2) + a][:, 0:S])
                last.then_inc(q_ready, 1)
                copy(q_pe[:, n, :], pg[n % 2][:, 0:S]).then_inc(q_ready, 1)
            act.wait_ge(centred, CT)
            act.wait_ge(norm_sum, NI["kv"] + 1)
            norm_squares(NI["ln"], conv_a, tmp)
            for n in range(HEADS // 2):
                if n == 2:
                    norm_root(NI["ln"])
                elif n == 3:
                    act.wait_ge(norm_out, tiles_before(NI["ln"] + 1))
                    for c in range(CT):
                        activation(mix[:, c, :], conv_a[:, c, :], ACT.Silu, bias=col("conv_ln_b", c)).then_inc(conv_silu, 1)
                    act.wait_ge(conv_silu, CT)
                    norm_squares(NI["conv"], mix, conv_a)
                act.wait_ge(plain_used, PLAIN0["ukv"] + n + 1)
                copy(k_nope[:, 2 * n:2 * n + 2, :], two(pl[n])).then_inc(kv_ready, 1)
                if n % 2:
                    for a in range(2):
                        copy(v_tok[:, a, n // 2 * 512:(n // 2 + 1) * 512], pg[a][:]).then_inc(kv_ready, 1)
            score = tmp[:, 0:4, :].rearrange("p a b -> p (a b)")
            prob = tmp[:, 8:12, :].rearrange("p a b -> p (a b)")
            probT = tmp[:, 12:16, :].rearrange("p a b -> p (a b)")

            def exponentials(hd):
                b = hd % 2 * 512
                act.wait_ge(s_max, hd + 1)
                if hd >= 2:
                    act.wait_ge(pT_done, hd - 1)
                m = 40 + hd % 2 * 4
                activation(prob[:, b:b + P], score[:, b:b + P], ACT.Exp, bias=small[:, m:m + 1],
                           accum_out=small[:, m + 2:m + 3]).then_inc(exp_ready, 1)
                activation(prob[:, b + P:b + 3 * P], score[:, b + P:b + 3 * P], ACT.Exp, bias=small[:, m + 1:m + 2],
                           accum_out=small[:, m + 3:m + 4]).then_inc(exp_ready, 1)

            def outputs(hd):
                act.wait_ge(o_done, hd + 1)
                copy(mix[:, 8 + hd, :], pg[1 + hd % 2][:, 0:S]).then_inc(o_ready, 1)

            exponentials(0)
            for hd in range(HEADS):
                if hd + 1 < HEADS:
                    exponentials(hd + 1)
                act.wait_ge(pT_done, hd + 1)
                if hd >= 2:
                    act.wait_ge(o_done, hd - 1)
                copy(probT[:, hd % 2 * 512:hd % 2 * 512 + 3 * P], pl[2 + hd % 2][:, 0:3 * P]).then_inc(pT_ready, 1)
                if hd:
                    outputs(hd - 1)
                if hd == 1:
                    norm_root(NI["conv"])
                if hd == HEADS - 2:
                    weights_hi(UNIT0["out1"], PIECE0["out1"], halves=(0,))
            act.wait_ge(s_max, HEADS)
            act.wait_ge(norm_out, tiles_before(NI["conv"] + 1))
            for t in range(0, 8, 4):
                copy(xhi[:, t:t + 4, :], mix[:, t:t + 4, :]).then_inc(x_hi, 1)
            outputs(HEADS - 1)
            act.wait_ge(o_ready, HEADS)
            norm_squares(NI["attn"], mix[:, 8:16, :], tmp)
            weights_hi(UNIT0["out1"], PIECE0["out1"], halves=(1,))
            norm_root(NI["attn"])
            for t in range(8, DT, 4):
                act.wait_ge(norm_out, tiles_before(NI["attn"]) + t - 4)
                copy(xhi[:, t:t + 4, :], mix[:, t:t + 4, :]).then_inc(x_hi, 1)

            def layer(name, turns, ready, dst, sq):
                u, n = UNIT0[name], PIECE0[name]

                def out(g, i=None):
                    done = n + 6 if g == 0 and i is None else n + 4 * (g + 1)
                    act.wait_ge(piece_used, done if i is None else i * 8 + done)
                    for a, fn, done in ((sq, ACT.Square, norm_sq), (dst, ACT.Copy, ready)):
                        for f in range(2):
                            t = 2 * g + f
                            d = a[:, t, :] if i is None else a[:, bass.ds(i * 4 + t, 1), :].rearrange("p a b -> p (a b)")
                            last = activation(d, PAIRS[g % 2][f][:, 0:S], fn)
                        last.then_inc(done, 1)

                weights_hi(u + 2, n + 4)
                out(0)
                with act.Fori(1, turns) as i:
                    weights_hi(u, n, i=i, step=8)
                    out(-1, i)
                    weights_hi(u + 2, n + 4, i=i, step=8)
                    out(0, i)
                out(2 * turns - 1)

            layer("out1", 4, out1_ready, tmp, mix)
            weights_hi(UNIT0["gu0"], PIECE0["gu0"])
            norm_root(NI["post"])
            input_hi(res1_ready, "pre_ffn_norm")
            pairs = 0
            for c, (t0, n) in enumerate(CHUNKS):
                u, pc = UNIT0[f"gu{c}"], PIECE0[f"gu{c}"]

                def gate_out(i=None):
                    act.wait_ge(gate_scaled, pairs + 2 if i is None else i + (pairs + 2))
                    activation(silu[:], silu[:], ACT.Silu).then_inc(silu_ready, 1)

                def hidden_hi(at, i=None):
                    act.wait_ge(mul_ready, pairs + at + 2 if i is None else i + (pairs + at + 2))
                    d = hhi[:, 2 * at:2 * at + 2, :] if i is None else hhi[:, bass.ds(i * 2 + 2 * at, 2), :]
                    copy(d, hid[:]).then_inc(hid_hi, 1)

                weights_hi(u + 2, pc + 4)
                if c == 0:
                    norm_root(NI["ffn"])
                gate_out()
                with act.Fori(1, n // 2) as i:
                    weights_hi(u, pc, i=i, step=8)
                    hidden_hi(-1, i)
                    weights_hi(u + 2, pc + 4, i=i, step=8)
                    gate_out(i)
                ud, pd, k = UNIT0[f"down{c}"], PIECE0[f"down{c}"], n // 2
                weights_hi(ud, pd, k)
                hidden_hi(n // 2 - 1)
                def down_squares(g, i=None):
                    if c + 1 < len(CHUNKS):
                        return
                    act.wait_ge(down_ready, 3 + 8 * c + g if i is None else i * 2 + (3 + 8 * c + g))
                    activation(two_tiles(mix, g, i), two_tiles(tmp, g, i), ACT.Square).then_inc(norm_sq, 1)

                weights_hi(ud + 2, pd + 4, k)
                down_squares(0)
                with act.Fori(1, 4) as i:
                    weights_hi(ud, pd, k, i=i, step=8)
                    down_squares(-1, i)
                    weights_hi(ud + 2, pd + 4, k, i=i, step=8)
                    down_squares(0, i)
                pairs += n // 2
                after = f"gu{c + 1}" if c + 1 < len(CHUNKS) else "in2a"
                weights_hi(UNIT0[after], PIECE0[after])
                down_squares(7)
            norm_root(NI["postf"])
            input_hi(res2_ready, "norm1_g_2")
            act.wait_ge(lam_abs, 1)
            activation(small[:, 0:8], small[:, 0:8], ACT.Exp, scale=-1.0).then_inc(lam_exp, 1)

            def in2_hi(g):
                weights_hi(in2_unit(g), PIECE0["in2a"] + 4 * g)

            def gelu(g):
                act.wait_ge(in2_ready, 2 + g + 1)
                t = slice(2 * (g - 8), 2 * (g - 8) + 2)
                activation(l_gelu[:, t, :], l_gelu[:, t, :], ACT.Gelu_apprx_tanh).then_inc(gelu_ready, 1)

            in2_hi(1)
            norm_root(NI["n1"])
            for g in range(2, 9):
                in2_hi(g)
            act.wait_ge(x_lo, 4 * (SPLITS["in2"] + 1))
            for hd in range(8):
                act.wait_ge(gates_done, hd + 1)
                if hd == 0:
                    act.wait_ge(xc_ready, 8)
                activation(l_r[:, hd, :], pg[hd % 3][:, 0:S], ACT.Sigmoid, bias=col("gate_a_b_2", hd)).then_inc(gates_ready, 1)
                activation(l_i[:, hd, :], pg[hd % 3][:, S:2 * S], ACT.Sigmoid, bias=col("gate_x_b_2", hd)).then_inc(gates_ready, 1)
            in2_hi(9)
            gelu(8)
            act.wait_ge(lam_ready, 1)
            act.wait_ge(gates_ready, 16)
            for hd in range(8):
                activation(l_m[:, hd, :], l_r[:, hd, :], ACT.Tanh, scale=small[:, 16 + hd:17 + hd]).then_inc(decay, 1)
            act.wait_ge(decay, 8)
            for hd in range(8):
                activation(l_r[:, hd, :], l_r[:, hd, :], ACT.Exp, scale=small[:, 8 + hd:9 + hd]).then_inc(decay, 1)
            in2_hi(10)
            gelu(9)
            for hd in range(8):
                act.wait_ge(mult_arg, hd + 1)
                activation(l_m[:, hd, :], l_m[:, hd, :], ACT.Sqrt).then_inc(mult_ready, 1)
            in2_hi(11)
            gelu(10)
            weights_hi(UNIT0["out2"], PIECE0["out2"])
            act.wait_ge(piece_used, PIECE0["out2"])
            for t in range(0, DT, 4):
                act.wait_ge(*((pool_y, t + 4) if t < 8 else (lru_y, t - 4)))
                copy(xhi[:, t:t + 4, :], mix[:, t:t + 4, :]).then_inc(x_hi, 1)
                if t == 0:
                    gelu(11)
            u, pc = UNIT0["out2"], PIECE0["out2"]

            def query_input(g, i=None):
                act.wait_ge(z_scaled, g + 1 if i is None else i * 2 + (g + 1))
                copy(two_tiles(zhi, g, i), two_tiles(mix, g, i)).then_inc(z_hi, 1)
                if g >= 2 or i is not None:
                    k = 7 * WIDE.index("n2") + g - 2
                    act.wait_ge(sq_added, max(k, 7 * WIDE.index("n2") + 1) if i is None else i * 2 + k)
                activation(sq_r[:, g % 2], two_tiles(res, g, i), ACT.Square).then_inc(norm_sq, 1)

            weights_hi(u + 2, pc + 4)
            query_input(0)
            weights_hi(u + 4, pc + 8)
            query_input(1)
            weights_hi(u + 6, pc + 12)
            query_input(2)
            with act.Fori(2, 4) as i:
                weights_hi(u, pc, i=i, step=8)
                query_input(-1, i)
                weights_hi(u + 2, pc + 4, i=i, step=8)
                query_input(0, i)
            weights_hi(UNIT0["wq"], PIECE0["wq"])
            query_input(7)
            for n in range(4):
                act.wait_ge(key_T, n + 1)
                copy(keysT[:, 4 * n:4 * n + 4, :], four(pg[n % 3])).then_inc(key_ready, 1)
            norm_root(NI["n2"])

            def score_copy(n):
                act.wait_ge(sc_done, n + 1)
                if n >= 2:
                    act.wait_ge(sel_max, TT * (n - 1))
                copy(sc[:, n % 2], four(pg[n % 2])).then_inc(sc_ready, 1)

            def gate_exp(n):
                act.wait_ge(sel_max, TT * (n + 1))
                g = gate[:, n * HSLOTS:(n + 1) * HSLOTS]
                activation(g, g, ACT.Exp).then_inc(sel_exp, 1)

            weights_hi(UNIT0["wq"] + 2, PIECE0["wq"] + 4)
            score_copy(0)
            act.wait_ge(rstd_T, 1)
            copy(small[:, 56:56 + TT], pl[2][:, 0:TT * P].rearrange("p (t c) -> p t c", t=TT)[:, :, 0]).then_inc(rstd_tok, 1)
            for n in range(8):
                act.wait_ge(tok_T, n + 1)
                t, f4 = n // 4, n % 4
                copy(acc[:, t, f4 * 512:(f4 + 1) * 512], pg[1 + n % 2][:]).then_inc(tok_r, 1)
            for n in range(1, PH + 2):
                if n + 1 < PH:
                    weights_hi(UNIT0["wq"] + 2 * (n + 1), PIECE0["wq"] + 4 * (n + 1))
                if n < PH:
                    score_copy(n)
                if n >= 2:
                    gate_exp(n - 2)
            for n in range(PH):
                act.wait_ge(row_used, GR + (n + 1) * HSLOTS)
                d = dots[:, n * HSLOTS:(n + 1) * HSLOTS]
                activation(d, d, ACT.Gelu_apprx_tanh).then_inc(act_ready, 1)
            for t in range(TT):
                act.wait_ge(row_used, GR + 2 * SLOTS - (TT - 1 - t) * TOPK)
                activation(zc[:, t, :], acc[:, t, :], ACT.Square, accum_out=small[:, 32 + t:33 + t]).then_inc(fin_sq, 1)
                act.wait_ge(fin_inv, t + 1)
                activation(small[:, 36 + t:37 + t], small[:, 34 + t:35 + t], ACT.Sqrt).then_inc(fin_rstd, 1)

        @block.vector
        def _(dve):
            V = nc.vector
            steps = [0]

            def link(ins):
                steps[0] += 1
                ins.then_inc(dve_step, 1)
                dve.wait_ge(dve_step, steps[0])

            def norm_inverse(n, d):
                dve.wait_ge(norm_sum, n + 1)
                link(V.tensor_scalar(meansq[:], pnorm, 1.0 / d, EPS, ALU.mult, ALU.add))
                if n:
                    dve.wait_ge(norm_rstd, n)
                V.reciprocal(invms[:], meansq[:]).then_inc(norm_inv, 1)

            def norm_scale(n, d):
                norm_inverse(n, d)
                dve.wait_ge(norm_rstd, n + 1)

            def norm_finish(n, src, gain, dst, d):
                norm_scale(n, d)
                for t in range(NORMS[n][1]):
                    V.scalar_tensor_tensor(dst[:, t, :], src[:, t, :], col(gain, t), rstd[:], ALU.mult, ALU.mult)\
                        .then_inc(norm_out, 1)

            def weights_lo(unit, piece, k=KU, i=None, step=0, between=None, halves=(0, 1)):
                for half in halves:
                    u = unit + half
                    w = raw[:, u % RING, 0:k * CG].rearrange("p (k f c) -> p k f c", k=k, f=2)
                    for f in range(2):
                        n = piece + 2 * half + f
                        dve.wait_ge(w_hi, n + 1 if i is None else i * step + (n + 1))
                        V.tensor_tensor(wlo[:, n % 4, 0:k, :], w[:, :, f, :], whi[:, n % 4, 0:k, :].bitcast(F32), ALU.subtract)\
                            .then_inc(w_lo, 1)
                        if between:
                            between()

            def input_lo(name, src, tiles=range(0, DT, 4)):
                for t in tiles:
                    dve.wait_ge(x_hi, 4 * SPLITS[name] + t // 4 + 1)
                    V.tensor_tensor(xlo[:, t:t + 4, :], src[:, t:t + 4, :], xhi[:, t:t + 4, :].bitcast(F32), ALU.subtract)\
                        .then_inc(x_lo, 1)

            TURN = 2 * np.pi
            T1 = 6.28125
            T2 = float(np.float32(np.round((TURN - T1) * 2.0 ** 21) / 2.0 ** 21))
            T3 = float(np.float32(TURN - T1 - T2))
            MAGIC = 1.5 * 2.0 ** 23
            a_ = angle[:]
            s_ = sinT[:]
            c_ = cosT[:]
            for s, n in ((out2_ready, 2), (wq_ready, 2), (in2_ready, 2), (down_ready, 2), (in1_ready, 2), (out1_ready, 2),
                         (gate_scaled, 1), (mul_ready, 1), (hid_lo, 1)):
                dve.sem_inc(s, n)
            for t in range(TT):
                dve.wait_ge(x_sq, t + 1)
                link(V.tensor_scalar(x_stat[:, 2 + t:3 + t], x_stat[:, t:t + 1], 1.0 / D, EPS, ALU.mult, ALU.add))
                V.reciprocal(x_stat[:, 2 + t:3 + t], x_stat[:, 2 + t:3 + t]).then_inc(x_inv, 1)
                dve.wait_ge(x_rstd, t + 1)
                V.tensor_scalar(xn[:, t, :], xin[:, t, :], x_stat[:, 4 + t:5 + t], None, ALU.mult).then_inc(x_norm, 1)
            dve.wait_ge(par_ready, 1)
            dve.wait_ge(x_T, 8)
            dve.wait_ge(x_norm, TT)
            for n in range(8):
                t, f4 = n // 4, n % 4
                dve.wait_ge(xn_T, n + 1)
                V.tensor_tensor(mix[:, f4 * 4:f4 * 4 + 4, t * P:(t + 1) * P], pl[1 + n % 3][:].rearrange("p (a b) -> p a b", a=4),
                                col("pre_mix_norm", f4 * 4, 4).unsqueeze(2).broadcast_to([P, 4, P]), ALU.mult).then_inc(xn_ready, 1)
            V.memset(conv_u[:, :, 0:CPAD], 0.0)
            for half in range(2):
                input_lo("in1", mix, range(8 * half, 8 * half + 8, 4))
                weights_lo(UNIT0["in1"], PIECE0["in1"], halves=(half,))

            taps = []
            n_taps = [0]

            def add_taps(n):
                for k, c in taps[n_taps[0]:n_taps[0] + n]:
                    u = conv_u[:, c, k:k + S]
                    if k == 0:
                        ins = V.tensor_scalar(conv_a[:, c, :], u, conv_tap(0, c), col("conv_b", c), ALU.mult, ALU.add)
                    else:
                        dve.wait_ge(conv_step, n_taps[0] - 1)
                        ins = V.scalar_tensor_tensor(conv_a[:, c, :], u, conv_tap(k, c), conv_a[:, c, :], ALU.mult, ALU.add)
                    ins.then_inc(conv_step, 1)
                    n_taps[0] += 1

            for g in range(1, len(IN1_COLS)):
                weights_lo(UNIT0["in1"] + 2 * g, PIECE0["in1"] + 4 * g, between=lambda: add_taps(4))
                if g % 2 == 0 and g <= 8:
                    j = g // 2 - 1
                    dve.wait_ge(in1_ready, 2 + g)
                    V.tensor_tensor(conv_u[:, 2 * j:2 * j + 2, CPAD:], conv_a[:, 2 * j:2 * j + 2, :], sig[:, j % 2], ALU.mult)\
                        .then_inc(u_ready, 1)
                    dve.wait_ge(u_ready, j + 1)
                    taps += [(k, c) for k in range(CONV_K) for c in (2 * j, 2 * j + 1)]
            dve.wait_ge(pos_in, 16)
            dve.wait_ge(par_ready, 2)
            link(V.tensor_copy(c_, a_.bitcast(I32)))
            link(V.tensor_scalar(a_, c_, small[:, 32:33], None, ALU.mult))
            link(V.tensor_scalar(s_, a_, 1.0 / TURN, None, ALU.mult))
            link(V.tensor_scalar(s_, s_, MAGIC, None, ALU.add))
            link(V.tensor_scalar(s_, s_, MAGIC, None, ALU.subtract))
            for part in (T1, T2, T3):
                link(V.scalar_tensor_tensor(a_, s_, -part, a_, ALU.mult, ALU.add))
            V.tensor_scalar(s_, a_, 3.1415925, -3.1415925, ALU.min, ALU.max).then_inc(trig_arg, 1)
            V.scalar_tensor_tensor(c_, a_, -1.0, a_, ALU.mult, ALU.max).then_inc(trig_arg, 1)
            norm_finish(NI["q"], q_lat, "q_norm", q_lat, QLT * P)
            norm_finish(NI["kv"], kv_lat, "kv_norm", kv_lat, KVT * P)
            add_taps(len(taps))
            dve.wait_ge(trig_ready, 2)
            dve.wait_ge(rot_done, 1)
            rot = tmp[:, 8:8 + HEADS // 2, :]
            for n in range(2):
                V.tensor_tensor(rot[:, 2 * n:2 * n + 2, :], pl[n][:].rearrange("p (a b) -> p a b", a=2),
                                s_.unsqueeze(1).broadcast_to([P, 2, S]), ALU.mult)
            V.tensor_tensor(k_pe[:], pg[0][:, 0:S], s_, ALU.mult).then_inc(rot_read, 1)
            dve.wait_ge(mean_sum, 1)
            link(V.tensor_scalar(mean_b[:], pg[2][:, 0:S], 1.0 / CONV_CH, None, ALU.mult))
            for c in range(CT):
                V.tensor_tensor(conv_a[:, c, :], conv_a[:, c, :], mean_b[:], ALU.subtract).then_inc(centred, 1)
            dve.wait_ge(rot_read, 1)
            V.tensor_tensor(q_pe[:], q_pe[:], c_.unsqueeze(1).broadcast_to([P, HEADS // 2, S]), ALU.mult)
            link(V.tensor_tensor(k_raw[:], k_raw[:], c_, ALU.mult))
            V.tensor_tensor(q_pe[:], q_pe[:], rot, ALU.add)
            V.tensor_tensor(k_pe[:], k_pe[:], k_raw[:], ALU.add).then_inc(roped, 1)
            dve.wait_ge(centred, CT)
            norm_finish(NI["ln"], conv_a, "conv_ln_g", conv_a, CONV_CH)
            score = tmp[:, 0:4, :].rearrange("p a b -> p (a b)")
            prob = tmp[:, 8:12, :].rearrange("p a b -> p (a b)")
            dve.wait_ge(roped, 1)
            dve.wait_ge(const_ready, 7)

            def head_scores(hd):
                b = hd % 2 * 512
                m = 40 + hd % 2 * 4
                dve.wait_ge(s_done, hd + 1)
                if hd >= 2:
                    dve.wait_ge(exp_ready, 2 * (hd - 1))
                V.scalar_tensor_tensor(score[:, b:b + 3 * P], pl[hd % 2][:, 0:3 * P], SCALE,
                                       mask[:].rearrange("p a b -> p (a b)"), ALU.mult, ALU.add).then_inc(s_ready, 1)
                dve.wait_ge(s_ready, hd + 1)
                V.tensor_reduce(small[:, 48:49], score[:, b:b + P], AX.X, ALU.max)
                link(V.tensor_reduce(small[:, 49:50], score[:, b + P:b + 3 * P], AX.X, ALU.max))
                V.tensor_scalar(small[:, m:m + 2], small[:, 48:50], -1.0, None, ALU.mult).then_inc(s_max, 1)

            def normalise(hd):
                b = hd % 2 * 512
                m = 42 + hd % 2 * 4
                r = 52 + hd % 2 * 2
                dve.wait_ge(exp_ready, 2 * hd + 2)
                link(V.reciprocal(small[:, r:r + 2], small[:, m:m + 2]))
                link(V.tensor_scalar(prob[:, b:b + P], prob[:, b:b + P], small[:, r:r + 1], None, ALU.mult))
                V.tensor_scalar(prob[:, b + P:b + 3 * P], prob[:, b + P:b + 3 * P], small[:, r + 1:r + 2], None, ALU.mult)\
                    .then_inc(prob_ready, 1)

            head_scores(0)
            dve.wait_ge(s_max, 1)
            head_scores(1)
            normalise(0)
            for hd in range(HEADS):
                if hd + 1 < HEADS:
                    normalise(hd + 1)
                if hd + 2 < HEADS:
                    dve.wait_ge(s_max, hd + 2)
                    head_scores(hd + 2)
                if hd == 1:
                    norm_inverse(NI["conv"], CONV_CH)
                elif 2 <= hd < 6:
                    dve.wait_ge(norm_rstd, NI["conv"] + 1)
                    for t in range(2 * hd - 4, 2 * hd - 2):
                        V.scalar_tensor_tensor(mix[:, t, :], mix[:, t, :], col("conv_out_norm", t), rstd[:], ALU.mult, ALU.mult)\
                            .then_inc(norm_out, 1)
            weights_lo(UNIT0["out1"], PIECE0["out1"], halves=(0,))
            input_lo("out1", mix, (0, 4))
            weights_lo(UNIT0["out1"], PIECE0["out1"], halves=(1,))
            norm_finish(NI["attn"], mix[:, 8:16, :], "attn_out_norm", mix[:, 8:16, :], HEADS * VH)
            input_lo("out1", mix, (8, 12))

            def layer(name, turns):
                u, n = UNIT0[name], PIECE0[name]
                weights_lo(u + 2, n + 4)
                with dve.Fori(1, turns) as i:
                    weights_lo(u, n, i=i, step=8)
                    weights_lo(u + 2, n + 4, i=i, step=8)

            def residual(n, gain, ready, next_gain, name):
                norm_scale(n, D)
                for k in range(5):
                    if k < 4:
                        for t in range(4 * k, 4 * k + 4):
                            V.scalar_tensor_tensor(tmp[:, t, :], tmp[:, t, :], col(gain, t), rstd[:], ALU.mult, ALU.mult)\
                                .then_inc(norm_out, 1)
                    if k:
                        dve.wait_ge(x_hi, 4 * SPLITS[name] + k)
                        for t in range(4 * k - 4, 4 * k):
                            last = V.scalar_tensor_tensor(xlo[:, t, :], res[:, t, :], col(next_gain, t), xhi[:, t, :].bitcast(F32),
                                                          ALU.mult, ALU.subtract)
                        last.then_inc(x_lo, 1)
                    if k < 4:
                        f = slice(4 * k, 4 * k + 4)
                        dve.wait_ge(norm_out, tiles_before(n) + 4 * k + 4)
                        V.tensor_tensor(res[:, f, :], res[:, f, :], tmp[:, f, :], ALU.add).then_inc(ready, 1)

            layer("out1", 4)
            residual(NI["post"], "post_mix_norm", res1_ready, "pre_ffn_norm", "ffn")
            both = rstd[:].unsqueeze(1).broadcast_to([P, 2, S])
            pairs = 0
            for c, (t0, n) in enumerate(CHUNKS):
                u, pc = UNIT0[f"gu{c}"], PIECE0[f"gu{c}"]

                def scale_gates(i=None):
                    k = pairs + 1
                    done = pc + 6 if i is None and c == 0 else pc + 4
                    dve.wait_ge(piece_used, done if i is None else i * 8 + done)
                    dve.wait_ge(mul_ready, k if i is None else i + k)
                    for f in range(2):
                        last = V.tensor_tensor(silu[:, f, :], pl[f][:, 0:S], rstd[:], ALU.mult)
                    last.then_inc(gate_scaled, 1)

                def multiply(at, i=None):
                    k = pairs + at
                    dve.wait_ge(silu_ready, k + 1 if i is None else i + (k + 1))
                    V.tensor_tensor(silu[:], silu[:], both, ALU.mult).then_inc(silu_scaled, 1)
                    dve.wait_ge(piece_used, pc + 8 * at + 8 if i is None else i * 8 + (pc + 8 * at + 8))
                    dve.wait_ge(silu_scaled, k + 1 if i is None else i + (k + 1))
                    dve.wait_ge(hid_lo, k + 1 if i is None else i + (k + 1))
                    for f in range(2):
                        last = V.tensor_tensor(hid[:, f, :], silu[:, f, :], pl[2 + f][:, 0:S], ALU.mult)
                    last.then_inc(mul_ready, 1)

                def hidden_lo(at, i=None):
                    k = pairs + at
                    dve.wait_ge(hid_hi, k + 1 if i is None else i + (k + 1))
                    if i is None:
                        d, s = hlo[:, 2 * at:2 * at + 2, :], hhi[:, 2 * at:2 * at + 2, :]
                    else:
                        d, s = hlo[:, bass.ds(i * 2 + 2 * at, 2), :], hhi[:, bass.ds(i * 2 + 2 * at, 2), :]
                    V.tensor_tensor(d, hid[:], s.bitcast(F32), ALU.subtract).then_inc(hid_lo, 1)

                dve.wait_ge(w_lo, pc + 4)
                weights_lo(u + 2, pc + 4)
                if c == 0:
                    norm_scale(NI["ffn"], D)
                scale_gates()
                with dve.Fori(1, n // 2) as i:
                    weights_lo(u, pc, i=i, step=8)
                    multiply(-1, i)
                    weights_lo(u + 2, pc + 4, i=i, step=8)
                    hidden_lo(-1, i)
                    scale_gates(i)
                ud, pd, k = UNIT0[f"down{c}"], PIECE0[f"down{c}"], n // 2
                weights_lo(ud, pd, k)
                multiply(n // 2 - 1)
                hidden_lo(n // 2 - 1)

                def down_out(g, i=None):
                    dve.wait_ge(piece_used, pd + 4 * (g + 1) if i is None else i * 8 + (pd + 4 * (g + 1)))
                    for f in range(2):
                        t = 2 * g + f
                        d = tmp[:, t, :] if i is None else tmp[:, bass.ds(i * 4 + t, 1), :].rearrange("p a b -> p (a b)")
                        bank = pl[2 * (g % 2) + f][:, 0:S]
                        last = V.tensor_copy(d, bank) if c == 0 else V.tensor_tensor(d, d, bank, ALU.add)
                    last.then_inc(down_ready, 1)

                weights_lo(ud + 2, pd + 4, k)
                down_out(0)
                with dve.Fori(1, 4) as i:
                    weights_lo(ud, pd, k, i=i, step=8)
                    down_out(-1, i)
                    weights_lo(ud + 2, pd + 4, k, i=i, step=8)
                    down_out(0, i)
                pairs += n // 2
                if c + 1 < len(CHUNKS):
                    weights_lo(UNIT0[f"gu{c + 1}"], PIECE0[f"gu{c + 1}"])
                down_out(7)
            residual(NI["postf"], "post_ffn_norm", res2_ready, "norm1_g_2", "in2")
            lam = col("lru_lambda_2", 0, 8)
            V.scalar_tensor_tensor(small[:, 0:8], lam, -1.0, lam, ALU.mult, ALU.max).then_inc(lam_abs, 1)
            V.memset(p_u[:, :, 0:WMAX], 0.0)
            V.memset(l_x[:, :, 0:LPAD], 0.0)
            for g, w in enumerate(POOL_WINDOWS):
                for n in range(w):
                    V.memset(edge[:, g, n:n + 1], 1.0 / (n + 1))
            link(V.memset(win[:], 0.0))
            link(V.memset(win2[:], 0.0))

            def in2_lo(g):
                weights_lo(in2_unit(g), PIECE0["in2a"] + 4 * g)

            def in2_out(g):
                dve.wait_ge(piece_used, PIECE0["in2a"] + (4 * (g + 1) if g else 6))
                t = slice(2 * (g % 4), 2 * (g % 4) + 2)
                dst = (l_x[:, t, LPAD:], p_u[:, t, WMAX:], l_gelu[:, t, :])[g // 4]
                for f in range(2):
                    last = V.tensor_tensor(dst[:, f, :], pl[2 * (g % 2) + f][:, 0:S], rstd[:], ALU.mult)
                last.then_inc(in2_ready, 1)

            dve.wait_ge(w_lo, PIECE0["in2a"] + 4)
            in2_lo(1)
            norm_scale(NI["n1"], D)
            in2_out(0)
            dve.wait_ge(lam_exp, 1)
            y, s8, s2, ser = small[:, 0:8], small[:, 24:32], small[:, 16:24], small[:, 8:16]
            link(V.tensor_scalar(s2, y, 2.0, None, ALU.add))
            link(V.reciprocal(s2, s2))
            link(V.tensor_tensor(s8, y, s2, ALU.mult))
            link(V.tensor_tensor(s2, s8, s8, ALU.mult))
            TERMS = 9
            link(V.tensor_scalar(ser, s2, 1.0 / (2 * TERMS + 1), 1.0 / (2 * TERMS - 1), ALU.mult, ALU.add))
            for n in range(TERMS - 2, -1, -1):
                link(V.tensor_tensor(ser, ser, s2, ALU.mult))
                link(V.tensor_scalar(ser, ser, 1.0 / (2 * n + 1), None, ALU.add))
            link(V.tensor_tensor(ser, ser, s8, ALU.mult))
            link(V.tensor_scalar(s2, lam, 0.0, None, ALU.min))
            link(V.scalar_tensor_tensor(ser, ser, -2.0, s2, ALU.mult, ALU.add))
            link(V.tensor_scalar(ser, ser, LRU_C, None, ALU.mult))
            V.tensor_scalar(s2, ser, -1.0, None, ALU.mult).then_inc(lam_ready, 1)

            def short_conv(c):
                dve.wait_ge(in2_ready, 2 + c // 2 + 1)
                for k in range(LCONV):
                    src, wk = l_x[:, c, k:k + S], col("conv_w_2", k * 8 + c)
                    if k == 0:
                        ins = V.tensor_scalar(l_xc[:, c, :], src, wk, col("conv_b_2", c), ALU.mult, ALU.add)
                    else:
                        ins = V.scalar_tensor_tensor(l_xc[:, c, :], src, wk, l_xc[:, c, :], ALU.mult, ALU.add)
                    if k < LCONV - 1:
                        link(ins)
                    else:
                        ins.then_inc(xc_ready, 1)

            def pool_group(g):
                w = POOL_WINDOWS[g]
                dve.wait_ge(in2_ready, 2 + 4 + g + 1)
                for f in (2 * g, 2 * g + 1):
                    cur, other, spare, step = p_u[:, f, :], win[:], win2[:], 1
                    while step < w:
                        link(V.tensor_tensor(other[:, step:], cur[:, step:], cur[:, 0:WMAX + S - step], ALU.add))
                        cur, other, spare, step = other, spare, other, 2 * step
                    V.scalar_tensor_tensor(p_d[:, f, w:], cur[:, WMAX + w:], 1.0 / w, p_u[:, f, WMAX + w:], ALU.mult, ALU.subtract)
                    link(V.tensor_tensor(p_d[:, f, 0:w], cur[:, WMAX:WMAX + w], edge[:, g, 0:w], ALU.mult))
                    link(V.tensor_tensor(p_d[:, f, 0:w], p_d[:, f, 0:w], p_u[:, f, WMAX:WMAX + w], ALU.subtract))
                    dve.sem_inc(pool_d, 1)

            for g in range(2, 9):
                in2_lo(g)
                in2_out(g - 1)
                if g <= 5:
                    short_conv(2 * g - 4)
                    short_conv(2 * g - 3)
                else:
                    pool_group(g - 6)
            dve.wait_ge(gates_ready, 16)
            V.tensor_tensor(l_i[:], l_i[:], l_xc[:], ALU.mult)
            in2_lo(9)
            in2_out(8)
            pool_group(3)
            for hd in range(8):
                dve.wait_ge(decay, 8 + hd + 1)
                link(V.tensor_tensor(l_xc[:, hd, :], l_r[:, hd, :], l_r[:, hd, :], ALU.mult))
                V.scalar_tensor_tensor(l_m[:, hd, :], l_xc[:, hd, :], 1.0, l_m[:, hd, :], ALU.add, ALU.mult).then_inc(mult_arg, 1)
            in2_lo(10)
            in2_out(9)
            for hd in range(8):
                dve.wait_ge(mult_ready, hd + 1)
                link(V.tensor_tensor(l_i[:, hd, :], l_i[:, hd, :], l_m[:, hd, :], ALU.mult))
                link(V.tensor_tensor_scan(l_xc[:, hd, :], l_r[:, hd, :], l_i[:, hd, :], 0.0, ALU.mult, ALU.add))
            for g in range(4):
                dve.wait_ge(pool_done, g + 1)
                for f in range(2):
                    t = 2 * g + f
                    V.tensor_scalar(mix[:, t, :], pg[g % 3][:, f * S:(f + 1) * S], col("pool_b_2", t), col("pool_scale_2", t),
                                    ALU.add, ALU.mult).then_inc(pool_y, 1)
            in2_lo(11)
            in2_out(10)
            weights_lo(UNIT0["out2"], PIECE0["out2"])
            in2_out(11)
            for q in range(2):
                input_lo("out2", mix, (4 * q,))
                for hd in range(4 * q, 4 * q + 4):
                    if hd % 2 == 0:
                        dve.wait_ge(gelu_ready, hd // 2 + 1)
                    V.tensor_tensor(mix[:, 8 + hd, :], l_xc[:, hd, :], l_gelu[:, hd, :], ALU.mult).then_inc(lru_y, 1)
            input_lo("out2", mix, (8, 12))
            u, pc = UNIT0["out2"], PIECE0["out2"]
            gain2 = PC["norm2_g_2"]
            dve.wait_ge(x_lo, 4 * (SPLITS["out2"] + 1))

            def out2_out(g, i=None):
                dve.wait_ge(piece_used, pc + 4 * (g + 1) if i is None else i * 8 + (pc + 4 * (g + 1)))
                for f in range(2):
                    t = 2 * g + f
                    r = res[:, t, :] if i is None else res[:, bass.ds(i * 4 + t, 1), :].rearrange("p a b -> p (a b)")
                    last = V.tensor_tensor(r, r, pl[2 * (g % 2) + f][:, 0:S], ALU.add)
                last.then_inc(out2_ready, 1)
                dve.wait_ge(out2_ready, 2 + g + 1 if i is None else i * 2 + (2 + g + 1))
                t = gain2 + 2 * g
                gains = par[:, t:t + 2] if i is None else par[:, bass.ds(i * 4 + t, 2)]
                V.tensor_tensor(two_tiles(mix, g, i), two_tiles(res, g, i), gains.unsqueeze(2).broadcast_to([P, 2, S]), ALU.mult)\
                    .then_inc(z_scaled, 1)

            def query_input(g, i=None):
                dve.wait_ge(z_hi, g + 1 if i is None else i * 2 + (g + 1))
                V.tensor_tensor(two_tiles(zlo, g, i), two_tiles(mix, g, i), two_tiles(zhi, g, i).bitcast(F32), ALU.subtract)\
                    .then_inc(z_lo, 1)

            weights_lo(u + 2, pc + 4)
            out2_out(0)
            with dve.Fori(1, 4) as i:
                weights_lo(u, pc, i=i, step=8)
                out2_out(-1, i)
                query_input(-2, i)
                weights_lo(u + 2, pc + 4, i=i, step=8)
                out2_out(0, i)
                query_input(-1, i)
            weights_lo(UNIT0["wq"], PIECE0["wq"])
            out2_out(7)
            query_input(6)
            query_input(7)
            norm_scale(NI["n2"], D)

            def wide(ap, axis, shape):
                return ap.unsqueeze(axis).broadcast_to(shape)

            def best(sets):
                for s, rest, v, ix in sets:
                    last = V.max(v[:, 0:8], s)
                link(last)
                for s, rest, v, ix in sets:
                    V.max_index(ix[:, 0:8], v[:, 0:8], s)
                    last = V.match_replace(rest, v[:, 0:8], s, NEG)
                link(last)
                for s, rest, v, ix in sets:
                    last = V.max(v[:, 8:16], rest)
                link(last)
                for s, rest, v, ix in sets:
                    last = V.max_index(ix[:, 8:16], v[:, 8:16], rest)
                link(last)

            def best_keys(n, t):
                dve.wait_ge(sc_ready, n + 1)
                best([(sc[:, n % 2, m, :], work[:, m, :], top_v[:, m, :], top_i[:, m, :]) for m in (2 * t, 2 * t + 1)])
                V.tensor_copy(top_f[:, 2 * t:2 * t + 2, :], top_i[:, 2 * t:2 * t + 2, :])
                link(V.tensor_tensor(cand[:, t, :].rearrange("p (a b) -> p a b", a=TOPK),
                                     wide(top_v[:, 2 * t, :], 2, [P, TOPK, TOPK]),
                                     wide(top_v[:, 2 * t + 1, :], 1, [P, TOPK, TOPK]), ALU.add))

            def choose(n, t):
                best([(cand[:, t, :], cand2[:, t, :], ctop[:, t, :], cpos[:, t, :])])
                ci = cpos[:, t, :].bitcast(I32)
                V.tensor_scalar(cposi[:, 0, t, :], ci, 4, None, ALU.logical_shift_right)
                link(V.tensor_scalar(cposi[:, 1, t, :], ci, 15, None, ALU.bitwise_and))
                at = n * HSLOTS + t * TOPK
                V.tensor_tensor(gate[:, at:at + TOPK], ctop[:, t, :], ctop[:, t, 0:1].broadcast_to([P, TOPK]), ALU.subtract)\
                    .then_inc(sel_max, 1)
                link(V.tensor_copy(cposf[:, :, t, :], cposi[:, :, t, :]))
                full = [P, TOPK, TOPK]
                j16 = iota16[:].unsqueeze(1).broadcast_to(full)
                picks = [c_[:, t, :].rearrange("p (k j) -> p k j", k=TOPK) for c_ in (cand, cand2)]
                for half in range(2):
                    last = V.tensor_tensor(picks[half], wide(cposf[:, half, t, :], 2, full), j16, ALU.is_equal)
                link(last)
                for half in range(2):
                    last = V.tensor_tensor(picks[half], picks[half], wide(top_f[:, 2 * t + half, :], 1, full), ALU.mult)
                link(last)
                for half in range(2):
                    last = V.tensor_reduce(cposf[:, half, t, :], picks[half], AX.X, ALU.add)
                link(last)
                V.scalar_tensor_tensor(expert[:, at:at + TOPK], cposf[:, 0, t, :], float(NKEY), cposf[:, 1, t, :],
                                       ALU.mult, ALU.add).then_inc(sel_ready, 1)
                dve.wait_ge(sel_ready, n * TT + t + 1)

            def products(n, t, part):
                first = n * HSLOTS + t * TOPK + part * TOPK // 2
                for j in range(first, first + TOPK // 2):
                    dve.wait_ge(row_full[j % GR], 16 * (j // GR + 1))
                    r = row[j % GR][:]
                    V.tensor_tensor_reduce(r, r, zc[:, t, :], 1.0, 0.0, ALU.mult, ALU.add, dots[:, j:j + 1]).then_inc(row_used, 1)

            def queries(n):
                dve.wait_ge(piece_used, PIECE0["wq"] + 4 * (n + 1))
                if n >= 2:
                    dve.wait_ge(sc_done, n - 1)
                for half in range(2):
                    last = V.tensor_tensor(qh[:, n % 2, half, :], pl[2 * (n % 2) + half][:, 0:S], rstd[:], ALU.mult)
                last.then_inc(wq_ready, 1)

            weights_lo(UNIT0["wq"] + 2, PIECE0["wq"] + 4)
            queries(0)
            best_keys(0, 0)
            choose(0, 0)
            dve.wait_ge(tok_r, 8)
            dve.sem_inc(row_used, GR)
            best_keys(0, 1)
            choose(0, 1)

            def input_tokens(t):
                dve.wait_ge(rstd_tok, 1)
                dve.wait_ge(zgain_in, 16 * TT)
                link(V.scalar_tensor_tensor(zc[:, t, :], acc[:, t, :], small[:, 56 + t:57 + t], zc[:, t, :], ALU.mult, ALU.mult))

            input_tokens(0)
            for n in range(PH):
                for t in range(TT):
                    products(n, t, 0)
                    if t == 0 and n == 0:
                        queries(1)
                        input_tokens(1)
                    if n + 1 < PH:
                        best_keys(n + 1, t)
                    products(n, t, 1)
                    if n + 1 < PH:
                        choose(n + 1, t)
                    m = n + 3 if n else t + 2
                    if m < PH:
                        weights_lo(UNIT0["wq"] + 2 * m, PIECE0["wq"] + 4 * m, halves=(t,) if n else (0, 1))
                if n + 2 < PH:
                    queries(n + 2)
                if n == PH - 2:
                    dve.wait_ge(sel_exp, PH)
                    g3 = gate[:].rearrange("p (s k) -> p s k", k=TOPK)
                    link(V.tensor_reduce(small[:, 0:PH * TT], g3, AX.X, ALU.add))
                    link(V.reciprocal(small[:, 0:PH * TT], small[:, 0:PH * TT]))
                    link(V.tensor_tensor(g3, g3, wide(small[:, 0:PH * TT], 2, [P, PH * TT, TOPK]), ALU.mult))
            dve.wait_ge(act_ready, PH)
            link(V.tensor_tensor(dots[:], gate[:], dots[:], ALU.mult))
            with dve.Fori(0, PH) as n:
                V.tensor_copy(w_r[:], dots[:, bass.ds(n * HSLOTS, HSLOTS)]).then_inc(w_copied, 1)
                dve.wait_ge(w_copied, n + 1)
                for j in range(HSLOTS):
                    t = j // TOPK
                    dve.wait_ge(row_full[j % GR], n * (16 * HSLOTS // GR) + 16 * (SLOTS // GR + j // GR + 1))
                    V.scalar_tensor_tensor(acc[:, t, :], row[j % GR][:], w_r[:, j:j + 1], acc[:, t, :], ALU.mult, ALU.add)\
                        .then_inc(row_used, 1)
                    dve.wait_ge(row_used, n * HSLOTS + (GR + SLOTS + j + 1))
            dve.wait_ge(gain_in, 16)
            for t in range(TT):
                dve.wait_ge(fin_sq, t + 1)
                link(V.tensor_scalar(small[:, 34 + t:35 + t], small[:, 32 + t:33 + t], 1.0 / D, EPS, ALU.mult, ALU.add))
                link(V.reciprocal(small[:, 34 + t:35 + t], small[:, 34 + t:35 + t]))
                dve.sem_inc(fin_inv, 1)
                dve.wait_ge(fin_rstd, t + 1)
                for half in range(2):
                    c = slice(half * D // 2, (half + 1) * D // 2)
                    V.scalar_tensor_tensor(zc[:, t, c], acc[:, t, c], small[:, 36 + t:37 + t], gain_f[:, c], ALU.mult, ALU.mult)\
                        .then_inc(fin_out, 1)


_INS = ['x', 'positions', 'pre_mix_norm', 'w_in', 'q_norm', 'w_uq', 'kv_norm', 'w_ukv', 'conv_w', 'conv_b', 'conv_ln_g',
        'conv_ln_b', 'conv_out_norm', 'attn_out_norm', 'w_out', 'post_mix_norm', 'pre_ffn_norm', 'w_gate', 'w_up',
        'w_down', 'post_ffn_norm', 'norm1_g_2', 'w_in_2', 'pool_w_2', 'pool_b_2', 'pool_scale_2', 'conv_w_2',
        'conv_b_2', 'gate_a_w_2', 'gate_a_b_2', 'gate_x_w_2', 'gate_x_b_2', 'lru_lambda_2', 'w_out_2', 'norm2_g_2',
        'peer_wq_2', 'peer_keys1_2', 'peer_keys2_2', 'peer_u_2', 'peer_v_2', 'norm_f_g_2']


def kernel(**inputs):
    import concourse.bacc as bacc
    from concourse.bass_utils import run_bass_kernel_spmd

    nc = bacc.Bacc("TRN2", target_bir_lowering=False, num_devices=1)
    arrays, args = {}, {}
    for name in _INS:
        a = np.ascontiguousarray(inputs[name])
        arrays[f"in_{name}"] = a
        args[name] = nc.dram_tensor(f"in_{name}", a.shape, mybir.dt.from_np(a.dtype), kind="ExternalInput").ap()
    out = nc.dram_tensor("out", (1, S, D), F32, kind="ExternalOutput").ap()
    build(nc, args, out)
    r = run_bass_kernel_spmd(nc, [arrays], core_ids=[0])
    return r.results[0]["out"]
```
